# Optimizing a Trainium2 kernel written in Bass

```python
import math
import jax
import jax.numpy as jnp
from jax import lax
import numpy as np

D_MODEL = 1024
BATCH = 1
SEQ = 128
DEPTH = 1
DEC_BATCH = 1
DEC_SEQ = 512
PAST_LEN = 128

GRID_W = 64
RMS_EPS = 1e-6
DN_HEADS = 8
DN_DK = 128
DN_DV = 128
DN_WK = DN_HEADS * DN_DK
DN_WV = DN_HEADS * DN_DV
DN_CONV = 3
DN_CHUNK = 64
NA_HEADS = 8
NA_HD = 64
NA_W = NA_HEADS * NA_HD
NA_KR = 8
NA_KC = 16
NA_QCB = 16
NA_SLAB = 32
NA_NCB = GRID_W // NA_QCB
FFN_HIDDEN = -(-8 * D_MODEL // (3 * 256)) * 256
OFF_Z = 2 * DN_WK + DN_WV
OFF_BETA = OFF_Z + DN_WV
OFF_A = OFF_BETA + 2 * DN_HEADS
OFF_NA = OFF_A + 2 * DN_HEADS
OFF_GATE = OFF_NA + 3 * NA_W
N_IN = OFF_GATE + 2 * D_MODEL

kernel_name = 'hybrid_deltanet_natten_dit_step'

def rmsnorm(x, g):
    xf = x.astype(jnp.float32)
    y = xf * lax.rsqrt(jnp.mean(xf * xf, axis=-1, keepdims=True) + RMS_EPS)
    return (y * g.astype(jnp.float32)).astype(x.dtype)

def l2norm(x):
    xf = x.astype(jnp.float32)
    return xf * lax.rsqrt(jnp.sum(xf * xf, axis=-1, keepdims=True) + RMS_EPS)

def adaln(cond, w, b):
    m = jax.nn.silu(cond) @ w + b
    return jnp.split(m, 6, axis=-1)

def modulate(x, g, shift, scale):
    return rmsnorm(x, g) * (1 + scale[:, None]) + shift[:, None]

def short_conv(x, w):
    return lax.conv_general_dilated(x, w[:, None, :], window_strides=(1,),
                                    padding=[(DN_CONV // 2, DN_CONV // 2)],
                                    dimension_numbers=('NWC', 'WIO', 'NWC'),
                                    feature_group_count=x.shape[-1])

def gated_delta_chunked(q, k, v, g, beta, s0):
    b, l, h, _ = q.shape
    dv = v.shape[-1]
    c = DN_CHUNK
    n = l // c

    def chunks(t):
        t = t.reshape((b, n, c, h) + t.shape[3:])
        return jnp.moveaxis(t, (1, 3), (0, 2))

    q, k, v, g, beta = (chunks(t) for t in (q, k, v, g, beta))
    gc = jnp.cumsum(g, axis=-1)
    causal = jnp.tril(jnp.ones((c, c), bool))
    strict = jnp.tril(jnp.ones((c, c), bool), -1)
    decay = jnp.exp(jnp.where(causal, gc[..., :, None] - gc[..., None, :], -jnp.inf))
    kb = k * beta[..., None]
    lmat = jnp.where(strict, jnp.einsum('nbhid,nbhjd->nbhij', kb, k) * decay, 0.0)
    eye = jnp.eye(c, dtype=jnp.float32)
    tinv = lax.linalg.triangular_solve(lmat + eye, jnp.broadcast_to(eye, lmat.shape),
                                       left_side=True, lower=True, unit_diagonal=True)
    u = tinv @ (v * beta[..., None])
    w = tinv @ (kb * jnp.exp(gc)[..., None])
    aqk = jnp.einsum('nbhid,nbhjd->nbhij', q, k) * decay
    qg = q * jnp.exp(gc)[..., None]
    kd = k * jnp.exp(gc[..., -1:] - gc)[..., None]
    glast = jnp.exp(gc[..., -1])[..., None, None]

    def step(s, xs):
        u_i, w_i, a_i, qg_i, kd_i, gl_i = xs
        v_new = u_i - w_i @ s
        o_i = qg_i @ s + a_i @ v_new
        s = s * gl_i + jnp.swapaxes(kd_i, -1, -2) @ v_new
        return s, o_i

    s_fin, o = lax.scan(step, s0, (u, w, aqk, qg, kd, glast))
    o = jnp.moveaxis(o, (0, 2), (1, 3)).reshape(b, l, h, dv)
    return o, s_fin

def deltanet_branch(qkv, z, beta_logit, a_logit, conv_w, a_log, dt_bias, norm_g, s0):
    b, l, _ = qkv.shape
    qkv = jax.nn.silu(short_conv(qkv, conv_w))
    q, k, v = jnp.split(qkv, [DN_WK, 2 * DN_WK], axis=-1)
    q = l2norm(q.reshape(b, l, DN_HEADS, DN_DK)) * DN_DK ** -0.5
    k = l2norm(k.reshape(b, l, DN_HEADS, DN_DK))
    v = v.reshape(b, l, DN_HEADS, DN_DV).astype(jnp.float32)
    beta = jax.nn.sigmoid(beta_logit.astype(jnp.float32))
    g = -jnp.exp(a_log.astype(jnp.float32)) * jax.nn.softplus(
        a_logit.astype(jnp.float32) + dt_bias.astype(jnp.float32))
    s0 = s0.astype(jnp.float32)
    o_f, s_f = gated_delta_chunked(q, k, v, g[:, :, 0], beta[:, :, 0], s0[:, 0])
    flip = lambda t: jnp.flip(t, axis=1)
    o_b, s_b = gated_delta_chunked(flip(q), flip(k), flip(v), flip(g[:, :, 1]),
                                   flip(beta[:, :, 1]), s0[:, 1])
    o = o_f + flip(o_b)
    zz = z.reshape(b, l, DN_HEADS, DN_DV).astype(jnp.float32)
    o = rmsnorm(o, norm_g) * jax.nn.silu(zz)
    return o.reshape(b, l, DN_WV).astype(qkv.dtype), jnp.stack([s_f, s_b], axis=1)

def na_qkv(u, qn_g, kn_g):
    b, l, _ = u.shape
    u = u.reshape(b, l, 3, NA_HEADS, NA_HD)
    q = rmsnorm(u[:, :, 0], qn_g) * NA_HD ** -0.5
    k = rmsnorm(u[:, :, 1], kn_g)
    return q, k, u[:, :, 2]

def na_context(q, k, v):
    b, l = q.shape[:2]
    logits = jnp.einsum('bqhd,bkhd->bhqk', q, k, preferred_element_type=jnp.float32)
    p = jax.nn.softmax(logits, axis=-1).astype(v.dtype)
    return jnp.einsum('bhqk,bkhd->bqhd', p, v).reshape(b, l, NA_W)

def na_tables(rows):
    kr = min(NA_KR, rows)
    p = np.arange(rows)
    rs = np.clip(p - kr // 2, 0, rows - kr)
    row_idx = rs[:, None] + np.arange(kr)[None]
    row_off = row_idx - p[:, None] + (NA_KR - 1)
    cb = np.arange(NA_NCB)
    c0 = np.clip(cb * NA_QCB - NA_KC // 2, 0, GRID_W - NA_SLAB)
    col_idx = c0[:, None] + np.arange(NA_SLAB)[None]
    qcol = cb[:, None] * NA_QCB + np.arange(NA_QCB)[None]
    cs = np.clip(qcol - NA_KC // 2, 0, GRID_W - NA_KC)[..., None]
    keycol = col_idx[:, None, :]
    col_mask = (keycol >= cs) & (keycol < cs + NA_KC)
    col_off = np.clip(keycol - qcol[..., None] + (NA_KC - 1), 0, 2 * NA_KC - 2)
    return row_idx, row_off, col_idx, col_mask, col_off

def na_latent(q, k, v, k_ctx, v_ctx, rpb):
    b, l, h, d = q.shape
    rows = l // GRID_W
    row_idx, row_off, col_idx, col_mask, col_off = na_tables(rows)
    ri = row_idx[:, :, None, None]
    ci = col_idx[None, None]
    kg = k.reshape(b, rows, GRID_W, h, d)[:, ri, ci]
    vg = v.reshape(b, rows, GRID_W, h, d)[:, ri, ci]
    qb = q.reshape(b, rows, NA_NCB, NA_QCB, h, d)
    s_nb = jnp.einsum('bpcqhd,bpkcshd->bhpcqks', qb, kg, preferred_element_type=jnp.float32)
    bias = rpb[:, row_off[:, None, None, :, None], col_off[None, :, :, None, :]]
    s_nb = jnp.where(col_mask[:, :, None, :], s_nb + bias.astype(jnp.float32), -jnp.inf)
    s_ctx = jnp.einsum('bpcqhd,bjhd->bhpcqj', qb, k_ctx, preferred_element_type=jnp.float32)
    m = jnp.maximum(jnp.max(s_nb, axis=(-2, -1)), jnp.max(s_ctx, axis=-1))
    e_nb = jnp.exp(s_nb - m[..., None, None])
    e_ctx = jnp.exp(s_ctx - m[..., None])
    denom = jnp.sum(e_nb, axis=(-2, -1)) + jnp.sum(e_ctx, axis=-1)
    o = (jnp.einsum('bhpcqks,bpkcshd->bpcqhd', e_nb.astype(v.dtype), vg, preferred_element_type=jnp.float32)
         + jnp.einsum('bhpcqj,bjhd->bpcqhd', e_ctx.astype(v.dtype), v_ctx, preferred_element_type=jnp.float32))
    o = o / jnp.moveaxis(denom, 1, -1)[..., None]
    return o.astype(v.dtype).reshape(b, l, NA_W)

def split_in(h, w_in):
    b, l, _ = h.shape
    u = h @ w_in
    qkv, z, bl, al, na, gt = jnp.split(u, [OFF_Z, OFF_BETA, OFF_A, OFF_NA, OFF_GATE], axis=-1)
    return qkv, z, bl.reshape(b, l, 2, DN_HEADS), al.reshape(b, l, 2, DN_HEADS), na, gt

def merge(o_dn, o_na, gt, w_pa, w_pb, w_out):
    g_a, g_b = jnp.split(jax.nn.sigmoid(gt), 2, axis=-1)
    return (g_a * (o_dn @ w_pa) + g_b * (o_na @ w_pb)) @ w_out

def swiglu(h, w1, w3, w2):
    return (jax.nn.silu(h @ w1) * (h @ w3)) @ w2

def setup_inputs(seed: int = 0) -> dict:
    key = jax.random.key(seed)
    ks = jax.random.split(key, 26)
    f32 = jnp.float32
    D = D_MODEL

    def nrm(k, shape, s):
        return jax.random.normal(k, shape, f32) * s

    dt = jnp.exp(jax.random.uniform(ks[13], (DEPTH, 2, DN_HEADS), f32, math.log(1e-3), math.log(1e-1)))
    return {
        'x_prompt': nrm(ks[0], (BATCH, SEQ, D), 1.0),
        'x_sample': nrm(ks[1], (DEC_BATCH, DEC_SEQ, D), 1.0),
        'c': nrm(ks[2], (DEC_BATCH, D), 1.0),
        'cache_na_k': nrm(ks[3], (DEC_BATCH, DEPTH, PAST_LEN, NA_HEADS, NA_HD), 1.0),
        'cache_na_v': nrm(ks[4], (DEC_BATCH, DEPTH, PAST_LEN, NA_HEADS, NA_HD), 1.0),
        'state_dn': nrm(ks[5], (DEC_BATCH, DEPTH, 2, DN_HEADS, DN_DK, DN_DV), DN_DK ** -0.5),
        'c_ctx': nrm(ks[6], (D,), 1.0),
        'w_ada': nrm(ks[7], (DEPTH, D, 6 * D), 0.5 * D ** -0.5),
        'b_ada': nrm(ks[8], (DEPTH, 6 * D), 0.02),
        'norm1_g': 1.0 + nrm(ks[9], (DEPTH, D), 0.02),
        'w_in': nrm(ks[10], (DEPTH, D, N_IN), D ** -0.5),
        'dn_conv': nrm(ks[11], (DEPTH, DN_CONV, 2 * DN_WK + DN_WV), DN_CONV ** -0.5),
        'dn_a_log': jnp.log(jax.random.uniform(ks[12], (DEPTH, 2, DN_HEADS), f32, 1.0, 16.0)),
        'dn_dt_bias': dt + jnp.log(-jnp.expm1(-dt)),
        'dn_norm_g': 1.0 + nrm(ks[14], (DEPTH, DN_DV), 0.02),
        'w_pa': nrm(ks[15], (DEPTH, DN_WV, D), DN_WV ** -0.5),
        'na_qnorm_g': 1.0 + nrm(ks[16], (DEPTH, NA_HD), 0.02),
        'na_knorm_g': 1.0 + nrm(ks[17], (DEPTH, NA_HD), 0.02),
        'na_rpb': nrm(ks[18], (DEPTH, NA_HEADS, 2 * NA_KR - 1, 2 * NA_KC - 1), 0.1),
        'w_pb': nrm(ks[19], (DEPTH, NA_W, D), NA_W ** -0.5),
        'w_out': nrm(ks[20], (DEPTH, D, D), D ** -0.5),
        'norm2_g': 1.0 + nrm(ks[21], (DEPTH, D), 0.02),
        'ffn_w1': nrm(ks[22], (DEPTH, D, FFN_HIDDEN), D ** -0.5),
        'ffn_w3': nrm(ks[23], (DEPTH, D, FFN_HIDDEN), D ** -0.5),
        'ffn_w2': nrm(ks[24], (DEPTH, FFN_HIDDEN, D), FFN_HIDDEN ** -0.5),
    }

def reference(x_prompt, x_sample, c, cache_na_k, cache_na_v, state_dn, c_ctx, w_ada, b_ada,
              norm1_g, w_in, dn_conv, dn_a_log, dn_dt_bias, dn_norm_g, w_pa, na_qnorm_g,
              na_knorm_g, na_rpb, w_pb, w_out, norm2_g, ffn_w1, ffn_w3, ffn_w2):
    xp = x_prompt
    xs = x_sample
    new_k, new_v, new_s = [], [], []
    for i in range(DEPTH):
        sh1, sc1, g1, sh2, sc2, g2 = adaln(c_ctx[None], w_ada[i], b_ada[i])
        h = modulate(xp, norm1_g[i], sh1, sc1)
        qkv, z, bl, al, na, gt = split_in(h, w_in[i])
        s0 = jnp.zeros((xp.shape[0], 2, DN_HEADS, DN_DK, DN_DV), jnp.float32)
        o_dn, s_ctx = deltanet_branch(qkv, z, bl, al, dn_conv[i], dn_a_log[i], dn_dt_bias[i],
                                      dn_norm_g[i], s0)
        q, k, v = na_qkv(na, na_qnorm_g[i], na_knorm_g[i])
        o_na = na_context(q, k, v)
        xp = xp + g1[:, None] * merge(o_dn, o_na, gt, w_pa[i], w_pb[i], w_out[i])
        xp = xp + g2[:, None] * swiglu(modulate(xp, norm2_g[i], sh2, sc2), ffn_w1[i], ffn_w3[i], ffn_w2[i])
        new_k.append(k)
        new_v.append(v)
        new_s.append(s_ctx.astype(xp.dtype))

        sh1, sc1, g1, sh2, sc2, g2 = adaln(c, w_ada[i], b_ada[i])
        h = modulate(xs, norm1_g[i], sh1, sc1)
        qkv, z, bl, al, na, gt = split_in(h, w_in[i])
        o_dn, _ = deltanet_branch(qkv, z, bl, al, dn_conv[i], dn_a_log[i], dn_dt_bias[i],
                                  dn_norm_g[i], state_dn[:, i])
        q, k, v = na_qkv(na, na_qnorm_g[i], na_knorm_g[i])
        o_na = na_latent(q, k, v, cache_na_k[:, i], cache_na_v[:, i], na_rpb[i])
        xs = xs + g1[:, None] * merge(o_dn, o_na, gt, w_pa[i], w_pb[i], w_out[i])
        xs = xs + g2[:, None] * swiglu(modulate(xs, norm2_g[i], sh2, sc2), ffn_w1[i], ffn_w3[i], ffn_w2[i])

    return (xp, xs, jnp.stack(new_k, axis=1), jnp.stack(new_v, axis=1), jnp.stack(new_s, axis=1))


_drawn_inputs = setup_inputs


def setup_inputs(seed=0):
    import zlib

    import numpy as np

    out = dict(_drawn_inputs(seed))
    spreads = {}
    factors = {'cache_na_k': 5.32,
     'cache_na_v': 3.913,
     'state_dn': 6.653,
     'dn_norm_g': 26.873,
     'na_qnorm_g': 8.0,
     'na_knorm_g': 8.21,
     'na_rpb': 64.0,
     'norm2_g': 8.0}
    for name, (base, spread) in spreads.items():
        noise = np.random.default_rng([zlib.crc32(name.encode()), seed]).standard_normal(out[name].shape)
        drawn = base * np.exp(spread * noise) if base else spread * noise
        out[name] = jnp.asarray(drawn.astype(out[name].dtype))
    for name, factor in factors.items():
        out[name] = (out[name] * factor).astype(out[name].dtype)
    return out
```

```python
from contextlib import ExitStack

import numpy as np

import concourse.bass as bass
from concourse import mybir

F32 = mybir.dt.float32
ACT = mybir.ActivationFunctionType
ALU = mybir.AluOpType
AX = mybir.AxisListType
ds = bass.ds

P = 128
D = 1024
KD = D // P
CTX, LAT = 128, 512
TOK = LAT + CTX
NT = TOK // P
CT = LAT // P
EPS = 1e-6
H, DK = 8, 128
U = 2 * NT
OFF_Z = 3 * D
OFF_BETA = OFF_Z + D
OFF_NA = OFF_BETA + 4 * H
NA_H, NA_D = 8, 64
NA_W = NA_H * NA_D
OFF_GATE = OFF_NA + 3 * NA_W
FFN = 2816
KF = FFN // P
KP = NA_W // P
GRID_W, ROWS = 64, 8
KR, KC = 8, 16
RPB = (2 * KR - 1) * (2 * KC - 1)
NEG = -1e30
G, EG, NEG_EG, EK, GL, BETA = range(6)
NPRM = 6
LEVELS = (1, 2, 4, 8, 16)
LE, GE, GT, LT, ID, ONE = range(6)


def shape_constants():
    k, i = np.arange(P)[:, None], np.arange(P)[None]
    squares = np.stack([k <= i, k >= i, k > i, k < i, k == i, k + i >= 0], 1).astype(np.float32)
    row, col = np.arange(P)[:, None] % 32, np.arange(32)[None]
    level = []
    for b in LEVELS:
        pair = row // (2 * b) == col // (2 * b)
        lower = pair & (row // b % 2 == 1) & (col // b % 2 == 0)
        upper = pair & (row // b % 2 == 0) & (col // b % 2 == 1)
        level += [lower, upper]
    level.append(row == col)
    levels = np.stack(level, 1).astype(np.float32)
    window = np.zeros((P, GRID_W // KC, 3 * KC), np.float32)
    for cb in range(GRID_W // KC):
        q = cb * KC + np.arange(P)[:, None] % KC
        key = (cb - 1) * KC + np.arange(3 * KC)[None]
        first = np.clip(q - KC // 2, 0, GRID_W - KC)
        window[:, cb] = np.where((key >= first) & (key < first + KC), 0.0, NEG)
    return squares.reshape(P, -1), levels.reshape(P, -1), window.reshape(P, -1)


class Steps:

    def __init__(self, sem, names):
        self.sem, self.names, self.at = sem, names, {n: i + 1 for i, n in enumerate(names)}
        assert len(self.at) == len(names), names
        self.n, self.next = len(names), 0

    def done(self, ins, name):
        assert self.names[self.next % self.n] == name, (self.names[self.next % self.n], name)
        self.next += 1
        ins.then_inc(self.sem, 1)

    def value(self, turn, name):
        return (turn + 1) * self.n + self.at[name]


def wait_apart(e, passed, *waits):
    values = [value if isinstance(value, int) else e.to_reg(value) for _, value in waits]
    e.wait_ge(passed, 1)
    for (sem, _), value in zip(waits, values):
        e.wait_ge(sem, value)


def pe_steps():
    names = ["dt", "norm", "kq", "turn k v", "P0"]
    for n in (1, 2, 3, 4, 5):
        names += [f"P{n}", f"Y{n}"]
    names += ["P6", "Y6"]
    for s in range(NT):
        if s:
            names += [f"ks {s} {d}" for d in "fb"]
        names += [f"y {s} {d}" for d in "fb"]
        names += [f"av {s} {d}" for d in "fb"]
    return names + ["ada rows", "ada", "turn o"]


def act_steps():
    names = ["decay", "silu q", "silu k", "silu v", "square", "norm", "kq", "k rows", "L diag", "L pairs", "P5", "Y5", "P6", "Y6"]
    for s in range(NT):
        if s:
            names += [f"qs {s} {d}" for d in "fb"]
        names += [f"v {s} {d}" for d in "fb"]
        names += [f"state {d}" for d in "fb"] if not s else []
    return names + ["silu z", "ada rows", "o square", "o norm", "ada"]


NE = 4
assert NE * (H - 1) * P == 3 * NA_W + 2 * D


def dve_steps():
    names = ["prm", "taps", "conv q", "conv k", "conv v", "1/norm", "beta", "-beta", "v rows", "kv ctx", "L", "L diag"]
    names += ["P0", "X0", "XT0"]
    for n in (1, 2, 3, 4):
        names += [f"P{n}", f"X{n}", f"XT{n}"]
    names += ["X64", "XT diag", "Y5", "XT64", "P6", "Y6"]
    for s in range(NT):
        if s:
            names += [f"r {s} {d}" for d in "fb"]
        names += [f"S {s} {d}" for d in "fb"] if 0 < s < NT - 1 else []
        names += [f"o {s} {d}" for d in "fb"]
    return names + ["o sum", "o scaled", "1/o norm", "o normed", "o out"]


UNITS = [(hh, c) for hh in range(2) for c in range(NT)]
NU = len(UNITS)


def key_tiles(c):
    if c == CT:
        return [], 3 * P, (3 * P, 4 * P)
    first, last = max(c - 1, 0), min(c + 1, CT - 1)
    at = P if last - first == 1 else 0
    return list(range(first, last + 1)), at, (at, 4 * P)


def pe_na_steps():
    names = ["turn", "score 0", "score 1"]
    for i in range(NU):
        names += [f"turn P {i}"] + ([f"score {i + 2}"] if i + 2 < NU else []) + [f"PV {i}"]
    return names


def act_na_steps():
    names = ["v rows", "T lat"]
    for i in range(NU + 1):
        names += ([f"exp {i}"] if i < NU else []) + ([f"PT {i - 1}"] if i else [])
    return names + ["out"]


def dve_na_steps():
    names = ["q rows", "k rows", "T ctx"]
    for i in range(NU + 1):
        names += ([f"max {i}", f"-max {i}"] if i < NU else []) + ([f"1/sum {i - 1}", f"P {i - 1}"] if i else [])
    return names


POOL_STEPS = ["g mask", "decay", "kd", "A"]


def build(nc, A):
    top = ExitStack()
    with top:
        def sb(name, shape, stack=top):
            return stack.enter_context(nc.sbuf_tensor(name, shape, F32))

        def sem(name):
            return top.enter_context(nc.semaphore(name))

        sq_c = sb("sq_c", [P, 6, P])
        lv_c = sb("lv_c", [P, 2 * len(LEVELS) + 1, 32])
        cols = sb("cols", [P, 160])
        mods = sb("mods", [P, 48, 2])
        gain1 = sb("gain1", [P, KD, 2])
        gain2 = sb("gain2", [P, KD, 2])
        epsc = sb("epsc", [P, 2])
        csT = sb("csT", [P, 2, KD])
        xT = sb("xT", [P, KD, TOK])
        hT = sb("hT", [P, KD, TOK])
        oT = sb("oT", [P, H, TOK])
        naT = sb("naT", [P, KP, TOK])
        W = sb("W", [P, 4, KD, P])
        ps = top.enter_context(nc.psum_tensor("ps", [P, 8, 512], F32))

        WE = naT[:, 2:4, :].rearrange("p a c -> p (a c)")[:, 0:D].rearrange("p (k c) -> p k c", k=KD)
        stage = naT[:, 0:2, :]

        IDN = sq_c[:, ID, :]
        ONES = sq_c[:, ONE, :]
        B_ADA, N1, N2, DNG, CONV = 0, 48, 56, 64, 65

        w_in = A["w_in"][0].rearrange("(k p) n -> p k n", p=P)
        w_ada = A["w_ada"][0].rearrange("(k p) n -> p k n", p=P)

        ld_const = sem("ld_const")
        ld_vec = sem("ld_vec")
        ld_x = [sem(f"ld_x{t}") for t in range(NT)]
        ld_wa = [sem(f"ld_wa{s}") for s in range(4)]
        vec_turned = sem("vec_turned")
        vec_out = sem("vec_out")
        cond_silu = sem("cond_silu")
        x_turned = sem("x_turned")
        x_out = sem("x_out")
        sq_done = sem("sq_done")
        ss_done = sem("ss_done")
        rms_done = sem("rms_done")
        rstd_done = sem("rstd_done")
        xn_done = sem("xn_done")
        h_done = sem("h_done")
        ada_mm = sem("ada_mm")
        ada_row = sem("ada_row")
        ada_out = sem("ada_out")
        gain_done = sem("gain_done")
        ld_ba = sem("ld_ba")
        ba_mm = sem("ba_mm")
        ba_act = sem("ba_act")
        ba_dve = sem("ba_dve")
        cum_mm = sem("cum_mm")
        prm_done = sem("prm_done")
        zero_done = sem("zero_done")

        ld_w = {k: sem(f"ld_w_{k}") for k in "qkvz"}
        strip = {k: sem(f"strip_{k}") for k in "qkvz"}
        raw = {k: sem(f"raw_{k}") for k in "qkv"}
        conv_part = sem("conv_part")
        bk_part = sem("bk_part")
        ld_e = sem("ld_e")
        strip_e = sem("strip_e")
        e_out = sem("e_out")
        st_e = [sem(f"st_e{i}") for i in range(2)]
        ext_dram = nc.dram_tensor("ext_dram", (NE * (H - 1), P, TOK), F32)
        ld_S = sem("ld_S")
        st_S = sem("st_S")
        slot = {"q": 0, "k": 1, "v": 2, "z": 3}

        pe_dn = Steps(sem("pe_dn"), pe_steps())
        act_dn = Steps(sem("act_dn"), act_steps())
        dve_dn = Steps(sem("dve_dn"), dve_steps())
        pool_dn = Steps(sem("pool_dn"), POOL_STEPS)

        ld_fq = [sem(f"ld_fq{j}") for j in range(3)]
        ld_nc = sem("ld_nc")
        rpb_pad = sem("rpb_pad")
        rpb_rows = sem("rpb_rows")
        ld_bias = [sem(f"ld_bias{hh}") for hh in range(2)]
        zrow_done = sem("zrow_done")
        proj_mm = sem("proj_mm")
        proj_out = sem("proj_out")
        nsq_done = sem("nsq_done")
        nss_done = sem("nss_done")
        nrms_done = sem("nrms_done")
        nrn_done = sem("nrn_done")
        nrow_done = sem("nrow_done")
        ngain_done = sem("ngain_done")
        st_k = sem("st_k")
        st_v = sem("st_v")
        pe_na = Steps(sem("pe_na"), pe_na_steps())
        act_na = Steps(sem("act_na"), act_na_steps())
        dve_na = Steps(sem("dve_na"), dve_na_steps())
        pool_na = Steps(sem("pool_na"), ["bias 0", "bias 1"])

        ld_m = [sem(f"ld_m{i}") for i in range(4)]
        ld_g = [sem(f"ld_g{i}") for i in range(2)]
        mods_done = sem("mods_done")
        pe_mg = Steps(sem("pe_mg"), ["pA0", "pB0", "pA1", "pB1"])
        act_mg = Steps(sem("act_mg"), ["g0", "g1"])
        dve_mg = Steps(sem("dve_mg"), ["yA0", "yB0", "y0", "yA1", "yB1", "y1"])
        ld_o = [sem(f"ld_o{i}") for i in range(4)]
        pe_wo = Steps(sem("pe_wo"), [f"o{i}" for i in range(4)])
        dve_wo = Steps(sem("dve_wo"), [f"x{i}" for i in range(4)])
        sq2_done = sem("sq2_done")
        ss2_mm = sem("ss2_mm")
        rms2_done = sem("rms2_done")
        dg2_done = sem("dg2_done")
        rstd2_mm = sem("rstd2_mm")
        xn2_done = sem("xn2_done")
        h2_done = sem("h2_done")
        ld_f = [sem(f"ld_f{i}") for i in range(4)]
        pe_f1 = Steps(sem("pe_f1"), ["a0", "b0", "a1", "b1"])
        act_f1 = Steps(sem("act_f1"), ["a0", "a1"])
        dve_f1 = Steps(sem("dve_f1"), ["h0", "h1"])
        ld_f2 = [sem(f"ld_f2{i}") for i in range(2)]
        pe_f2 = Steps(sem("pe_f2"), ["m0", "m1", "turn 0", "turn 1"])
        dve_f2 = Steps(sem("dve_f2"), ["x0", "x1"])
        act_f2 = Steps(sem("act_f2"), ["y0", "y1"])
        st_y = [sem(f"st_y{i}") for i in range(2)]

        rpb_dram = nc.dram_tensor("rpb_dram", (1, NA_H * RPB + 64), F32)
        rpb_rows_dram = nc.dram_tensor("rpb_rows_dram", (KC, NA_H * (2 * KR - 1) * 3 * KC), F32)

        work = top.enter_context(ExitStack())
        params = sb("params", [P, H, NPRM, U], work)
        WA = sb("WA", [P, 4, KD, P], work)
        start = work.enter_context(ExitStack())
        xin = sb("xin", [P, NT, D], start)
        rows = sb("rows", [P, 2, P], start)
        sqx = sb("sqx", [P, 2, TOK], start)
        rstd = sb("rstd", [P, TOK], start)
        rms = sb("rms", [P, TOK], start)
        wba = sb("wba", [P, KD, 4 * H], start)
        ba = sb("ba", [P, NT, 4 * H], start)
        alog = sb("alog", [P, 2 * H], start)
        dtb = sb("dtb", [P, 2 * H], start)
        sp = sb("sp", [P, 4, NT, 2 * H], start)
        arow0 = sb("arow0", [2, 16 * P], start)
        start.close()
        dn = work.enter_context(ExitStack())
        prm = sb("prm", [P, NPRM, U], dn)
        arow = sb("arow", [2, 4 * P], dn)
        taps = sb("taps", [P, 3, 3], dn)
        raws = sb("raws", [P, 3, TOK + 4], dn)
        conv = sb("conv", [P, 3, TOK + 4], dn)
        kq = sb("kq", [P, NT, 2, P], dn)
        zs = sb("zs", [P, TOK], dn)
        sqkq = sb("sqkq", [P, NT, 2, P], dn)
        nrm = sb("nrm", [P, 2, NT], dn)
        rn = sb("rn", [P, 2, NT], dn)
        bk = sb("bk", [P, 2, U], dn)
        krow = sb("krow", [P, NT, P], dn)
        vrow = sb("vrow", [P, NT, P], dn)
        kd = sb("kd", [P, U, P], dn)
        gm = sb("gm", [P, U, P], dn)
        dt = sb("dt", [P, U, P], dn)
        dtm = dt
        kqs = sqkq
        AT = gm
        LNT = sb("LNT", [P, U, P], dn)
        LNTd = sb("LNTd", [P, U, P], dn)
        LNTp = sb("LNTp", [P, U, P], dn)
        Xc = sb("Xc", [P, U, 32], dn)
        Pc = sb("Pc", [P, U, 32], dn)
        Yc = sb("Yc", [P, U, 32], dn)
        XTd = sb("XTd", [P, U, P], dn)
        X64 = sb("X64", [P, U, 64], dn)
        P6c = sb("P6c", [P, U, 64], dn)
        XT = sb("XT", [P, U, P], dn)
        S = sb("S", [P, 2, P], dn)
        Sc = sb("Sc", [P, 2, P], dn)
        rr = sb("rr", [P, 2, P], dn)
        vn = sb("vn", [P, 2, P], dn)
        tq = sb("tq", [P, 2, P], dn)
        ob = sb("ob", [P, 2, NT, P], dn)
        osum = sb("osum", [P, NT, P], dn)
        osq, osc = ob[:, 0, :, :], ob[:, 1, :, :]
        oss = sb("oss", [P, NT], dn)
        orm = sb("orm", [P, NT], dn)
        orn = sb("orn", [P, NT], dn)
        dn.close()
        na = work.enter_context(ExitStack())
        fq = WA[:, :, :, :].rearrange("p s k c -> p (s k c)")[:, 0:KP * TOK].rearrange("p (s c) -> p s c", s=KP)
        fk = W[:, :, :, :].rearrange("p s k c -> p (s k c)")[:, 0:KP * TOK].rearrange("p (s c) -> p s c", s=KP)
        fv = sb("fv", [P, KP, TOK], na)
        qkv = sb("qkv", [P, 3, NT, NA_W], na)
        nsq = sb("nsq", [P, 2, NA_W], na)
        nss = sb("nss", [P, 2, NT, NA_H], na)
        nrms = sb("nrms", [P, 2, NT, NA_H], na)
        nrn = sb("nrn", [P, 2, NT, NA_H], na)
        ngain = sb("ngain", [P, 2, NA_D], na)
        ck = sb("ck", [P, NA_W], na)
        cv = sb("cv", [P, NA_W], na)
        win = sb("win", [P, CT, 3 * KC], na)
        bias = sb("bias", [P, 2, ROWS, 3 * KC], na)
        bm = sb("bm", [P, 2, CT, 4 * P], na)
        qrow = sb("qrow", [P, NT, P], na)
        krow_n = sb("krow_n", [P, NT + 1, P], na)
        vrow_n = sb("vrow_n", [P, NT + 1, P], na)
        qT = sb("qT", [P, CT, P], na)
        kT = sb("kT", [P, CT, P], na)
        cT = sb("cT", [P, 3, P], na)
        Sx = sb("Sx", [P, 2, 4 * P], na)
        PT = sb("PT", [P, 2, 4 * P], na)
        mx = sb("mx", [P, NU], na)
        nmx = sb("nmx", [P, NU], na)
        sm = sb("sm", [P, NU], na)
        rs = sb("rs", [P, NU], na)
        zrow = sb("zrow", [1, 32], na)
        na.close()
        work.close()
        late = top.enter_context(ExitStack())
        act = sb("act", [P, KF, TOK], late)
        yT = act[:, 0:KD, :]
        sg = sb("sg", [P, 2, TOK], late)
        pr = sb("pr", [P, 2, TOK], late)
        gates = act[:, KD:KD + 4, :].rearrange("p (i g) c -> p i g c", i=2)
        sgm = act[:, KD + 4:KD + 8, :].rearrange("p (i g) c -> p i g c", i=2)
        prod = act[:, KD + 8:KD + 12, :].rearrange("p (i g) c -> p i g c", i=2)
        W2 = sb("W2", [P, 2, KF, P], late)
        ss2 = sb("ss2", [P, NT], late)
        rn2 = sb("rn2", [P, NT], late)
        dg2 = sb("dg2", [P, NT, P], late)
        xo = sb("xo", [P, 2, TOK], late)
        yo = sb("yo", [P, 2, NT, P], late)
        late.close()

        block = top.enter_context(nc.Block())
        SEG = ((0, LAT), (LAT, CTX))

        def wide(w):
            return w[:, :, :, :].rearrange("p s k c -> p (s k c)").rearrange("p (k c) -> p k c", k=KD)

        def typed(t, lo=0, n=NT):
            return t.rearrange("p (d t) c -> p d t c", d=2)[:, :, lo:lo + n, :]

        @block.sync
        def _(e):
            e.dma_start(sq_c[:, :, :], A["squares"].rearrange("p (a b) -> p a b", a=6)).then_inc(ld_const, 16)
            e.dma_start(lv_c[:, :, :], A["levels"].rearrange("p (a b) -> p a b", b=32)).then_inc(ld_const, 16)
            e.dma_start(rows[0:48, 0, :], A["b_ada"][0].rearrange("(r c) -> r c", c=P)).then_inc(ld_vec, 16)
            e.dma_start(rows[48:56, 0, :], A["norm1_g"][0].rearrange("(r c) -> r c", c=P)).then_inc(ld_vec, 16)
            e.dma_start(rows[56:64, 0, :], A["norm2_g"][0].rearrange("(r c) -> r c", c=P)).then_inc(ld_vec, 16)
            e.dma_start(rows[64:65, 0, :], A["dn_norm_g"]).then_inc(ld_vec, 16)
            e.dma_start(rows[65:73, 0, :], A["c"][0].rearrange("(r c) -> r c", c=P)).then_inc(ld_vec, 16)
            e.dma_start(rows[73:81, 0, :], A["c_ctx"].rearrange("(r c) -> r c", c=P)).then_inc(ld_vec, 16)
            e.dma_start(rows[0:72, 1, :], A["dn_conv"][0].rearrange("t (r c) -> (t r) c", c=P)).then_inc(ld_vec, 16)
            for t in range(NT):
                src = A["x_sample"][0, t * P:(t + 1) * P, :] if t < CT else A["x_prompt"][0]
                e.dma_start(xin[:, t, :], src).then_inc(ld_x[t], 16)
            e.dma_start(alog[:, :], A["dn_a_log"].rearrange("o d h -> o (d h)").partition_broadcast(P)).then_inc(ld_ba, 16)
            e.dma_start(dtb[:, :], A["dn_dt_bias"].rearrange("o d h -> o (d h)").partition_broadcast(P)).then_inc(ld_ba, 16)
            e.dma_start(wba[:, :, :], w_in[:, :, OFF_BETA:OFF_BETA + 4 * H]).then_inc(ld_ba, 16)
            for s in range(4):
                e.dma_start(WA[:, s, :, :], w_ada[:, :, s * P:(s + 1) * P]).then_inc(ld_wa[s], 16)
            with e.Fori(1, 4) as i:
                for s in range(4):
                    if s % 2 == 0:
                        e.wait_ge(ada_mm, i * 2 + (s // 2 - 1))
                    e.dma_start(WA[:, s, :, :], w_ada[:, :, ds((i * 4 + s) * P, P)]).then_inc(ld_wa[s], 16)
            for kind in "qkv":
                off = "qkv".index(kind) * D
                e.dma_start(W[:, slot[kind], :, :], w_in[:, :, off:off + P]).then_inc(ld_w[kind], 16)

            def head(h, more):
                for d in range(2):
                    e.wait_ge(pe_dn.sem, pe_dn.value(h - 1, f"ks {NT - 1} b"))
                    e.wait_ge(dve_dn.sem, dve_dn.value(h - 1, f"S {NT - 2} b"))
                    e.dma_start(S[:, d, :], A["state_dn"][0, 0, d, ds(h, 1), :, :].rearrange("o k v -> k (o v)")).then_inc(ld_S, 16)
                e.wait_ge(strip["z"], h + 1)
                e.dma_start(W[:, slot["z"], :, :], w_in[:, :, ds(OFF_Z + h * P, P)]).then_inc(ld_w["z"], 16)
                if more:
                    for kind in "qkv":
                        off = "qkv".index(kind) * D
                        e.wait_ge(strip[kind], h + 1)
                        e.dma_start(W[:, slot[kind], :, :], w_in[:, :, ds(off + (h + 1) * P, P)]).then_inc(ld_w[kind], 16)
                for s in range(4):
                    e.wait_ge(pe_dn.sem, pe_dn.value(h - 1, "ada rows"))
                    e.dma_start(WA[:, s, :, :], w_ada[:, :, ds((16 + h * 4 + s) * P, P)]).then_inc(ld_wa[s], 16)
                def extra_in(j):
                    e.wait_ge(strip_e, h * NE + (j + 1))
                    e.dma_start(WE, w_in[:, :, ds(OFF_NA + (h * NE + j) * P, P)]).then_inc(ld_e, 16)

                def extra_store(j):
                    e.wait_ge(e_out, h * NE + (j + 2))
                    e.dma_start(ext_dram[ds(h * NE + j, 1), :, :].rearrange("o p c -> p (o c)"), stage[:, j % 2, :]).then_inc(st_e[j % 2], 16)

                if more:
                    extra_in(0)
                    for j in (1, 2, 3):
                        extra_in(j)
                        extra_store(j - 1)
                for d in range(2):
                    e.wait_ge(act_dn.sem, act_dn.value(h, f"state {'fb'[d]}"))
                    e.dma_start(A["new_state"][0, 0, d, ds(h, 1), :, :].rearrange("o k v -> k (o v)"), Sc[:, d, :]).then_inc(st_S, 16)
                if more:
                    extra_store(3)

            e.wait_ge(ada_mm, 9)
            with e.Fori(0, H - 1) as h:
                head(h, True)
            head(H - 1, False)
            for i in range(2):
                e.wait_ge(st_e[i], 16 * NE // 2 * (H - 1) + 16)
            e.dma_start(fk, ext_dram[KP:2 * KP, :, :].rearrange("s p c -> p s c")).then_inc(ld_fq[1], 16) 
            e.wait_ge(pe_dn.sem, pe_dn.value(H - 1, "ada rows"))
            e.dma_start(fq, ext_dram[0:KP, :, :].rearrange("s p c -> p s c")).then_inc(ld_fq[0], 16)
            e.wait_ge(st_S, 16 * 2 * H + 32)

            e.wait_ge(zrow_done, 1)
            e.dma_start(rpb_dram[0:1, 0:32], zrow[:, :]).then_inc(rpb_pad, 16)
            e.dma_start(rpb_dram[0:1, 32 + NA_H * RPB:], zrow[:, :]).then_inc(rpb_pad, 16)
            e.dma_start(rpb_dram[0:1, 32:32 + NA_H * RPB], A["na_rpb"][0].rearrange("h a b -> (h a b)").unsqueeze(0)).then_inc(rpb_pad, 16)
            e.wait_ge(rpb_pad, 48)
            shifted = rpb_dram[0:1, 31:32]
            shifted = bass.AP(shifted.tensor, shifted.offset, [[2 * KC - 1, NA_H * (2 * KR - 1)], [-1, KC], [1, 3 * KC]])
            e.dma_start(rpb_rows_dram[:, :].rearrange("c (r x) -> r c x", x=3 * KC), shifted).then_inc(rpb_rows, 16)
            e.wait_ge(dve_dn.sem, dve_dn.value(H - 1, "o out"))
            e.wait_ge(act_dn.sem, act_dn.value(H - 1, "ada"))
            e.wait_ge(pe_dn.sem, pe_dn.value(H - 1, "turn o"))
            e.wait_ge(pool_dn.sem, pool_dn.value(H - 1, "A"))
            e.dma_start(fv[:, :, :], ext_dram[2 * KP:3 * KP, :, :].rearrange("s p c -> p s c")).then_inc(ld_fq[2], 16)
            e.dma_start(ck[:, :], A["cache_na_k"][0, 0].rearrange("t h d -> t (h d)")).then_inc(ld_nc, 16)
            e.dma_start(cv[:, :], A["cache_na_v"][0, 0].rearrange("t h d -> t (h d)")).then_inc(ld_nc, 16)
            e.dma_start(win[:, :, :], A["window"].rearrange("p (c x) -> p c x", c=CT)).then_inc(ld_nc, 16)
            e.dma_start(ngain[:, 0, :], A["na_qnorm_g"].partition_broadcast(P).rearrange("p o d -> p (o d)")).then_inc(ld_nc, 16)
            e.dma_start(ngain[:, 1, :], A["na_knorm_g"].partition_broadcast(P).rearrange("p o d -> p (o d)")).then_inc(ld_nc, 16)
            e.wait_ge(rpb_rows, 16)

            def bias_in(p, hh):
                for r in range(ROWS):
                    src = rpb_rows_dram[:, ds(((2 * p + hh) * (2 * KR - 1) + KR - 1 - r) * 3 * KC, ROWS * 3 * KC)]
                    e.dma_start(bias[r * KC:(r + 1) * KC, hh, :, :], src.rearrange("c (r x) -> c r x", r=ROWS)).then_inc(ld_bias[hh], 16)

            for hh in range(2):
                bias_in(0, hh)
            e.wait_ge(proj_out, 3 * NT)
            e.dma_start(A["new_v"][0, 0].rearrange("t h d -> t (h d)"), qkv[:, 2, CT, :]).then_inc(st_v, 16)

            pa_w = A["w_pa"][0].rearrange("(k p) n -> p k n", p=P)
            pb_w = A["w_pb"][0].rearrange("(k p) n -> p k n", p=P)
            merge_w = ((pa_w, KD), (pb_w, KP)) * 2

            def merge_in(f, i):
                w, k = merge_w[i]
                e.dma_start(W[:, i, 0:k, :], w[:, :, ds((2 * f + i // 2) * P, P)]).then_inc(ld_m[i], 16)

            e.wait_ge(proj_mm, 2 * NT)
            for i in range(4):
                merge_in(0, i)

            def pair(p, more):
                following = e.snap(p + 1) if more else None
                e.wait_ge(dve_na.sem, dve_na.value(p, "k rows"))
                e.dma_start(A["new_k"][0, 0].rearrange("t h d -> t (h d)")[:, ds(p * P, P)], krow_n[:, CT, :]).then_inc(st_k, 16)
                if more:
                    for hh in range(2):
                        e.wait_ge(pool_na.sem, pool_na.value(p, f"bias {hh}"))
                        bias_in(following, hh)

            with e.Fori(0, KP - 1) as p:
                pair(p, True)
            pair(KP - 1, False)
            e.wait_ge(st_k, 16 * KP + 16)
            e.wait_ge(st_v, 16)

            def gates_in(f, i):
                for g in range(2):
                    src = ext_dram[ds(3 * KP + g * KD + 2 * f + i, 1), :, :].rearrange("o p c -> p (o c)")
                    e.dma_start(gates[:, i, g, :], src).then_inc(ld_g[i], 16)

            e.wait_ge(act_na.sem, act_na.value(KP - 1, "out"))
            e.wait_ge(dve_na.sem, dve_na.value(KP - 1, f"P {NU - 1}"))
            e.wait_ge(pool_na.sem, pool_na.value(KP - 1, "bias 1"))
            for i in range(2):
                gates_in(0, i)
            with e.Fori(1, KD // 2) as f:
                for i in range(2):
                    for n in (2 * i, 2 * i + 1):
                        wait_apart(e, zrow_done, (pe_mg.sem, pe_mg.value(f - 1, pe_mg.names[n])))
                        merge_in(f, n)
                    wait_apart(e, zrow_done, (act_mg.sem, act_mg.value(f - 1, f"g{i}")))
                    gates_in(f, i)

            wo = A["w_out"][0].rearrange("(k p) n -> p k n", p=P)
            for i, name in enumerate(pe_mg.names):
                e.wait_ge(pe_mg.sem, pe_mg.value(KD // 2 - 1, name))
                e.dma_start(W[:, i, :, :], wo[:, :, i * P:(i + 1) * P]).then_inc(ld_o[i], 16)
            for i in range(4):
                e.wait_ge(pe_wo.sem, pe_wo.value(0, f"o{i}"))
                e.dma_start(W[:, i, :, :], wo[:, :, (4 + i) * P:(5 + i) * P]).then_inc(ld_o[i], 16)

            f1 = [A[w][0].rearrange("(k p) n -> p k n", p=P) for w in ("ffn_w1", "ffn_w3")]
            f2 = A["ffn_w2"][0].rearrange("(k p) n -> p k n", p=P)

            def ffn_in(f, i):
                e.dma_start(W[:, i, :, :], f1[i % 2][:, :, ds((2 * f + i // 2) * P, P)]).then_inc(ld_f[i], 16)

            for i in range(4):
                e.wait_ge(pe_wo.sem, pe_wo.value(1, f"o{i}"))
                ffn_in(0, i)
            with e.Fori(1, KF // 2) as f:
                for i, name in enumerate(pe_f1.names):
                    e.wait_ge(pe_f1.sem, pe_f1.value(f - 1, name))
                    ffn_in(f, i)
            for i in range(2):
                e.dma_start(W2[:, i, :, :], f2[:, :, i * P:(i + 1) * P]).then_inc(ld_f2[i], 16)

            def y_out(n, i):
                e.wait_ge(act_f2.sem, act_f2.value(n, f"y{i}"))
                c = ds((2 * n + i) * P, P)
                e.dma_start(A["y_sample"][0].rearrange("(t p) c -> p t c", p=P)[:, :, c], yo[:, i, 0:CT, :]).then_inc(st_y[i], 16)
                e.dma_start(A["y_prompt"][0][:, c], yo[:, i, CT, :]).then_inc(st_y[i], 16)

            with e.Fori(1, KD // 2) as n:
                for i in range(2):
                    e.wait_ge(pe_f2.sem, pe_f2.value(n - 1, f"m{i}"))
                    e.dma_start(W2[:, i, :, :], f2[:, :, ds((2 * n + i) * P, P)]).then_inc(ld_f2[i], 16)
                for i in range(2):
                    y_out(n - 1, i)
            for i in range(2):
                y_out(KD // 2 - 1, i)
            for i in range(2):
                e.wait_ge(st_y[i], 32 * (KD // 2))

        @block.tensor
        def _(e):
            e.wait_ge(ld_const, 32)
            e.wait_ge(ld_vec, 16 * 7)
            e.transpose(ps[:, 0, 0:81], rows[0:81, 0, :], sq_c[0:81, ID, 0:81])
            e.transpose(ps[:, 0, 128:200], rows[0:72, 1, :], sq_c[0:72, ID, 0:72]).then_inc(vec_turned, 1)
            for t in range(NT):
                e.wait_ge(ld_x[t], 16)
                for j in range(2):
                    n = 2 * t + j
                    if n >= 4:
                        e.wait_ge(x_out, n - 3)
                    for k in range(4):
                        m = e.transpose(ps[:, 1 + n % 4, k * P:(k + 1) * P], xin[:, t, (4 * j + k) * P:(4 * j + k + 1) * P], IDN)
                    m.then_inc(x_turned, 1)
            for k in range(KD):
                e.wait_ge(sq_done, k + 1)
                for b, (a, n) in enumerate(SEG):
                    m = e.matmul(ps[:, 5 + b, 0:n], ONES, sqx[:, k % 2, a:a + n], start=k == 0, stop=k == KD - 1, skip_group_check=True)
                m.then_inc(ss_done, 1)
            def ada_rows(dst, s):
                for k in range(KD):
                    m = e.matmul(dst, csT[:, :, k], WA[:, s:s + 2, k, :], start=k == 0, stop=k == KD - 1, skip_group_check=True)
                return m

            e.wait_ge(cond_silu, 1)
            e.wait_ge(x_out, 2 * NT)
            with e.Fori(0, 4) as i:
                for s in (0, 2):
                    for n in (s, s + 1):
                        e.wait_ge(ld_wa[n], i * 16 + 16)
                    e.wait_ge(ada_row, i * 2 + s // 2 + 1)
                    ada_rows(ps[0:2, 3 + s // 2, 0:2 * P], s).then_inc(ada_mm, 1)
            e.wait_ge(ada_row, 10)
            for c in range(16):
                m = e.transpose(ps[:, 7, 2 * c:2 * c + 2], arow0[0:2, c * P:(c + 1) * P], sq_c[0:2, ID, 0:2])
            m.then_inc(ada_mm, 1)
            e.wait_ge(h_done, KD)
            e.wait_ge(ld_ba, 48)
            for t in range(NT):
                for k in range(KD):
                    m = e.matmul(ps[:, 1, t * 32:(t + 1) * 32], hT[:, k, t * P:(t + 1) * P], wba[:, k, :], start=k == 0, stop=k == KD - 1, skip_group_check=True)
            m.then_inc(ba_mm, 1)
            e.wait_ge(ba_dve, 6)
            gl = sp[:, 3, :, :]
            for n, (mat, d) in enumerate(((LE, 0), (GE, 1), (GT, 0), (LT, 1), (ONE, 0), (ONE, 1))):
                m = e.matmul(ps[:, 2, n * 40:(n + 1) * 40], sq_c[:, mat, :], gl[:, :, d * H:(d + 1) * H], start=True, stop=True, skip_group_check=True)
            m.then_inc(cum_mm, 1)

            def strip_mm(kind, k, h1):
                if k == 0:
                    e.wait_ge(ld_w[kind], h1 * 16)
                for b, (a, n) in enumerate(SEG):
                    m = e.matmul(ps[:, b, 0:n], W[:, slot[kind], k, :], hT[:, k, a:a + n], start=k == 0, stop=k == KD - 1, skip_group_check=True)
                if k == KD - 1:
                    m.then_inc(strip[kind], 1)

            e.wait_ge(vec_out, 1)
            for kind, before in (("q", None), ("k", "q"), ("v", "k")):
                if before:
                    e.wait_ge(raw[before], 1)
                for k in range(KD):
                    strip_mm(kind, k, 1)
            e.sem_inc(strip_e, 1)
            e.sem_inc(pe_dn.sem, pe_dn.n)

            def head(h, more):
                def wait(steps, name, turn=h):
                    e.wait_ge(steps.sem, steps.value(turn, name))

                fill = [(kind, k) for kind in ("k", 1, "v", 2) for k in range(KD)] if more else []
                zfill = [("z", k) for k in range(KD)]

                def filler(queue, n=1):
                    for _ in range(min(n, len(queue))):
                        kind, k = queue.pop(0)
                        if k == 0:
                            if kind == "z" and not more:
                                e.wait_ge(e_out, h * NE + 1)
                            elif kind == "v":
                                e.wait_ge(e_out, h * NE + 3)
                            elif kind in ("k", "z"):
                                e.wait_ge(e_out, h * NE + (2 if kind == "k" else 4))
                            else:
                                e.wait_ge(raw[{1: "k", 2: "v"}[kind]], h + 2)
                        if kind in (1, 2):
                            extra_mm(kind, k)
                        else:
                            strip_mm(kind, k, h + 1 if kind == "z" else h + 2)

                def extra_mm(j, k):
                    if k == 0:
                        e.wait_ge(ld_e, h * (16 * NE) + 16 * (j + 1))
                    for b, (a, n) in enumerate(SEG):
                        m = e.matmul(ps[:, b, 0:n], WE[:, k, :], hT[:, k, a:a + n], start=k == 0, stop=k == KD - 1, skip_group_check=True)
                    if k == KD - 1:
                        m.then_inc(strip_e, 1)

                wait(pool_dn, "g mask")
                wait(dve_dn, "o out", h - 1)
                wait(act_dn, "ada", h - 1)
                for d in range(2):
                    e.matmul(ps[:, 2 + d, :], sq_c[:, (GT, LT)[d], :], gm[:, d * NT:d * NT + CT, :], start=True, stop=True)
                    m = e.matmul(ps[:, 4, d * P:(d + 1) * P], sq_c[:, (GT, LT)[d], :], gm[:, d * NT + CT, :], start=True, stop=True, skip_group_check=True)
                pe_dn.done(m, "dt")
                if more:
                    e.wait_ge(e_out, h * NE + 1)
                    e.wait_ge(raw["v"], h + 1)
                    for k in range(KD):
                        strip_mm("q", k, h + 2)
                wait(act_dn, "square")
                for w in range(2):
                    for t in range(NT):
                        m = e.matmul(ps[:, 7, 256 + w * NT + t:257 + w * NT + t], sqkq[:, t, w, :], sq_c[:, ONE, 0:1], start=True, stop=True, skip_group_check=True)
                pe_dn.done(m, "norm")
                for t in range(NT):
                    m = e.matmul(ps[:, 5 + t // 2, (t % 2) * 256:(t % 2) * 256 + 256], kq[:, t, 0, :], kq[:, t, :, :], start=True, stop=True, skip_group_check=True)
                pe_dn.done(m, "kq")
                wait(act_dn, "decay")
                wait(act_dn, "silu v")
                for w in range(2):
                    for t in range(NT):
                        at = 1 + t * P + (t == CT)
                        src = kq[:, t, 0, :] if w == 0 else conv[:, 2, at:at + P]
                        dst = ps[:, 2 + w, t * P:(t + 1) * P] if t < CT else ps[:, 4, w * P:(w + 1) * P]
                        m = e.transpose(dst, src, IDN)
                pe_dn.done(m, "turn k v")
                if more:
                    e.wait_ge(raw["q"], h + 2)
                    for k in range(KD):
                        extra_mm(0, k)
                wait(act_dn, "L diag")
                wait(dve_dn, "L diag")
                for u in range(U):
                    m = e.matmul(ps[:, 5, u * 32:(u + 1) * 32], LNTd[:, u, :], lv_c[:, 2 * len(LEVELS), :], start=True, stop=True, skip_group_check=True)
                pe_dn.done(m, "P0")
                for n in range(1, 6):
                    filler(fill, (3, 2, 3)[(2 * n - 2) % 3])
                    wait(dve_dn, f"X{n - 1}")
                    if n == 5:
                        wait(act_dn, "L pairs")
                    for u in range(U):
                        m = e.matmul(ps[:, 5, u * 32:(u + 1) * 32], (LNTd if n < 5 else LNTp)[:, u, :], Xc[:, u, :], start=True, stop=True, skip_group_check=True)
                    pe_dn.done(m, f"P{n}")
                    filler(fill, (3, 2, 3)[(2 * n - 1) % 3])
                    wait(dve_dn, f"XT{n - 1}")
                    if n < 5:
                        wait(dve_dn, f"P{n}")
                    else:
                        wait(act_dn, "P5")
                    for u in range(U):
                        m = e.matmul(ps[:, 6, u * 32:(u + 1) * 32], XTd[:, u, :], Pc[:, u, :], start=True, stop=True, skip_group_check=True)
                    pe_dn.done(m, f"Y{n}")
                filler(fill, 2)
                wait_apart(e, vec_out, (act_dn.sem, act_dn.value(h, "Y5")), (dve_dn.sem, dve_dn.value(h, "Y5")))
                for u in range(U):
                    lo, hi, d = (0, 64, 0) if u < NT else (64, 0, 1)
                    c = (u % NT) * 64
                    m = e.matmul(ps[hi:hi + 64, 5 + d, c:c + 64], LNT[lo:lo + 64, u, hi:hi + 64], X64[lo:lo + 64, u, :], start=True, stop=True, skip_group_check=True)
                pe_dn.done(m, "P6")
                filler(fill, 3)
                wait_apart(e, vec_out, (act_dn.sem, act_dn.value(h, "P6")), (dve_dn.sem, dve_dn.value(h, "P6")))
                for u in range(U):
                    lo, hi, d = (0, 64, 0) if u < NT else (64, 0, 1)
                    c = (u % NT) * 64
                    m = e.matmul(ps[lo:lo + 64, 2 + d, c:c + 64], P6c[hi:hi + 64, u, :], XT[hi:hi + 64, u, hi:hi + 64], start=True, stop=True, skip_group_check=True)
                pe_dn.done(m, "Y6")
                wait(act_dn, "Y6")
                wait(dve_dn, "Y6")
                wait(pool_dn, "kd")
                wait(pool_dn, "A")
                e.wait_ge(ld_S, 32 * (h + 1))
                for s in range(NT):
                    tile = ((CT, CT), (0, 3), (1, 2), (2, 1), (3, 0))[s]
                    if s:
                        for d in range(2):
                            if s > 1:
                                wait(dve_dn, f"S {s - 1} {'fb'[d]}")
                            for w in range(2):
                                m = e.matmul(ps[:, 2 + d, w * P:(w + 1) * P], kq[:, tile[d], w, :], S[:, d, :], start=True, stop=True, skip_group_check=True)
                            pe_dn.done(m, f"ks {s} {'fb'[d]}")
                        filler(zfill)
                    for d in range(2):
                        u = d * NT + tile[d]
                        if s:
                            wait(dve_dn, f"r {s} {'fb'[d]}")
                        m = e.matmul(ps[:, (4, 6)[d], 0:P], XT[:, u, :], rr[:, d, :] if s else vrow[:, CT, :], start=True, stop=True)
                        pe_dn.done(m, f"y {s} {'fb'[d]}")
                    filler(zfill)
                    for d in range(2):
                        u = d * NT + tile[d]
                        wait(act_dn, f"v {s} {'fb'[d]}")
                        if s:
                            wait(dve_dn, f"o {s - 1} {'fb'[d]}")
                        if s == 1:
                            wait(act_dn, f"state {'fb'[d]}")
                        if s < NT - 1:
                            e.matmul(ps[:, (5, 7)[d], P:2 * P], kd[:, u, :], vn[:, d, :], start=True, stop=True, skip_group_check=True)
                        m = e.matmul(ps[:, (5, 7)[d], 0:P], AT[:, u, :], vn[:, d, :], start=True, stop=True, skip_group_check=True)
                        pe_dn.done(m, f"av {s} {'fb'[d]}")
                filler(zfill, 99)
                wait(act_dn, f"v {NT - 1} f")
                for s in (0, 2):
                    for n in (s, s + 1):
                        e.wait_ge(ld_wa[n], h * 16 + 80)
                    m = ada_rows(ps[0:2, 4, s * P:(s + 2) * P], s)
                pe_dn.done(m, "ada rows")
                if more:
                    wait(act_dn, "silu z")
                    for k in range(KD):
                        extra_mm(3, k)
                wait_apart(e, vec_out, (act_dn.sem, act_dn.value(h, "ada rows")), (dve_dn.sem, dve_dn.value(h, f"o {NT - 1} b")))
                for s in range(4):
                    m = e.transpose(ps[:, 7, 272 + 2 * s:274 + 2 * s], arow[0:2, s * P:(s + 1) * P], sq_c[0:2, ID, 0:2])
                pe_dn.done(m, "ada")
                wait(dve_dn, "o normed")
                for t in range(NT):
                    dst = ps[:, 2, t * P:(t + 1) * P] if t < CT else ps[:, 3, 0:P]
                    m = e.transpose(dst, osum[:, t, :], IDN)
                pe_dn.done(m, "turn o")

            with e.Fori(0, H - 1) as h:
                head(h, True)
            head(H - 1, False)

            e.wait_ge(act_dn.sem, act_dn.value(H - 1, "ada"))
            e.wait_ge(dve_dn.sem, dve_dn.value(H - 1, "o out"))
            for j in range(3):
                e.wait_ge(ld_fq[j], 16)
                for t in range(NT):
                    n = j * NT + t
                    if n >= 4:
                        e.wait_ge(proj_out, n - 3)
                    for s in range(KP):
                        m = e.transpose(ps[:, n % 4, s * P:(s + 1) * P], (fq, fk, fv)[j][:, s, t * P:(t + 1) * P], IDN)
                    m.then_inc(proj_mm, 1)
            e.wait_ge(proj_out, 3 * NT)
            e.sem_inc(pe_na.sem, pe_na.n)

            def pair(p):
                def wait(steps, name, turn=p):
                    e.wait_ge(steps.sem, steps.value(turn, name))

                def score(i):
                    hh, c = UNITS[i]
                    tiles, at, _ = key_tiles(c)
                    rows_ = slice(64 * hh, 64 * hh + 64)
                    if i >= 2:
                        wait(dve_na, f"max {i - 2}")
                    q = qT[rows_, c, :] if c < CT else cT[rows_, 0, :]
                    if tiles:
                        keys = kT[rows_, tiles[0]:tiles[-1] + 1, :]
                        e.matmul(ps[:, i % 2, at:at + len(tiles) * P], q, keys, start=True, stop=True, skip_group_check=True)
                    m = e.matmul(ps[:, i % 2, 3 * P:4 * P], q, cT[rows_, 2 if c < CT else 1, :], start=True, stop=True, skip_group_check=True)
                    pe_na.done(m, f"score {i}")

                wait(dve_na, "k rows")
                wait(act_na, "T lat", p - 1)
                wait(dve_na, "T ctx", p - 1)
                wait(act_na, "out", p - 1)
                for t in range(CT):
                    e.transpose(ps[:, 6, t * P:(t + 1) * P], qrow[:, t, :], IDN)
                    e.transpose(ps[:, 7, t * P:(t + 1) * P], krow_n[:, t, :], IDN)
                e.transpose(ps[:, 5, 0:P], qrow[:, CT, :], IDN)
                e.transpose(ps[:, 5, P:2 * P], krow_n[:, CT, :], IDN)
                pe_na.done(e.transpose(ps[:, 5, 2 * P:3 * P], krow_n[:, NT, :], IDN), "turn")
                wait(act_na, "T lat")
                wait(dve_na, "T ctx")
                score(0)
                score(1)
                wait(act_na, "v rows")
                for i, (hh, c) in enumerate(UNITS):
                    tiles, at, _ = key_tiles(c)
                    chunks = [(at // P + j, t) for j, t in enumerate(tiles)] + [(3, NT if c < CT else CT)]
                    wait(dve_na, f"P {i}")
                    if i >= 2:
                        wait(act_na, f"PT {i - 2}")
                    for b, _ in chunks:
                        m = e.transpose(ps[:, 2 + i % 2, b * P:(b + 1) * P], Sx[:, i % 2, b * P:(b + 1) * P], IDN)
                    pe_na.done(m, f"turn P {i}")
                    if i + 2 < NU:
                        score(i + 2)
                    wait(act_na, f"PT {i}")
                    out = ps[64 * hh:64 * hh + 64, 4, c * P:(c + 1) * P] if c < CT else ps[64 * hh:64 * hh + 64, 5, 3 * P:4 * P]
                    for j, (b, t) in enumerate(chunks):
                        m = e.matmul(out, vrow_n[:, t, 64 * hh:64 * hh + 64], PT[:, i % 2, b * P:(b + 1) * P],
                                     start=j == 0, stop=j == len(chunks) - 1, skip_group_check=True)
                    pe_na.done(m, f"PV {i}")

            with e.Fori(0, KP) as p:
                pair(p)

            def product(bank, w, k_n, x, wait_k=None):
                for k in range(k_n):
                    if wait_k:
                        e.wait_ge(wait_k, k + 1)
                    for b, (a, n) in enumerate(SEG):
                        m = e.matmul(ps[:, bank + b, 0:n], w[:, k, :], x[:, k, a:a + n], start=k == 0, stop=k == k_n - 1, skip_group_check=True)
                return m

            e.wait_ge(act_na.sem, act_na.value(KP - 1, "out"))
            e.sem_inc(pe_mg.sem, pe_mg.n)
            with e.Fori(0, KD // 2) as f:
                for i, name in enumerate(pe_mg.names):
                    e.wait_ge(ld_m[i], f * 16 + 16)
                    e.wait_ge(dve_mg.sem, dve_mg.value(f - 1, "y" + name[1:]))
                    x, k_n = ((oT, KD), (naT, KP))[i % 2]
                    pe_mg.done(product(2 * i, W[:, i, :, :], k_n, x), name)

            e.wait_ge(dve_mg.sem, dve_mg.value(KD // 2 - 1, "y1"))
            e.sem_inc(pe_wo.sem, 4)
            with e.Fori(0, 2) as j:
                for i in range(4):
                    e.wait_ge(ld_o[i], j * 16 + 16)
                    e.wait_ge(dve_wo.sem, dve_wo.value(j - 1, f"x{i}"))
                    pe_wo.done(product(2 * i, W[:, i, :, :], KD, yT), f"o{i}")
            e.wait_ge(sq2_done, KD)
            e.wait_ge(dve_wo.sem, dve_wo.value(1, "x3"))
            for t in range(NT):
                for k in range(KD):
                    m = e.matmul(ps[:, 0, t:t + 1], hT[:, k, t * P:(t + 1) * P], sq_c[:, ONE, 0:1], start=k == 0, stop=k == KD - 1, skip_group_check=True)
            m.then_inc(ss2_mm, 1)
            e.wait_ge(dg2_done, 2)
            e.matmul(ps[:, 6, :], ONES, dg2[:, 0:CT, :], start=True, stop=True)
            e.matmul(ps[:, 7, 0:P], ONES, dg2[:, CT, :], start=True, stop=True).then_inc(rstd2_mm, 1)

            e.sem_inc(pe_f1.sem, 4)
            e.wait_ge(xn2_done, KD)
            e.wait_ge(h2_done, KD)
            with e.Fori(0, KF // 2) as f:
                for i, name in enumerate(pe_f1.names):
                    e.wait_ge(ld_f[i], f * 16 + 16)
                    if i % 2 == 0:
                        e.wait_ge(act_f1.sem, act_f1.value(f - 1, name))
                    else:
                        e.wait_ge(dve_f1.sem, dve_f1.value(f - 1, f"h{i // 2}"))
                    pe_f1.done(product(2 * i, W[:, i, :, :], KD, hT), name)
            e.wait_ge(dve_f1.sem, dve_f1.value(KF // 2 - 1, "h1"))
            e.sem_inc(pe_f2.sem, 4)
            with e.Fori(0, KD // 2) as n:
                for i in range(2):
                    e.wait_ge(ld_f2[i], n * 16 + 16)
                    e.wait_ge(dve_f2.sem, dve_f2.value(n - 1, f"x{i}"))
                    pe_f2.done(product(2 * i, W2[:, i, :, :], KF, act), f"m{i}")
                for i in range(2):
                    e.wait_ge(dve_f2.sem, dve_f2.value(n, f"x{i}"))
                    e.wait_ge(act_f2.sem, act_f2.value(n - 1, f"y{i}"))
                    for t in range(NT):
                        m = e.transpose(ps[:, 4 + 2 * i + t // CT, (t % CT) * P:(t % CT + 1) * P], xo[:, i, t * P:(t + 1) * P], IDN)
                    pe_f2.done(m, f"turn {i}")

        @block.scalar
        def _(e):
            e.wait_ge(vec_turned, 1)
            e.activation(csT[:, :, :], ps[:, 0, 65:81].rearrange("p (a k) -> p a k", a=2), ACT.Silu).then_inc(cond_silu, 1)
            e.activation(cols[:, 0:65], ps[:, 0, 0:65], ACT.Copy)
            e.activation(cols[:, CONV:CONV + 72], ps[:, 0, 128:200], ACT.Copy).then_inc(vec_out, 1)
            for t in range(NT):
                for j in range(2):
                    n = 2 * t + j
                    e.wait_ge(x_turned, n + 1)
                    e.activation(xT[:, 4 * j:4 * j + 4, t * P:(t + 1) * P], ps[:, 1 + n % 4, :].rearrange("p (k c) -> p k c", k=4), ACT.Copy).then_inc(x_out, 1)
            e.wait_ge(x_out, 2 * NT)
            for k in range(KD):
                if k >= 2:
                    e.wait_ge(ss_done, k - 1)
                e.activation(sqx[:, k % 2, :], xT[:, k, :], ACT.Square).then_inc(sq_done, 1)
            e.wait_ge(ss_done, KD)
            e.wait_ge(zero_done, 1)
            for b, (a, n) in enumerate(SEG):
                m = e.activation(rms[:, a:a + n], ps[:, 5 + b, 0:n], ACT.Sqrt, bias=epsc[:, 0:1], scale=1.0 / D)
            m.then_inc(rms_done, 1)
            e.sem_inc(ada_row, 2)
            with e.Fori(0, 4) as i:
                for s in range(2):
                    e.wait_ge(ada_mm, i * 2 + (s + 1))
                    e.activation(arow0[0:2, ds(i * 4 * P + s * 2 * P, 2 * P)], ps[0:2, 3 + s, 0:2 * P], ACT.Copy).then_inc(ada_row, 1)
            e.wait_ge(ld_ba, 48)
            e.activation(alog[:, :], alog[:, :], ACT.Exp).then_inc(ba_act, 1)
            e.wait_ge(ba_dve, 1)
            e.activation(sp[:, 1, :, :], sp[:, 0, :, :], ACT.Abs).then_inc(ba_act, 1)
            e.wait_ge(ba_act, 2)
            e.activation(sp[:, 2, :, :], sp[:, 1, :, :], ACT.Exp, scale=-1.0).then_inc(ba_act, 1)
            e.wait_ge(ba_act, 3)
            e.activation(sp[:, 1, :, :], sp[:, 2, :, :], ACT.Ln, bias=1.0).then_inc(ba_act, 1)
            bet = ba[:, :, 0:2 * H].rearrange("p t (d h) -> p t d h", d=2)
            e.wait_ge(ba_dve, 1)
            pu = params[:, :, :, :].rearrange("p h k (d t) -> p h k d t", d=2)
            for d in range(2):
                e.activation(pu[:, :, BETA, d, :].rearrange("p h t -> p t h"), bet[:, :, d, :], ACT.Sigmoid)
            e.wait_ge(cum_mm, 1)
            for n in range(6):
                kind, d = (EG, EG, EK, EK, GL, GL)[n], n % 2
                src = ps[:, 2, n * 40:(n + 1) * 40].rearrange("p (t h) -> p t h", h=H)
                m = e.activation(pu[:, :, kind, d, :].rearrange("p h t -> p t h"), src, ACT.Exp)
            m.then_inc(prm_done, 1)

            def raw_out(kind, h1):
                j = "qkv".index(kind)
                e.wait_ge(strip[kind], h1)
                e.activation(raws[:, j, 1:1 + LAT], ps[:, 0, :], ACT.Copy)
                e.activation(raws[:, j, 2 + LAT:2 + TOK], ps[:, 1, 0:CTX], ACT.Copy).then_inc(raw[kind], 1)

            def extra_out(j, h):
                e.wait_ge(strip_e, h * NE + (j + 2))
                e.wait_ge(st_e[j % 2], h * (16 * NE // 2) + 16 * (j // 2) + 16)
                blocks = ps[:, 0, :].rearrange("p (r b c) -> p b r c", r=ROWS, c=KC)
                e.activation(stage[:, j % 2, 0:LAT].rearrange("p (b r c) -> p b r c", b=CT, c=KC), blocks, ACT.Copy)
                e.activation(stage[:, j % 2, LAT:TOK], ps[:, 1, 0:CTX], ACT.Copy).then_inc(e_out, 1)

            e.wait_ge(zero_done, 2)
            for kind in "qkv":
                raw_out(kind, 1)
            for i in range(2):
                e.sem_inc(st_e[i], 16)
            e.sem_inc(e_out, 1)
            e.sem_inc(act_dn.sem, act_dn.n)

            def head(h, more):
                def wait(steps, name, turn=h):
                    e.wait_ge(steps.sem, steps.value(turn, name))

                wait(pe_dn, "dt")
                wait(dve_dn, "L", h - 1)
                wait(pool_dn, "A", h - 1)
                for d in range(2):
                    e.activation(dt[:, d * NT:d * NT + CT, :], ps[:, 2 + d, :].rearrange("p (t c) -> p t c", t=CT), ACT.Exp)
                    m = e.activation(dt[:, d * NT + CT, :], ps[:, 4, d * P:(d + 1) * P], ACT.Exp)
                act_dn.done(m, "decay")
                wait(pe_dn, "turn o", h - 1)
                for kind in "qkv":
                    j = "qkv".index(kind)
                    wait(dve_dn, f"conv {kind}")
                    lat, ctx = conv[:, j, 1:1 + LAT], conv[:, j, 2 + LAT:2 + TOK]
                    to_lat, to_ctx = (lat, ctx) if kind == "v" else (kq[:, 0:CT, 1 - j, :], kq[:, CT, 1 - j, :])
                    if kind != "v":
                        lat = lat.rearrange("p (t c) -> p t c", t=CT)
                    e.activation(to_lat, lat, ACT.Silu)
                    m = e.activation(to_ctx, ctx, ACT.Silu)
                    act_dn.done(m, f"silu {kind}")
                wait(act_dn, "silu k")
                act_dn.done(e.activation(sqkq[:, :, :, :], kq[:, :, :, :], ACT.Square), "square")
                if more:
                    raw_out("q", h + 2)
                wait(pe_dn, "norm")
                wait(pe_dn, "kq")
                e.activation(nrm[:, 0, :], ps[:, 7, 256:256 + NT], ACT.Sqrt, bias=epsc[:, 0:1], scale=1.0)
                m = e.activation(nrm[:, 1, :], ps[:, 7, 256 + NT:256 + 2 * NT], ACT.Sqrt, bias=epsc[:, 1:2], scale=float(DK))
                act_dn.done(m, "norm")
                wait(pool_dn, "A", h - 1)
                for b in range(3):
                    n = 2 if b < 2 else 1
                    m = e.activation(kqs[:, 2 * b:2 * b + n, :, :], ps[:, 5 + b, 0:n * 256].rearrange("p (t w c) -> p t w c", t=n, w=2), ACT.Copy)
                act_dn.done(m, "kq")
                wait(pe_dn, "turn k v")
                wait(pool_dn, "kd", h - 1)
                act_dn.done(e.activation(krow[:, 0:CT, :], ps[:, 2, :].rearrange("p (t c) -> p t c", t=CT), ACT.Copy), "k rows")
                wait(dve_dn, "L")
                for q in (2, 3):
                    m = e.activation(LNTd[q * 32:q * 32 + 32, :, q * 32:q * 32 + 32], LNT[q * 32:q * 32 + 32, :, q * 32:q * 32 + 32], ACT.Copy)
                act_dn.done(m, "L diag")
                for p, c, u in ((0, 32, 0), (64, 96, 0), (32, 0, NT), (96, 64, NT)):
                    m = e.activation(LNTp[p:p + 32, u:u + NT, c:c + 32], LNT[p:p + 32, u:u + NT, c:c + 32], ACT.Copy)
                act_dn.done(m, "L pairs")
                if more:
                    extra_out(0, h)
                    raw_out("k", h + 2)
                    extra_out(1, h)
                    raw_out("v", h + 2)
                wait(pe_dn, "P5")
                act_dn.done(e.activation(Pc[:, :, :], ps[:, 5, 0:U * 32].rearrange("p (u c) -> p u c", u=U), ACT.Copy), "P5")
                wait(pe_dn, "Y5")
                act_dn.done(e.activation(Yc[:, :, :], ps[:, 6, 0:U * 32].rearrange("p (u c) -> p u c", u=U), ACT.Copy), "Y5")
                wait(pe_dn, "P6")
                act_dn.done(e.activation(P6c[64:128, 0:NT, :], ps[64:128, 5, 0:NT * 64].rearrange("p (u c) -> p u c", u=NT), ACT.Copy), "P6")
                if more:
                    extra_out(2, h)
                wait(pe_dn, "Y6")
                act_dn.done(e.activation(XT[0:64, 0:NT, 64:128], ps[0:64, 2, 0:NT * 64].rearrange("p (u c) -> p u c", u=NT), ACT.Copy), "Y6")
                for s in range(NT):
                    tile = ((CT, CT), (0, 3), (1, 2), (2, 1), (3, 0))[s]
                    if s:
                        for d in range(2):
                            u = d * NT + tile[d]
                            wait(pe_dn, f"ks {s} {'fb'[d]}")
                            if s > 1:
                                wait(dve_dn, f"o {s - 1} {'fb'[d]}")
                            wait(dve_dn, f"r {s} {'fb'[d]}")
                            act_dn.done(e.activation(tq[:, d, :], ps[:, 2 + d, P:2 * P], ACT.Copy, scale=prm[:, EG, u:u + 1]), f"qs {s} {'fb'[d]}")
                    for d in range(2):
                        u = d * NT + tile[d]
                        wait(pe_dn, f"y {s} {'fb'[d]}")
                        if s:
                            wait(pe_dn, f"av {s - 1} {'fb'[d]}")
                        act_dn.done(e.activation(vn[:, d, :], ps[:, (4, 6)[d], 0:P], ACT.Copy, scale=bk[:, 0, u:u + 1]), f"v {s} {'fb'[d]}")
                    if not s:
                        e.wait_ge(st_S, (h * 2 + 2) * 16)
                        for d in range(2):
                            wait(pe_dn, f"av 0 {'fb'[d]}")
                            wait(dve_dn, f"o 0 {'fb'[d]}")
                            act_dn.done(e.activation(Sc[:, d, :], ps[:, (5, 7)[d], P:2 * P], ACT.Copy), f"state {'fb'[d]}")
                e.wait_ge(strip["z"], h + 2)
                wait(dve_dn, "o out", h - 1)
                e.activation(zs[:, 0:LAT], ps[:, 0, :], ACT.Silu)
                act_dn.done(e.activation(zs[:, LAT:TOK], ps[:, 1, 0:CTX], ACT.Silu), "silu z")
                wait(pe_dn, "ada rows")
                wait(pe_dn, "ada", h - 1)
                act_dn.done(e.activation(arow[0:2, :], ps[0:2, 4, :], ACT.Copy), "ada rows")
                wait(dve_dn, "o scaled")
                for t in range(NT):
                    m = e.activation(osq[:, t, :], osc[:, t, :], ACT.Square, accum_out=oss[:, t:t + 1])
                act_dn.done(m, "o square")
                wait(act_dn, "o square")
                act_dn.done(e.activation(orm[:, :], oss[:, :], ACT.Sqrt, bias=epsc[:, 0:1], scale=1.0 / DK), "o norm")
                wait(pe_dn, "ada")
                m = e.activation(mods[:, ds(16 + h * 4, 4), :], ps[:, 7, 272:280].rearrange("p (s c) -> p s c", s=4), ACT.Copy)
                act_dn.done(m, "ada")
                if more:
                    extra_out(3, h)

            with e.Fori(0, H - 1) as h:
                head(h, True)
            head(H - 1, False)

            e.wait_ge(dve_dn.sem, dve_dn.value(H - 1, "o out"))
            e.wait_ge(pe_dn.sem, pe_dn.value(H - 1, "turn o"))
            e.wait_ge(pool_dn.sem, pool_dn.value(H - 1, "A"))
            for j in range(3):
                for t in range(NT):
                    n = j * NT + t
                    e.wait_ge(proj_mm, n + 1)
                    e.activation(qkv[:, j, t, :], ps[:, n % 4, :], ACT.Copy).then_inc(proj_out, 1)
                    if j < 2:
                        if n >= 2:
                            e.wait_ge(nss_done, n - 1)
                        e.wait_ge(proj_out, n + 1)
                        e.activation(nsq[:, n % 2, :], qkv[:, j, t, :], ACT.Square).then_inc(nsq_done, 1)
                if j < 2:
                    e.wait_ge(nss_done, NT * (j + 1))
                    e.activation(nrms[:, j, :, :], nss[:, j, :, :], ACT.Sqrt, bias=epsc[:, 0:1], scale=1.0 / NA_D).then_inc(nrms_done, 1)
            e.wait_ge(ld_nc, 80)
            e.wait_ge(proj_out, 3 * NT)
            e.sem_inc(act_na.sem, act_na.n)

            def pair(p):
                def wait(steps, name, turn=p):
                    e.wait_ge(steps.sem, steps.value(turn, name))

                wait(pe_na, f"PV {NU - 1}", p - 1)
                e.activation(vrow_n[:, 0:NT, :], qkv[:, 2, :, ds(p * P, P)], ACT.Copy)
                act_na.done(e.activation(vrow_n[:, NT, :], cv[:, ds(p * P, P)], ACT.Copy), "v rows")
                wait(pe_na, "turn")
                e.activation(qT[:, :, :], ps[:, 6, :].rearrange("p (t c) -> p t c", t=CT), ACT.Copy)
                act_na.done(e.activation(kT[:, :, :], ps[:, 7, :].rearrange("p (t c) -> p t c", t=CT), ACT.Copy), "T lat")
                for i in range(NU + 1):
                    if i < NU:
                        _, _, (lo, hi) = key_tiles(UNITS[i][1])
                        wait(dve_na, f"-max {i}")
                        m = e.activation(Sx[:, i % 2, lo:hi], Sx[:, i % 2, lo:hi], ACT.Exp, bias=nmx[:, i:i + 1], accum_out=sm[:, i:i + 1])
                        act_na.done(m, f"exp {i}")
                    if i:
                        _, at, (lo, hi) = key_tiles(UNITS[i - 1][1])
                        wait(pe_na, f"turn P {i - 1}")
                        if i >= 3:
                            wait(pe_na, f"PV {i - 3}")
                        act_na.done(e.activation(PT[:, (i - 1) % 2, lo:hi], ps[:, 2 + (i - 1) % 2, lo:hi], ACT.Copy), f"PT {i - 1}")
                wait(pe_na, f"PV {NU - 1}")
                o = naT[:, ds(p, 1), 0:LAT].rearrange("p o (r b c) -> p (o b) r c", r=ROWS, c=KC)
                e.activation(o, ps[:, 4, :].rearrange("p (b r c) -> p b r c", b=CT, c=KC), ACT.Copy)
                act_na.done(e.activation(naT[:, ds(p, 1), LAT:TOK].rearrange("p o c -> p (o c)"), ps[:, 5, 3 * P:4 * P], ACT.Copy), "out")

            with e.Fori(0, KP) as p:
                pair(p)

            e.wait_ge(act_na.sem, act_na.value(KP - 1, "out"))
            e.wait_ge(dve_na.sem, dve_na.value(KP - 1, f"P {NU - 1}"))
            e.wait_ge(st_v, 16)
            e.wait_ge(st_k, 16 * KP + 16)
            e.wait_ge(pool_na.sem, pool_na.value(KP - 1, "bias 1"))
            e.sem_inc(act_mg.sem, 2)
            with e.Fori(0, KD // 2) as f:
                for i in range(2):
                    e.wait_ge(ld_g[i], f * 32 + 32)
                    e.wait_ge(dve_mg.sem, dve_mg.value(f - 1, f"yB{i}"))
                    for g in range(2):
                        blocks = gates[:, i, g, 0:LAT].rearrange("p (b r c) -> p r b c", b=CT, c=KC)
                        e.activation(sgm[:, i, g, 0:LAT].rearrange("p (r b c) -> p r b c", b=CT, c=KC), blocks, ACT.Sigmoid)
                    act_mg.done(e.activation(sgm[:, i, :, LAT:TOK], gates[:, i, :, LAT:TOK], ACT.Sigmoid), f"g{i}")

            e.wait_ge(pe_mg.sem, pe_mg.value(KD // 2 - 1, "pB1"))
            for n in range(KD):
                e.wait_ge(dve_wo.sem, dve_wo.value(n // 4, f"x{n % 4}"))
                e.activation(hT[:, n, :], xT[:, n, :], ACT.Square).then_inc(sq2_done, 1)
            e.wait_ge(ss2_mm, 1)
            e.activation(ss2[:, :], ps[:, 0, 0:NT], ACT.Sqrt, bias=epsc[:, 0:1], scale=1.0 / D).then_inc(rms2_done, 1)
            for k in range(KD):
                e.wait_ge(xn2_done, k + 1)
                for b, (a, n) in enumerate(SEG):
                    m = e.activation(hT[:, k, a:a + n], hT[:, k, a:a + n], ACT.Identity, scale=gain2[:, k, b:b + 1], bias=mods[:, 24 + k, b:b + 1])
                m.then_inc(h2_done, 1)

            e.sem_inc(act_f1.sem, 2)
            with e.Fori(0, KF // 2) as f:
                for i in range(2):
                    e.wait_ge(pe_f1.sem, pe_f1.value(f, f"a{i}"))
                    e.wait_ge(dve_f1.sem, dve_f1.value(f - 1, f"h{i}"))
                    e.activation(sg[:, i, 0:LAT], ps[:, 4 * i, :], ACT.Silu)
                    act_f1.done(e.activation(sg[:, i, LAT:TOK], ps[:, 4 * i + 1, 0:CTX], ACT.Silu), f"a{i}")
            e.sem_inc(act_f2.sem, 2)

            def y_turned(n, first):
                for i in range(2):
                    e.wait_ge(pe_f2.sem, pe_f2.value(n, f"turn {i}"))
                    if not first:
                        e.wait_ge(st_y[i], n * 32)
                    e.activation(yo[:, i, 0:CT, :], ps[:, 4 + 2 * i, :].rearrange("p (t c) -> p t c", t=CT), ACT.Copy)
                    act_f2.done(e.activation(yo[:, i, CT, :], ps[:, 5 + 2 * i, 0:P], ACT.Copy), f"y{i}")

            y_turned(0, True)
            with e.Fori(1, KD // 2) as n:
                y_turned(n, False)

        @block.vector
        def _(e):
            e.memset(epsc[:, 0:1], EPS)
            e.memset(epsc[:, 1:2], DK * EPS).then_inc(zero_done, 1)
            e.wait_ge(rms_done, 1)
            e.reciprocal(rstd[:, :], rms[:, :]).then_inc(rstd_done, 1)
            e.wait_ge(vec_out, 1)
            e.wait_ge(ada_mm, 9)
            b = cols[:, B_ADA:B_ADA + 16].unsqueeze(2).to_broadcast([P, 16, 2])
            e.tensor_tensor(mods[:, 0:16, :], ps[:, 7, 0:32].rearrange("p (s c) -> p s c", s=16), b, ALU.add).then_inc(ada_out, 1)
            e.wait_ge(ada_out, 1)
            e.scalar_tensor_tensor(gain1[:, :, :], mods[:, 8:16, :], 1.0, cols[:, N1:N1 + 8].unsqueeze(2).to_broadcast([P, KD, 2]), ALU.add, ALU.mult).then_inc(gain_done, 1)
            e.wait_ge(gain_done, 1)
            e.wait_ge(rstd_done, 1)
            e.wait_ge(x_out, 2 * NT)
            for k in range(KD):
                e.tensor_tensor(hT[:, k, :], xT[:, k, :], rstd[:, :], ALU.mult).then_inc(xn_done, 1)
                e.wait_ge(xn_done, k + 1)
                for b, (a, n) in enumerate(SEG):
                    m = e.tensor_scalar(hT[:, k, a:a + n], hT[:, k, a:a + n], gain1[:, k, b:b + 1], mods[:, k, b:b + 1], ALU.mult, ALU.add)
                m.then_inc(h_done, 1)
            e.wait_ge(ba_mm, 1)
            e.wait_ge(ld_ba, 48)
            e.tensor_copy(ba[:, :, :], ps[:, 1, 0:NT * 32].rearrange("p (t c) -> p t c", t=NT))
            e.tensor_tensor(sp[:, 0, :, :], ps[:, 1, 0:NT * 32].rearrange("p (t c) -> p t c", t=NT)[:, :, 2 * H:4 * H], dtb[:, :].unsqueeze(1).to_broadcast([P, NT, 2 * H]), ALU.add).then_inc(ba_dve, 1)
            e.wait_ge(ba_dve, 1)
            e.tensor_scalar(sp[:, 3, :, :], sp[:, 0, :, :], 0.0, None, ALU.max).then_inc(ba_dve, 1)
            e.wait_ge(ba_dve, 2)
            e.wait_ge(ba_act, 4)
            e.tensor_tensor(sp[:, 2, :, :], sp[:, 3, :, :], sp[:, 1, :, :], ALU.add).then_inc(ba_dve, 1)
            e.wait_ge(ba_dve, 3)
            e.tensor_scalar(sp[:, 0, :, :], sp[:, 2, :, :], -1.0, None, ALU.mult).then_inc(ba_dve, 1)
            e.wait_ge(ba_dve, 4)
            e.tensor_tensor(sp[:, 3, :, :], sp[:, 0, :, :], alog[:, :].unsqueeze(1).to_broadcast([P, NT, 2 * H]), ALU.mult).then_inc(ba_dve, 1)
            e.wait_ge(ba_dve, 5)
            pu = params[:, :, :, :].rearrange("p h k (d t) -> p h k d t", d=2)
            for d in range(2):
                m = e.tensor_copy(pu[:, :, G, d, :].rearrange("p h t -> p t h"), sp[:, 3, :, d * H:(d + 1) * H])
            m.then_inc(ba_dve, 1)
            e.wait_ge(prm_done, 1)
            e.tensor_scalar(params[:, :, NEG_EG, :], params[:, :, EG, :], -1.0, None, ALU.mult).then_inc(prm_done, 1)
            e.wait_ge(prm_done, 2)
            e.wait_ge(cum_mm, 1)
            e.memset(raws[:, :, :], 0.0).then_inc(zero_done, 1)
            e.memset(LNTd[:, :, :], 0.0)
            e.memset(LNTp[:, :, :], 0.0)
            e.memset(XTd[:, :, :], 0.0)
            e.memset(XT[:, :, :], 0.0)
            e.memset(X64[:, :, :], 0.0)
            e.memset(conv[:, :, :], 0.0).then_inc(zero_done, 1)
            e.wait_ge(zero_done, 3)
            e.sem_inc(dve_dn.sem, dve_dn.n)

            def head(h, more):
                def wait(steps, name, turn=h):
                    e.wait_ge(steps.sem, steps.value(turn, name))

                def done(m, name):
                    dve_dn.done(m, name)

                wait(act_dn, f"v {NT - 1} b", h - 1)
                wait(pool_dn, "kd", h - 1)
                done(e.tensor_copy(prm[:, :, :], params[:, ds(h, 1), :, :].rearrange("p o k u -> p (o k) u")), "prm")
                ctap = cols[:, CONV:CONV + 72].rearrange("p (t j h) -> p t j h", t=3, j=3)
                done(e.tensor_copy(taps[:, :, :], ctap[:, :, :, ds(h, 1)].rearrange("p t j o -> p t (j o)")), "taps")
                wait(dve_dn, "taps")
                w = TOK + 1
                for kind in "qkv":
                    j = "qkv".index(kind)
                    e.wait_ge(raw[kind], h + 1)
                    if kind == "v":
                        wait(pe_dn, "turn k v", h - 1)
                    else:
                        wait(act_dn, f"silu {kind}", h - 1)
                    e.tensor_scalar(conv[:, j, 1:1 + w], raws[:, j, 1:1 + w], taps[:, 1, j:j + 1], None, ALU.mult).then_inc(conv_part, 1)
                    e.wait_ge(conv_part, h * 6 + 2 * j + 1)
                    e.scalar_tensor_tensor(conv[:, j, 1:1 + w], raws[:, j, 0:w], taps[:, 0, j:j + 1], conv[:, j, 1:1 + w], ALU.mult, ALU.add).then_inc(conv_part, 1)
                    e.wait_ge(conv_part, h * 6 + 2 * j + 2)
                    done(e.scalar_tensor_tensor(conv[:, j, 1:1 + w], raws[:, j, 2:2 + w], taps[:, 2, j:j + 1], conv[:, j, 1:1 + w], ALU.mult, ALU.add), f"conv {kind}")
                wait(act_dn, "norm")
                done(e.reciprocal(rn[:, :, :], nrm[:, :, :]), "1/norm")
                wait(dve_dn, "1/norm")
                b2 = prm[:, BETA, :].rearrange("p (d t) -> p d t", d=2)
                bko = bk[:, :, :].rearrange("p s (d t) -> p s d t", d=2)
                rk = rn[:, 0, :].unsqueeze(1).to_broadcast([P, 2, NT])
                done(e.tensor_tensor(bko[:, 1, :, :], b2, rk, ALU.mult), "beta")
                wait(dve_dn, "beta")
                e.tensor_tensor(bko[:, 0, :, :], bko[:, 1, :, :], rk, ALU.mult).then_inc(bk_part, 1)
                e.wait_ge(bk_part, h + 1)
                done(e.tensor_scalar(bk[:, 1, :], bk[:, 0, :], -1.0, None, ALU.mult), "-beta")
                wait(pe_dn, "turn k v")
                vb = nrm[:, 0, 0:CT].unsqueeze(2).to_broadcast([P, CT, P])
                done(e.tensor_tensor(vrow[:, 0:CT, :], ps[:, 3, :].rearrange("p (t c) -> p t c", t=CT), vb, ALU.mult), "v rows")
                e.tensor_scalar(vrow[:, CT, :], ps[:, 4, P:2 * P], nrm[:, 0, CT:CT + 1], None, ALU.mult)
                done(e.tensor_copy(krow[:, CT, :], ps[:, 4, 0:P]), "kv ctx")
                wait(act_dn, "kq")
                wait(pool_dn, "decay")
                wait(dve_dn, "-beta")
                for u in range(U):
                    m = e.scalar_tensor_tensor(LNT[:, u, :], kqs[:, u % NT, 0, :], bk[:, 1, u:u + 1], dtm[:, u, :], ALU.mult, ALU.mult)
                done(m, "L")
                wait(dve_dn, "L")
                for q in (0, 1):
                    m = e.tensor_copy(LNTd[q * 32:q * 32 + 32, :, q * 32:q * 32 + 32], LNT[q * 32:q * 32 + 32, :, q * 32:q * 32 + 32])
                done(m, "L diag")
                pc4, xc4 = typed(Pc[:, :, :]), typed(Xc[:, :, :])
                for n in range(5):
                    wait(pe_dn, f"P{n}")
                    mask = lv_c[:, 2 * n:2 * n + 2, :].unsqueeze(2).to_broadcast([P, 2, NT, 32])
                    done(e.tensor_tensor(pc4, ps[:, 5, 0:U * 32].rearrange("p (d t c) -> p d t c", d=2, t=NT), mask, ALU.mult), f"P{n}")
                    if n:
                        wait(pe_dn, f"Y{n}")
                        done(e.tensor_tensor(Xc[:, :, :], Xc[:, :, :], ps[:, 6, 0:U * 32].rearrange("p (u c) -> p u c", u=U), ALU.add), f"X{n}")
                    else:
                        wait(dve_dn, "P0")
                        done(e.tensor_tensor(Xc[:, :, :], Pc[:, :, :], lv_c[:, 2 * len(LEVELS), :].unsqueeze(1).to_broadcast([P, U, 32]), ALU.add), "X0")
                    wait(dve_dn, f"X{n}")
                    for q in range(4):
                        m = e.transpose(XTd[q * 32:q * 32 + 32, :, q * 32:q * 32 + 32], Xc[q * 32:q * 32 + 32, :, :])
                    done(m, f"XT{n}")
                e.tensor_copy(X64[0:32, 0:NT, 0:32], Xc[0:32, 0:NT, :])
                e.tensor_copy(X64[32:64, 0:NT, 32:64], Xc[32:64, 0:NT, :])
                e.tensor_copy(X64[64:96, NT:U, 0:32], Xc[64:96, NT:U, :])
                done(e.tensor_copy(X64[96:128, NT:U, 32:64], Xc[96:128, NT:U, :]), "X64")
                for q in range(4):
                    m = e.transpose(XT[q * 32:q * 32 + 32, :, q * 32:q * 32 + 32], Xc[q * 32:q * 32 + 32, :, :])
                done(m, "XT diag")
                wait(act_dn, "Y5")
                e.tensor_copy(X64[32:64, 0:NT, 0:32], Yc[32:64, 0:NT, :])
                done(e.tensor_copy(X64[64:96, NT:U, 32:64], Yc[64:96, NT:U, :]), "Y5")
                e.transpose(XT[0:32, 0:NT, 32:64], Yc[32:64, 0:NT, :])
                e.transpose(XT[64:96, 0:NT, 96:128], Yc[96:128, 0:NT, :])
                e.transpose(XT[32:64, NT:U, 0:32], Yc[0:32, NT:U, :])
                done(e.transpose(XT[96:128, NT:U, 64:96], Yc[64:96, NT:U, :]), "XT64")
                wait(pe_dn, "P6")
                done(e.tensor_copy(P6c[0:64, NT:U, :], ps[0:64, 6, 0:NT * 64].rearrange("p (u c) -> p u c", u=NT)), "P6")
                wait(pe_dn, "Y6")
                done(e.tensor_copy(XT[64:128, NT:U, 0:64], ps[64:128, 3, 0:NT * 64].rearrange("p (u c) -> p u c", u=NT)), "Y6")
                for s in range(NT):
                    tile = ((CT, CT), (0, 3), (1, 2), (2, 1), (3, 0))[s]
                    if s:
                        for d in range(2):
                            u = d * NT + tile[d]
                            wait(pe_dn, f"ks {s} {'fb'[d]}")
                            wait(dve_dn, "kv ctx")
                            done(e.scalar_tensor_tensor(rr[:, d, :], ps[:, 2 + d, 0:P], prm[:, NEG_EG, u:u + 1], vrow[:, tile[d], :], ALU.mult, ALU.add), f"r {s} {'fb'[d]}")
                    for d in range(2):
                        u = d * NT + tile[d]
                        if 0 < s < NT - 1:
                            wait(pe_dn, f"av {s} {'fb'[d]}")
                            if s > 1:
                                wait(dve_dn, f"S {s - 1} {'fb'[d]}")
                            else:
                                e.wait_ge(ld_S, 32 * (h + 1))
                            done(e.scalar_tensor_tensor(S[:, d, :], S[:, d, :], prm[:, GL, u:u + 1], ps[:, (5, 7)[d], P:2 * P], ALU.mult, ALU.add), f"S {s} {'fb'[d]}")
                    for d in range(2):
                        wait(pe_dn, f"av {s} {'fb'[d]}")
                        if s:
                            wait(act_dn, f"qs {s} {'fb'[d]}")
                            m = e.tensor_tensor(ob[:, d, tile[d], :], ps[:, (5, 7)[d], 0:P], tq[:, d, :], ALU.add)
                        else:
                            m = e.tensor_copy(ob[:, d, CT, :], ps[:, (5, 7)[d], 0:P])
                        done(m, f"o {s} {'fb'[d]}")
                wait(dve_dn, f"o {NT - 1} b")
                wait(pe_dn, "turn o", h - 1)
                done(e.tensor_tensor(osum[:, :, :], ob[:, 0, :, :], ob[:, 1, :, :], ALU.add), "o sum")
                wait(dve_dn, "o sum")
                done(e.tensor_tensor(osc[:, :, :], osum[:, :, :], rn[:, 1, :].unsqueeze(2).to_broadcast([P, NT, P]), ALU.mult), "o scaled")
                wait(act_dn, "o norm")
                done(e.reciprocal(orn[:, :], orm[:, :]), "1/o norm")
                wait(dve_dn, "1/o norm")
                done(e.tensor_tensor(osum[:, :, :], osc[:, :, :], orn[:, :].unsqueeze(2).to_broadcast([P, NT, P]), ALU.mult), "o normed")
                wait(pe_dn, "turn o")
                wait(act_dn, "silu z")
                oh = oT[:, ds(h, 1), :].rearrange("p o c -> p (o c)")
                e.scalar_tensor_tensor(oT[:, ds(h, 1), 0:LAT].rearrange("p o c -> p (o c)"), ps[:, 2, :], cols[:, DNG:DNG + 1], zs[:, 0:LAT], ALU.mult, ALU.mult)
                done(e.scalar_tensor_tensor(oT[:, ds(h, 1), LAT:TOK].rearrange("p o c -> p (o c)"), ps[:, 3, 0:CTX], cols[:, DNG:DNG + 1], zs[:, LAT:TOK], ALU.mult, ALU.mult), "o out")

            with e.Fori(0, H - 1) as h:
                head(h, True)
            head(H - 1, False)

            for j in range(2):
                for t in range(NT):
                    n = j * NT + t
                    e.wait_ge(nsq_done, n + 1)
                    e.tensor_reduce(nss[:, j, t, :], nsq[:, n % 2, :].rearrange("p (h d) -> p h d", d=NA_D), AX.X, ALU.add).then_inc(nss_done, 1)
                e.wait_ge(nrms_done, j + 1)
                e.reciprocal(nrn[:, j, :, :], nrms[:, j, :, :]).then_inc(nrn_done, 1)
                e.wait_ge(nrn_done, j + 1)
                for t in range(NT):
                    row = qkv[:, j, t, :].rearrange("p (h d) -> p h d", d=NA_D)
                    m = e.tensor_tensor(row, row, nrn[:, j, t, :].unsqueeze(2).to_broadcast([P, NA_H, NA_D]), ALU.mult)
                m.then_inc(nrow_done, 1)
            e.wait_ge(ld_nc, 80)
            e.tensor_scalar(ngain[:, 0, :], ngain[:, 0, :], float(NA_D) ** -0.5, None, ALU.mult).then_inc(ngain_done, 1)
            e.wait_ge(ngain_done, 1)
            e.wait_ge(nrow_done, 2)
            e.sem_inc(dve_na.sem, dve_na.n)
            e.sem_inc(st_k, 16)

            def pair(p):
                def wait(steps, name, turn=p):
                    e.wait_ge(steps.sem, steps.value(turn, name))

                wait(pe_na, "turn", p - 1)
                for j, rows_ in enumerate((qrow, krow_n)):
                    if j:
                        e.wait_ge(st_k, p * 16 + 16)
                        e.tensor_copy(krow_n[:, NT, :], ck[:, ds(p * P, P)])
                    g = ngain[:, j, :].unsqueeze(1).to_broadcast([P, 2 * NT, NA_D])
                    src = qkv[:, j, :, ds(p * P, P)].rearrange("p t (h d) -> p t h d", d=NA_D)
                    dst = rows_[:, 0:NT, :].rearrange("p t (h d) -> p t h d", d=NA_D)
                    g = ngain[:, j, :].unsqueeze(1).unsqueeze(1).to_broadcast([P, NT, 2, NA_D])
                    dve_na.done(e.tensor_tensor(dst, src, g, ALU.mult), ("q rows", "k rows")[j])
                wait(pe_na, "turn")
                dve_na.done(e.tensor_copy(cT[:, :, :], ps[:, 5, 0:3 * P].rearrange("p (t c) -> p t c", t=3)), "T ctx")
                for i in range(NU + 1):
                    if i < NU:
                        hh, c = UNITS[i]
                        _, _, (lo, hi) = key_tiles(c)
                        wait_apart(e, ngain_done, (pe_na.sem, pe_na.value(p, f"score {i}")), (pool_na.sem, pool_na.value(p, f"bias {hh}")))
                        add = bm[:, hh, c if c < CT else 0, lo:hi]
                        m = e.tensor_tensor_reduce(Sx[:, i % 2, lo:hi], ps[:, i % 2, lo:hi], add, 1.0, -3.0e38, ALU.add, ALU.max, mx[:, i:i + 1])
                        dve_na.done(m, f"max {i}")
                        wait(dve_na, f"max {i}")
                        dve_na.done(e.tensor_scalar(nmx[:, i:i + 1], mx[:, i:i + 1], -1.0, None, ALU.mult), f"-max {i}")
                    if i:
                        _, _, (lo, hi) = key_tiles(UNITS[i - 1][1])
                        wait(act_na, f"exp {i - 1}")
                        dve_na.done(e.reciprocal(rs[:, i - 1:i], sm[:, i - 1:i]), f"1/sum {i - 1}")
                        wait(dve_na, f"1/sum {i - 1}")
                        row = Sx[:, (i - 1) % 2, lo:hi]
                        dve_na.done(e.tensor_scalar(row, row, rs[:, i - 1:i], None, ALU.mult), f"P {i - 1}")

            with e.Fori(0, KP) as p:
                pair(p)

            e.tensor_tensor(mods[:, 16:48, :], mods[:, 16:48, :], cols[:, B_ADA + 16:B_ADA + 48].unsqueeze(2).to_broadcast([P, 32, 2]), ALU.add).then_inc(mods_done, 1)
            e.wait_ge(mods_done, 1)
            e.scalar_tensor_tensor(gain2[:, :, :], mods[:, 32:40, :], 1.0, cols[:, N2:N2 + 8].unsqueeze(2).to_broadcast([P, KD, 2]), ALU.add, ALU.mult).then_inc(mods_done, 1)
            e.wait_ge(mods_done, 2)
            e.wait_ge(act_na.sem, act_na.value(KP - 1, "out"))
            e.sem_inc(dve_mg.sem, dve_mg.n)
            with e.Fori(0, KD // 2) as f:
                for i in range(2):
                    e.wait_ge(act_mg.sem, act_mg.value(f, f"g{i}"))
                    e.wait_ge(dve_mg.sem, dve_mg.value(f - 1, f"y{i}"))
                    for g, mixer in enumerate("AB"):
                        e.wait_ge(pe_mg.sem, pe_mg.value(f, f"p{mixer}{i}"))
                        for b, (a, n) in enumerate(SEG):
                            m = e.tensor_tensor(prod[:, i, g, a:a + n], sgm[:, i, g, a:a + n], ps[:, 4 * i + 2 * g + b, 0:n], ALU.mult)
                        dve_mg.done(m, f"y{mixer}{i}")
                    e.wait_ge(dve_mg.sem, dve_mg.value(f, f"yB{i}"))
                    y = yT[:, ds(2 * f + i, 1), :].rearrange("p o c -> p (o c)")
                    dve_mg.done(e.tensor_tensor(y, prod[:, i, 0, :], prod[:, i, 1, :], ALU.add), f"y{i}")

            e.sem_inc(dve_wo.sem, 4)
            with e.Fori(0, 2) as j:
                for i in range(4):
                    e.wait_ge(pe_wo.sem, pe_wo.value(j, f"o{i}"))
                    for b, (a, n) in enumerate(SEG):
                        x = xT[:, ds(j * 4 + i, 1), a:a + n].rearrange("p o c -> p (o c)")
                        gate = mods[:, ds(j * 4 + i + 16, 1), b]
                        m = e.scalar_tensor_tensor(x, ps[:, 2 * i + b, 0:n], gate, x, ALU.mult, ALU.add)
                    dve_wo.done(m, f"x{i}")
            e.wait_ge(rms2_done, 1)
            e.reciprocal(rn2[:, :], ss2[:, :]).then_inc(dg2_done, 1)
            e.wait_ge(dg2_done, 1)
            e.tensor_tensor(dg2[:, :, :], IDN.unsqueeze(1).to_broadcast([P, NT, P]), rn2[:, :].unsqueeze(2).to_broadcast([P, NT, P]), ALU.mult).then_inc(dg2_done, 1)
            e.wait_ge(rstd2_mm, 1)
            e.wait_ge(dve_wo.sem, dve_wo.value(1, "x3"))
            for k in range(KD):
                e.tensor_tensor(hT[:, k, 0:LAT], xT[:, k, 0:LAT], ps[:, 6, :], ALU.mult)
                e.tensor_tensor(hT[:, k, LAT:TOK], xT[:, k, LAT:TOK], ps[:, 7, 0:CTX], ALU.mult).then_inc(xn2_done, 1)

            e.sem_inc(dve_f1.sem, 2)
            with e.Fori(0, KF // 2) as f:
                for i in range(2):
                    e.wait_ge(act_f1.sem, act_f1.value(f, f"a{i}"))
                    e.wait_ge(pe_f1.sem, pe_f1.value(f, f"b{i}"))
                    for b, (a, n) in enumerate(SEG):
                        hid = act[:, ds(2 * f + i, 1), a:a + n].rearrange("p o c -> p (o c)")
                        m = e.tensor_tensor(hid, sg[:, i, a:a + n], ps[:, 4 * i + 2 + b, 0:n], ALU.mult)
                    dve_f1.done(m, f"h{i}")
            e.sem_inc(dve_f2.sem, 2)
            with e.Fori(0, KD // 2) as n:
                for i in range(2):
                    e.wait_ge(pe_f2.sem, pe_f2.value(n, f"m{i}"))
                    e.wait_ge(pe_f2.sem, pe_f2.value(n - 1, f"turn {i}"))
                    for b, (a, w) in enumerate(SEG):
                        x = xT[:, ds(2 * n + i, 1), a:a + w].rearrange("p o c -> p (o c)")
                        gate = mods[:, ds(2 * n + i + 40, 1), b]
                        m = e.scalar_tensor_tensor(xo[:, i, a:a + w], ps[:, 2 * i + b, 0:w], gate, x, ALU.mult, ALU.add)
                    dve_f2.done(m, f"x{i}")

        @block.gpsimd
        def _(e):
            e.wait_ge(prm_done, 2)
            e.wait_ge(zero_done, 3)
            e.sem_inc(strip["z"], 1)
            e.sem_inc(st_S, 32)
            e.sem_inc(pool_dn.sem, pool_dn.n)

            def head(h, more):
                def wait(steps, name, turn=h):
                    e.wait_ge(steps.sem, steps.value(turn, name))

                def per_unit(kind):
                    return prm[:, kind, :].rearrange("p (d t) -> p d t", d=2).unsqueeze(3).to_broadcast([P, 2, NT, P])

                wait(dve_dn, "prm")
                wait(pe_dn, f"av {NT - 1} b", h - 1)
                tri = sq_c[:, LE:GE + 1, :].unsqueeze(2).to_broadcast([P, 2, NT, P])
                pool_dn.done(e.tensor_tensor(typed(gm[:, :, :]), tri, per_unit(G), ALU.mult), "g mask")
                wait(act_dn, "decay")
                pool_dn.done(e.tensor_tensor(typed(dtm[:, :, :]), typed(dt[:, :, :]), tri, ALU.mult), "decay")
                wait(act_dn, "k rows")
                wait(dve_dn, "kv ctx")
                wait(pe_dn, "turn o", h - 1)
                pool_dn.done(e.tensor_tensor(typed(kd[:, :, :]), krow[:, :, :].unsqueeze(1).to_broadcast([P, 2, NT, P]), per_unit(EK), ALU.mult), "kd")
                wait(act_dn, "kq")
                wait(pool_dn, "decay")
                pool_dn.done(e.tensor_tensor(typed(AT[:, :, :]), kqs[:, :, 1, :].unsqueeze(1).to_broadcast([P, 2, NT, P]), typed(dtm[:, :, :]), ALU.mult), "A")

            with e.Fori(0, H - 1) as h:
                head(h, True)
            head(H - 1, False)

            e.wait_ge(dve_dn.sem, dve_dn.value(H - 1, "o out"))
            e.wait_ge(act_dn.sem, act_dn.value(H - 1, "ada"))
            e.wait_ge(pe_dn.sem, pe_dn.value(H - 1, "turn o"))
            e.memset(zrow[:, :], 0.0).then_inc(zrow_done, 1)
            e.memset(bm[:, :, :, :], 0.0).then_inc(zrow_done, 1)
            e.wait_ge(zrow_done, 2)
            e.wait_ge(ld_nc, 80)
            e.sem_inc(pool_na.sem, 2)

            def pair(p):
                for hh in range(2):
                    e.wait_ge(ld_bias[hh], p * (16 * ROWS) + 16 * ROWS)
                    e.wait_ge(dve_na.sem, dve_na.value(p - 1, f"max {NU // 2 * (hh + 1) - 1}"))
                    for c in range(CT):
                        tiles, at, _ = key_tiles(c)
                        rel = tiles[0] - c + 1
                        n = len(tiles)
                        b = bias[:, hh, :, :].rearrange("p r (t x) -> p t r x", t=3)
                        w = win[:, c, :].rearrange("p (t x) -> p t x", t=3)
                        for j in range(n):
                            dst = bm[:, hh, c, at + j * P:at + (j + 1) * P].rearrange("p (r x) -> p r x", r=ROWS)
                            m = e.tensor_tensor(dst, b[:, rel + j, :, :], w[:, rel + j, :].unsqueeze(1).to_broadcast([P, ROWS, KC]), ALU.add)
                    pool_na.done(m, f"bias {hh}")

            with e.Fori(0, KP) as p:
                pair(p)


_INS = ["x_prompt", "x_sample", "c", "cache_na_k", "cache_na_v", "state_dn", "c_ctx", "w_ada", "b_ada", "norm1_g", "w_in",
        "dn_conv", "dn_a_log", "dn_dt_bias", "dn_norm_g", "w_pa", "na_qnorm_g", "na_knorm_g", "na_rpb", "w_pb", "w_out",
        "norm2_g", "ffn_w1", "ffn_w3", "ffn_w2"]
_OUTS = [("y_prompt", (1, CTX, D)), ("y_sample", (1, LAT, D)), ("new_k", (1, 1, CTX, NA_H, NA_D)),
         ("new_v", (1, 1, CTX, NA_H, NA_D)), ("new_state", (1, 1, 2, H, DK, DK))]


def kernel(**inputs):
    import concourse.bacc as bacc
    from concourse.bass_utils import run_bass_kernel_spmd

    nc = bacc.Bacc("TRN2", target_bir_lowering=False, num_devices=1)
    arrays = {name: np.ascontiguousarray(inputs[name]) for name in _INS}
    arrays.update(zip(("squares", "levels", "window"), shape_constants()))
    A = {n: nc.dram_tensor("in_" + n, a.shape, mybir.dt.from_np(a.dtype), kind="ExternalInput").ap() for n, a in arrays.items()}
    for name, shape in _OUTS:
        A[name] = nc.dram_tensor("out_" + name, shape, F32, kind="ExternalOutput").ap()
    build(nc, A)
    r = run_bass_kernel_spmd(nc, [{"in_" + n: a for n, a in arrays.items()}], core_ids=[0])
    return tuple(r.results[0]["out_" + name] for name, _ in _OUTS)
```

```python
from contextlib import ExitStack

import numpy as np

import concourse.bass as bass
from concourse import mybir

F32 = mybir.dt.float32
F32R = mybir.dt.float32r
ACT = mybir.ActivationFunctionType
ALU = mybir.AluOpType
AX = mybir.AxisListType
ds = bass.ds

P = 128
D = 1024
KD = D // P
CTX, LAT = 128, 512
TOK = LAT + CTX
NT = TOK // P
CT = LAT // P
EPS = 1e-6
H, DK = 8, 128
U = 2 * NT
OFF_Z = 3 * D
OFF_BETA = OFF_Z + D
OFF_NA = OFF_BETA + 4 * H
NA_H, NA_D = 8, 64
NA_W = NA_H * NA_D
OFF_GATE = OFF_NA + 3 * NA_W
FFN = 2816
KF = FFN // P
KH = KF // 2
NU2 = KH + KD // 2
KP = NA_W // P
GRID_W, ROWS = 64, 8
KR, KC = 8, 16
RPB = (2 * KR - 1) * (2 * KC - 1)
NEG = -1e30
G, EG, NEG_EG, EK, GL, BETA = range(6)
NPRM = 6
LEVELS = (1, 2, 4, 8, 16)
LE, GE, GT, LT, ID, ONE = range(6)


def shape_constants():
    k, i = np.arange(P)[:, None], np.arange(P)[None]
    squares = np.stack([k <= i, k >= i, k > i, k < i, k == i, k + i >= 0], 1).astype(np.float32)
    row, col = np.arange(P)[:, None] % 32, np.arange(32)[None]
    level = []
    for b in LEVELS:
        pair = row // (2 * b) == col // (2 * b)
        lower = pair & (row // b % 2 == 1) & (col // b % 2 == 0)
        upper = pair & (row // b % 2 == 0) & (col // b % 2 == 1)
        level += [lower, upper]
    level.append(row == col)
    levels = np.stack(level, 1).astype(np.float32)
    window = np.zeros((P, GRID_W // KC, 3 * KC), np.float32)
    for cb in range(GRID_W // KC):
        q = cb * KC + np.arange(P)[:, None] % KC
        key = (cb - 1) * KC + np.arange(3 * KC)[None]
        first = np.clip(q - KC // 2, 0, GRID_W - KC)
        window[:, cb] = np.where((key >= first) & (key < first + KC), 0.0, NEG)
    return squares.reshape(P, -1), levels.reshape(P, -1), window.reshape(P, -1)


class Steps:

    def __init__(self, sem, names):
        self.sem, self.names, self.at = sem, names, {n: i + 1 for i, n in enumerate(names)}
        assert len(self.at) == len(names), names
        self.n, self.next = len(names), 0

    def done(self, ins, name):
        assert self.names[self.next % self.n] == name, (self.names[self.next % self.n], name)
        self.next += 1
        ins.then_inc(self.sem, 1)

    def value(self, turn, name):
        return (turn + 1) * self.n + self.at[name]


def wait_apart(e, passed, *waits):
    values = [value if isinstance(value, int) else e.to_reg(value) for _, value in waits]
    e.wait_ge(passed, 1)
    for (sem, _), value in zip(waits, values):
        e.wait_ge(sem, value)


def pe_steps():
    names = ["dt", "norm", "kq", "turn k v", "P0"]
    for n in (1, 2, 3, 4, 5):
        names += [f"P{n}", f"Y{n}"]
    names += ["P6", "Y6"]
    for s in range(NT):
        if s:
            names += [f"ks {s} {d}" for d in "fb"]
        names += [f"y {s} {d}" for d in "fb"]
        names += [f"av {s} {d}" for d in "fb"]
    return names + ["ada rows", "ada", "turn o"]


def act_steps():
    names = ["decay", "silu q", "silu k", "silu v", "square", "norm", "kq", "k rows", "L diag", "L pairs", "P5", "Y5", "P6", "Y6"]
    for s in range(NT):
        if s:
            names += [f"qs {s} {d}" for d in "fb"]
        names += [f"v {s} {d}" for d in "fb"]
        names += [f"state {d}" for d in "fb"] if not s else []
    return names + ["silu z", "ada rows", "o square", "o norm", "ada"]


NE, NE_LAST = 3, 7
assert (NE * (H - 1) + NE_LAST) * P == 3 * NA_W + 2 * D


def dve_steps():
    names = ["prm", "taps", "conv q", "conv k", "conv v", "1/norm", "beta", "-beta", "v rows", "kv ctx", "L", "L diag"]
    names += ["P0", "X0", "XT0"]
    for n in (1, 2, 3, 4):
        names += [f"P{n}", f"X{n}", f"XT{n}"]
    names += ["X64", "XT diag", "Y5", "XT64", "P6", "Y6"]
    for s in range(NT):
        if s:
            names += [f"r {s} {d}" for d in "fb"]
        names += [f"S {s} {d}" for d in "fb"] if 0 < s < NT - 1 else []
        names += [f"o {s} {d}" for d in "fb"]
    return names + ["o sum", "o scaled", "1/o norm", "o normed", "o out"]


UNITS = [(hh, c) for hh in range(2) for c in range(NT)]
NU = len(UNITS)


def key_tiles(c):
    if c == CT:
        return [], 3 * P, (3 * P, 4 * P)
    first, last = max(c - 1, 0), min(c + 1, CT - 1)
    at = P if last - first == 1 else 0
    return list(range(first, last + 1)), at, (at, 4 * P)


def pe_na_steps():
    names = ["turn", "score 0", "score 1"]
    for i in range(NU):
        names += [f"turn P {i}"] + ([f"score {i + 2}"] if i + 2 < NU else []) + [f"PV {i}"]
    return names


def act_na_steps():
    names = ["v rows", "T lat"]
    for i in range(NU + 1):
        names += ([f"exp {i}"] if i < NU else []) + ([f"PT {i - 1}"] if i else [])
    return names + ["out"]


def dve_na_steps():
    names = ["q rows", "k rows", "T ctx"]
    for i in range(NU + 1):
        names += ([f"max {i}", f"-max {i}"] if i < NU else []) + ([f"1/sum {i - 1}", f"P {i - 1}"] if i else [])
    return names


POOL_STEPS = ["g mask", "decay", "kd", "A"]


def build(nc, A):
    top = ExitStack()
    with top:
        def sb(name, shape, stack=top, dtype=F32):
            return stack.enter_context(nc.sbuf_tensor(name, shape, dtype))

        def sem(name):
            return top.enter_context(nc.semaphore(name))

        sq_c = sb("sq_c", [P, 6, P])
        lv_c = sb("lv_c", [P, 2 * len(LEVELS) + 1, 32])
        cols = sb("cols", [P, 160])
        mods = sb("mods", [P, 48, 2])
        gain1 = sb("gain1", [P, KD, 2])
        gain2 = sb("gain2", [P, KD, 2])
        epsc = sb("epsc", [P, 2])
        csT = sb("csT", [P, 2, KD])
        xT = sb("xT", [P, KD, TOK])
        oT = sb("oT", [P, H, TOK])
        naT = sb("naT", [P, KP, TOK])
        W = sb("W", [P, 4, KD, P])
        ps = top.enter_context(nc.psum_tensor("ps", [P, 8, 512], F32))

        mid = top.enter_context(ExitStack())
        hT = sb("hT", [P, KD, TOK], mid)
        WE = naT[:, 2:4, :].rearrange("p a c -> p (a c)")[:, 0:D].rearrange("p (k c) -> p k c", k=KD)
        stage = naT[:, 0, :]

        IDN = sq_c[:, ID, :]
        ONES = sq_c[:, ONE, :]
        B_ADA, N1, N2, DNG, CONV = 0, 48, 56, 64, 65

        w_in = A["w_in"][0].rearrange("(k p) n -> p k n", p=P)
        w_ada = A["w_ada"][0].rearrange("(k p) n -> p k n", p=P)

        ld_const = sem("ld_const")
        ld_vec = sem("ld_vec")
        ld_x = [sem(f"ld_x{t}") for t in range(NT)]
        ld_wa = [sem(f"ld_wa{s}") for s in range(4)]
        vec_turned = sem("vec_turned")
        vec_out = sem("vec_out")
        cond_silu = sem("cond_silu")
        x_turned = sem("x_turned")
        x_out = sem("x_out")
        sq_done = sem("sq_done")
        ss_done = sem("ss_done")
        rms_done = sem("rms_done")
        rstd_done = sem("rstd_done")
        xn_done = sem("xn_done")
        h_done = sem("h_done")
        ada_mm = sem("ada_mm")
        ada_row = sem("ada_row")
        ada_out = sem("ada_out")
        gain_done = sem("gain_done")
        ld_ba = sem("ld_ba")
        ba_mm = sem("ba_mm")
        ba_T = sem("ba_T")
        ba_turned = sem("ba_turned")
        ba_act = sem("ba_act")
        ba_dve = sem("ba_dve")
        cum_mm = sem("cum_mm")
        prm_done = sem("prm_done")
        zero_done = sem("zero_done")

        ld_w = {k: sem(f"ld_w_{k}") for k in "qkvz"}
        strip = {k: sem(f"strip_{k}") for k in "qkvz"}
        raw = {k: sem(f"raw_{k}") for k in "qkv"}
        conv_part = sem("conv_part")
        bk_part = sem("bk_part")
        ld_e = sem("ld_e")
        strip_e = sem("strip_e")
        e_out = sem("e_out")
        st_e = sem("st_e")
        ext_dram = nc.dram_tensor("ext_dram", (NE * (H - 1) + NE_LAST, P, TOK), F32)
        ld_S = sem("ld_S")
        st_S = sem("st_S")
        slot = {"q": 0, "k": 1, "v": 2, "z": 3}

        pe_dn = Steps(sem("pe_dn"), pe_steps())
        act_dn = Steps(sem("act_dn"), act_steps())
        dve_dn = Steps(sem("dve_dn"), dve_steps())
        pool_dn = Steps(sem("pool_dn"), POOL_STEPS)

        ld_fq = [sem(f"ld_fq{j}") for j in range(3)]
        ld_nc = sem("ld_nc")
        rpb_pad = sem("rpb_pad")
        rpb_rows = sem("rpb_rows")
        ld_bias = [sem(f"ld_bias{hh}") for hh in range(2)]
        zrow_done = sem("zrow_done")
        proj_mm = sem("proj_mm")
        proj_out = sem("proj_out")
        nsq_done = sem("nsq_done")
        nss_done = sem("nss_done")
        nrms_done = sem("nrms_done")
        nrn_done = sem("nrn_done")
        nrow_done = sem("nrow_done")
        ngain_done = sem("ngain_done")
        st_k = sem("st_k")
        st_v = sem("st_v")
        pe_na = Steps(sem("pe_na"), pe_na_steps())
        act_na = Steps(sem("act_na"), act_na_steps())
        dve_na = Steps(sem("dve_na"), dve_na_steps())
        pool_na = Steps(sem("pool_na"), ["bias 0", "bias 1"])

        ld_pa = [sem(f"ld_pa{i}") for i in range(2)]
        pa_mm = sem("pa_mm")
        pa_out = sem("pa_out")
        ld_m = [sem(f"ld_m{i}") for i in range(2)]
        ld_g = [sem(f"ld_g{i}") for i in range(2)]
        mods_done = sem("mods_done")
        pe_mg = Steps(sem("pe_mg"), ["pB0", "pB1"])
        act_mg = Steps(sem("act_mg"), ["g0", "g1"])
        dve_mg = Steps(sem("dve_mg"), ["yA0", "yB0", "y0", "yA1", "yB1", "y1"])
        ld_o = [sem(f"ld_o{i}") for i in range(4)]
        wo_mm = sem("wo_mm")
        wo_x = sem("wo_x")
        sq2_done = sem("sq2_done")
        ss2_mm = sem("ss2_mm")
        rms2_done = sem("rms2_done")
        rstd2_done = sem("rstd2_done")
        xn2_done = sem("xn2_done")
        h2_done = sem("h2_done")
        h_hi = sem("h_hi")
        h_lo = sem("h_lo")
        ld_u = [sem(f"ld_u{s}") for s in range(2)]
        w_hi = [sem(f"w_hi{s}") for s in range(2)]
        w_lo = [sem(f"w_lo{s}") for s in range(2)]
        w_used = [sem(f"w_used{s}") for s in range(2)]
        silu_done = sem("silu_done")
        hid_done = sem("hid_done")
        a_hi = sem("a_hi")
        a_lo = sem("a_lo")
        x_done = [sem(f"x_done{s}") for s in range(2)]
        y_turned = [sem(f"y_turned{s}") for s in range(2)]
        y_done = [sem(f"y_done{s}") for s in range(2)]
        st_y = [sem(f"st_y{s}") for s in range(2)]

        rpb_dram = nc.dram_tensor("rpb_dram", (1, NA_H * RPB + 64), F32)
        rpb_rows_dram = nc.dram_tensor("rpb_rows_dram", (KC, NA_H * (2 * KR - 1) * 3 * KC), F32)

        work = mid.enter_context(ExitStack())
        params = sb("params", [P, H, NPRM, U], work)
        WA = sb("WA", [P, 4, KD, P], work)
        start = work.enter_context(ExitStack())
        xin = sb("xin", [P, NT, D], start)
        rows = sb("rows", [P, 2, P], start)
        sqx = sb("sqx", [P, 2, TOK], start)
        rstd = sb("rstd", [P, TOK], start)
        rms = sb("rms", [P, TOK], start)
        wba = sb("wba", [P, KD, 4 * H], start)
        ba = sb("ba", [P, NT, 4 * H], start)
        alog = sb("alog", [P, 2 * H], start)
        dtb = sb("dtb", [P, 2 * H], start)
        sp = sb("sp", [P, 4, NT, 2 * H], start)
        baT = sb("baT", [4 * H, TOK], start)
        arow0 = sb("arow0", [2, 16 * P], start)
        start.close()
        dn = work.enter_context(ExitStack())
        kq = sb("kq", [P, NT, 2, P], dn)
        zs = sb("zs", [P, TOK], dn)
        sqkq = sb("sqkq", [P, NT, 2, P], dn)
        krow = sb("krow", [P, NT, P], dn)
        vrow = sb("vrow", [P, NT, P], dn)
        kd = sb("kd", [P, U, P], dn)
        gm = sb("gm", [P, U, P], dn)
        dt = sb("dt", [P, U, P], dn)
        LNT = sb("LNT", [P, U, P], dn)
        Sc = sb("Sc", [P, 2, P], dn)
        rr = sb("rr", [P, 2, P], dn)
        vn = sb("vn", [P, 2, P], dn)
        tq = sb("tq", [P, 2, P], dn)
        ob = sb("ob", [P, 2, NT, P], dn)
        prm = sb("prm", [P, NPRM, U], dn)
        arow = sb("arow", [2, 4 * P], dn)
        taps = sb("taps", [P, 3, 3], dn)
        raws = sb("raws", [P, 3, TOK + 4], dn)
        conv = sb("conv", [P, 3, TOK + 4], dn)
        nrm = sb("nrm", [P, 2, NT], dn)
        rn = sb("rn", [P, 2, NT], dn)
        bk = sb("bk", [P, 2, U], dn)
        dtm = dt
        kqs = sqkq
        AT = gm
        LNTd = sb("LNTd", [P, U, P], dn)
        LNTp = sb("LNTp", [P, U, P], dn)
        Xc = sb("Xc", [P, U, 32], dn)
        Pc = sb("Pc", [P, U, 32], dn)
        Yc = sb("Yc", [P, U, 32], dn)
        XTd = sb("XTd", [P, U, P], dn)
        X64 = sb("X64", [P, U, 64], dn)
        P6c = sb("P6c", [P, U, 64], dn)
        XT = sb("XT", [P, U, P], dn)
        S = sb("S", [P, 2, P], dn)
        osum = sb("osum", [P, NT, P], dn)
        osq, osc = ob[:, 0, :, :], ob[:, 1, :, :]
        oss = sb("oss", [P, NT], dn)
        orm = sb("orm", [P, NT], dn)
        orn = sb("orn", [P, NT], dn)
        dn.close()
        na = work.enter_context(ExitStack())
        fq = WA[:, :, :, :].rearrange("p s k c -> p (s k c)")[:, 0:KP * TOK].rearrange("p (s c) -> p s c", s=KP)
        fk = W[:, :, :, :].rearrange("p s k c -> p (s k c)")[:, 0:KP * TOK].rearrange("p (s c) -> p s c", s=KP)
        fv = sb("fv", [P, KP, TOK], na)
        qkv = sb("qkv", [P, 3, NT, NA_W], na)
        nsq = sb("nsq", [P, 2, NA_W], na)
        nss = sb("nss", [P, 2, NT, NA_H], na)
        nrms = sb("nrms", [P, 2, NT, NA_H], na)
        nrn = sb("nrn", [P, 2, NT, NA_H], na)
        ngain = sb("ngain", [P, 2, NA_D], na)
        ck = sb("ck", [P, NA_W], na)
        cv = sb("cv", [P, NA_W], na)
        win = sb("win", [P, CT, 3 * KC], na)
        bias = sb("bias", [P, 2, ROWS, 3 * KC], na)
        bm = sb("bm", [P, 2, CT, 4 * P], na)
        qrow = sb("qrow", [P, NT, P], na)
        krow_n = sb("krow_n", [P, NT + 1, P], na)
        vrow_n = sb("vrow_n", [P, NT + 1, P], na)
        qT = sb("qT", [P, CT, P], na)
        kT = sb("kT", [P, CT, P], na)
        cT = sb("cT", [P, 3, P], na)
        Sx = sb("Sx", [P, 2, 4 * P], na)
        PT = sb("PT", [P, 2, 4 * P], na)
        mx = sb("mx", [P, NU], na)
        nmx = sb("nmx", [P, NU], na)
        sm = sb("sm", [P, NU], na)
        rs = sb("rs", [P, NU], na)
        zrow = sb("zrow", [1, 32], na)
        na.close()
        work.close()
        mid.close()
        late = top.enter_context(ExitStack())
        merging = late.enter_context(ExitStack())
        sb("under_hT", [P, KD, TOK], merging)
        yT = sb("yT", [P, KD, TOK], merging)
        gates = sb("gates", [P, 2, 2, TOK], merging)
        sgm = sb("sgm", [P, 2, 2, TOK], merging)
        prod = sb("prod", [P, 2, 2, TOK], merging)
        merging.close()
        h_part = [sb(f"h_part{i}", [P, KD, TOK], late, F32R) for i in range(2)]
        a_part = [sb(f"a_part{i}", [P, KH, TOK], late, F32R) for i in range(2)]
        w_part = [sb(f"w_part{i}", [P, 2, KH, P], late, F32R) for i in range(2)]
        sq2 = sb("sq2", [P, 2, TOK], late)
        h2 = sq2
        rstd2 = sb("rstd2", [P, TOK], late)
        oTf = oT[:, :, :].rearrange("p a c -> p (a c)")
        naTf = naT[:, :, :].rearrange("p a c -> p (a c)")
        raw2 = oTf[:, 0:2 * KH * P].rearrange("p (s k c) -> p s k c", s=2, k=KH)
        xo = oTf[:, 2 * KH * P:2 * KH * P + 2 * TOK].rearrange("p (s c) -> p s c", s=2)
        rms2 = oTf[:, 2 * KH * P + 2 * TOK:2 * KH * P + 3 * TOK]
        yo = naTf[:, 0:2 * TOK].rearrange("p (s t c) -> p s t c", s=2, t=NT)
        sg = naTf[:, 2 * TOK:3 * TOK]
        hid = naTf[:, 3 * TOK:4 * TOK]
        late.close()

        block = top.enter_context(nc.Block())
        SEG = ((0, LAT), (LAT, CTX))
        HT = TOK // 2
        HALVES = ((0, HT), (HT, HT))
        PIECES = ((0, 0, HT, 0), (1, HT, LAT - HT, 0), (1, LAT, CTX, 1))

        def unit(q, kind, turn):
            return turn + (NU2 * q + (KH if kind == "down" else 0))

        def wide(w):
            return w[:, :, :, :].rearrange("p s k c -> p (s k c)").rearrange("p (k c) -> p k c", k=KD)

        def typed(t, lo=0, n=NT):
            return t.rearrange("p (d t) c -> p d t c", d=2)[:, :, lo:lo + n, :]

        @block.sync
        def _(e):
            e.dma_start(sq_c[:, :, :], A["squares"].rearrange("p (a b) -> p a b", a=6)).then_inc(ld_const, 16)
            e.dma_start(lv_c[:, :, :], A["levels"].rearrange("p (a b) -> p a b", b=32)).then_inc(ld_const, 16)
            e.dma_start(rows[0:48, 0, :], A["b_ada"][0].rearrange("(r c) -> r c", c=P)).then_inc(ld_vec, 16)
            e.dma_start(rows[48:56, 0, :], A["norm1_g"][0].rearrange("(r c) -> r c", c=P)).then_inc(ld_vec, 16)
            e.dma_start(rows[56:64, 0, :], A["norm2_g"][0].rearrange("(r c) -> r c", c=P)).then_inc(ld_vec, 16)
            e.dma_start(rows[64:65, 0, :], A["dn_norm_g"]).then_inc(ld_vec, 16)
            e.dma_start(rows[65:73, 0, :], A["c"][0].rearrange("(r c) -> r c", c=P)).then_inc(ld_vec, 16)
            e.dma_start(rows[73:81, 0, :], A["c_ctx"].rearrange("(r c) -> r c", c=P)).then_inc(ld_vec, 16)
            e.dma_start(rows[0:72, 1, :], A["dn_conv"][0].rearrange("t (r c) -> (t r) c", c=P)).then_inc(ld_vec, 16)
            for t in range(NT):
                src = A["x_sample"][0, t * P:(t + 1) * P, :] if t < CT else A["x_prompt"][0]
                e.dma_start(xin[:, t, :], src).then_inc(ld_x[t], 16)
            e.dma_start(alog[:, :], A["dn_a_log"].rearrange("o d h -> o (d h)").partition_broadcast(P)).then_inc(ld_ba, 16)
            e.dma_start(dtb[:, :], A["dn_dt_bias"].rearrange("o d h -> o (d h)").partition_broadcast(P)).then_inc(ld_ba, 16)
            e.dma_start(wba[:, :, :], w_in[:, :, OFF_BETA:OFF_BETA + 4 * H]).then_inc(ld_ba, 16)
            for s in range(4):
                e.dma_start(WA[:, s, :, :], w_ada[:, :, s * P:(s + 1) * P]).then_inc(ld_wa[s], 16)
            with e.Fori(1, 4) as i:
                for s in range(4):
                    if s % 2 == 0:
                        e.wait_ge(ada_mm, i * 2 + (s // 2 - 1))
                    e.dma_start(WA[:, s, :, :], w_ada[:, :, ds((i * 4 + s) * P, P)]).then_inc(ld_wa[s], 16)
            for kind in "qkv":
                off = "qkv".index(kind) * D
                e.dma_start(W[:, slot[kind], :, :], w_in[:, :, off:off + P]).then_inc(ld_w[kind], 16)

            def head(h, more):
                for d in range(2):
                    e.wait_ge(pe_dn.sem, pe_dn.value(h - 1, f"ks {NT - 1} b"))
                    e.wait_ge(dve_dn.sem, dve_dn.value(h - 1, f"S {NT - 2} b"))
                    e.dma_start(S[:, d, :], A["state_dn"][0, 0, d, ds(h, 1), :, :].rearrange("o k v -> k (o v)")).then_inc(ld_S, 16)
                e.wait_ge(strip["z"], h + 1)
                e.dma_start(W[:, slot["z"], :, :], w_in[:, :, ds(OFF_Z + h * P, P)]).then_inc(ld_w["z"], 16)
                if more:
                    for kind in "qkv":
                        off = "qkv".index(kind) * D
                        e.wait_ge(strip[kind], h + 1)
                        e.dma_start(W[:, slot[kind], :, :], w_in[:, :, ds(off + (h + 1) * P, P)]).then_inc(ld_w[kind], 16)
                for s in range(4):
                    e.wait_ge(pe_dn.sem, pe_dn.value(h - 1, "ada rows"))
                    e.dma_start(WA[:, s, :, :], w_ada[:, :, ds((16 + h * 4 + s) * P, P)]).then_inc(ld_wa[s], 16)
                def extra_in(j):
                    e.wait_ge(strip_e, h * NE + (j + 1))
                    e.dma_start(WE, w_in[:, :, ds(OFF_NA + (h * NE + j) * P, P)]).then_inc(ld_e, 16)

                def extra_store(j):
                    e.wait_ge(e_out, h * NE + (j + 2))
                    e.dma_start(ext_dram[ds(h * NE + j, 1), :, :].rearrange("o p c -> p (o c)"), stage).then_inc(st_e, 16)

                if not more:
                    e.wait_ge(st_e, 16 * 3 * KP + 16)
                    e.dma_start(fk, ext_dram[KP:2 * KP, :, :].rearrange("s p c -> p s c")).then_inc(ld_fq[1], 16)
                n = NE if more else NE_LAST
                extra_in(0)
                for j in range(1, n):
                    extra_in(j)
                    extra_store(j - 1)
                if not more:
                    e.wait_ge(pe_dn.sem, pe_dn.value(H - 1, "ada rows"))
                    e.dma_start(fq, ext_dram[0:KP, :, :].rearrange("s p c -> p s c")).then_inc(ld_fq[0], 16)
                for d in range(2):
                    e.wait_ge(act_dn.sem, act_dn.value(h, f"state {'fb'[d]}"))
                    e.dma_start(A["new_state"][0, 0, d, ds(h, 1), :, :].rearrange("o k v -> k (o v)"), Sc[:, d, :]).then_inc(st_S, 16)
                extra_store(n - 1)

            e.wait_ge(ada_mm, 9)
            with e.Fori(0, H - 1) as h:
                head(h, True)
            head(H - 1, False)
            e.wait_ge(st_e, 16 * (NE * (H - 1) + NE_LAST) + 16)
            e.wait_ge(st_S, 16 * 2 * H + 32)

            e.wait_ge(zrow_done, 1)
            e.dma_start(rpb_dram[0:1, 0:32], zrow[:, :]).then_inc(rpb_pad, 16)
            e.dma_start(rpb_dram[0:1, 32 + NA_H * RPB:], zrow[:, :]).then_inc(rpb_pad, 16)
            e.dma_start(rpb_dram[0:1, 32:32 + NA_H * RPB], A["na_rpb"][0].rearrange("h a b -> (h a b)").unsqueeze(0)).then_inc(rpb_pad, 16)
            e.wait_ge(rpb_pad, 48)
            shifted = rpb_dram[0:1, 31:32]
            shifted = bass.AP(shifted.tensor, shifted.offset, [[2 * KC - 1, NA_H * (2 * KR - 1)], [-1, KC], [1, 3 * KC]])
            e.dma_start(rpb_rows_dram[:, :].rearrange("c (r x) -> r c x", x=3 * KC), shifted).then_inc(rpb_rows, 16)
            e.wait_ge(dve_dn.sem, dve_dn.value(H - 1, "o out"))
            e.wait_ge(act_dn.sem, act_dn.value(H - 1, "ada"))
            e.wait_ge(pe_dn.sem, pe_dn.value(H - 1, "turn o"))
            e.wait_ge(pool_dn.sem, pool_dn.value(H - 1, "A"))
            e.dma_start(fv[:, :, :], ext_dram[2 * KP:3 * KP, :, :].rearrange("s p c -> p s c")).then_inc(ld_fq[2], 16)
            e.dma_start(ck[:, :], A["cache_na_k"][0, 0].rearrange("t h d -> t (h d)")).then_inc(ld_nc, 16)
            e.dma_start(cv[:, :], A["cache_na_v"][0, 0].rearrange("t h d -> t (h d)")).then_inc(ld_nc, 16)
            e.dma_start(win[:, :, :], A["window"].rearrange("p (c x) -> p c x", c=CT)).then_inc(ld_nc, 16)
            e.dma_start(ngain[:, 0, :], A["na_qnorm_g"].partition_broadcast(P).rearrange("p o d -> p (o d)")).then_inc(ld_nc, 16)
            e.dma_start(ngain[:, 1, :], A["na_knorm_g"].partition_broadcast(P).rearrange("p o d -> p (o d)")).then_inc(ld_nc, 16)
            e.wait_ge(rpb_rows, 16)

            def bias_in(p, hh):
                for r in range(ROWS):
                    src = rpb_rows_dram[:, ds(((2 * p + hh) * (2 * KR - 1) + KR - 1 - r) * 3 * KC, ROWS * 3 * KC)]
                    e.dma_start(bias[r * KC:(r + 1) * KC, hh, :, :], src.rearrange("c (r x) -> c r x", r=ROWS)).then_inc(ld_bias[hh], 16)

            for hh in range(2):
                bias_in(0, hh)
            e.wait_ge(proj_out, 3 * NT)
            e.dma_start(A["new_v"][0, 0].rearrange("t h d -> t (h d)"), qkv[:, 2, CT, :]).then_inc(st_v, 16)

            pa_w = A["w_pa"][0].rearrange("(k p) n -> p k n", p=P)
            pb_w = A["w_pb"][0].rearrange("(k p) n -> p k n", p=P)
            def pa_in(n, s):
                e.dma_start(W[:, s, :, :], pa_w[:, :, ds(n * P, P)]).then_inc(ld_pa[s], 16)

            def pb_in(n, s):
                e.dma_start(W[:, 2 + s, 0:KP, :], pb_w[:, :, ds(n * P, P)]).then_inc(ld_m[s], 16)

            e.wait_ge(proj_mm, 2 * NT)
            for s in range(2):
                pa_in(s, s)
                pb_in(s, s)

            def pair(p, more):
                following = e.snap(p + 1) if more else None
                e.wait_ge(dve_na.sem, dve_na.value(p, "k rows"))
                e.dma_start(A["new_k"][0, 0].rearrange("t h d -> t (h d)")[:, ds(p * P, P)], krow_n[:, CT, :]).then_inc(st_k, 16)
                if more:
                    for hh in range(2):
                        e.wait_ge(pool_na.sem, pool_na.value(p, f"bias {hh}"))
                        bias_in(following, hh)
                    for s in range(2):
                        wait_apart(e, zrow_done, (pa_mm, 2 * p + (s + 1)))
                        pa_in(2 * p + (2 + s), s)

            with e.Fori(0, KP - 1) as p:
                pair(p, True)
            pair(KP - 1, False)
            e.wait_ge(st_k, 16 * KP + 16)
            e.wait_ge(st_v, 16)

            wo = A["w_out"][0].rearrange("(k p) n -> p k n", p=P)
            for s in range(2):
                e.wait_ge(pa_mm, KD - 1 + s)
                e.dma_start(W[:, s, :, :], wo[:, :, s * P:(s + 1) * P]).then_inc(ld_o[s], 16)

            def gates_in(f, i):
                for g in range(2):
                    src = ext_dram[ds(3 * KP + g * KD + 2 * f + i, 1), :, :].rearrange("o p c -> p (o c)")
                    e.dma_start(gates[:, i, g, :], src).then_inc(ld_g[i], 16)

            e.wait_ge(act_na.sem, act_na.value(KP - 1, "out"))
            e.wait_ge(dve_na.sem, dve_na.value(KP - 1, f"P {NU - 1}"))
            e.wait_ge(pool_na.sem, pool_na.value(KP - 1, "bias 1"))
            for i in range(2):
                gates_in(0, i)
            with e.Fori(1, KD // 2) as f:
                for i in range(2):
                    wait_apart(e, zrow_done, (pe_mg.sem, pe_mg.value(f - 1, pe_mg.names[i])))
                    pb_in(2 * f + i, i)
                    wait_apart(e, zrow_done, (act_mg.sem, act_mg.value(f - 1, f"g{i}")))
                    gates_in(f, i)

            for i, name in enumerate(pe_mg.names):
                e.wait_ge(pe_mg.sem, pe_mg.value(KD // 2 - 1, name))
                e.dma_start(W[:, 2 + i, :, :], wo[:, :, (2 + i) * P:(3 + i) * P]).then_inc(ld_o[2 + i], 16)

            f1 = [A[w][0].rearrange("(k p) n -> p k n", p=P) for w in ("ffn_w1", "ffn_w3")]
            f2 = A["ffn_w2"][0].rearrange("(k p) n -> p k n", p=P)

            def up_in(q, f, s):
                if q or not isinstance(f, int):
                    e.wait_ge(w_lo[s], unit(q, "up", f) + 1)
                e.dma_start(raw2[:, s, 0:KD, :], f1[s][:, :, ds(f * P + q * KH * P, P)]).then_inc(ld_u[s], 16)

            def down_in(q, g, s):
                e.wait_ge(w_lo[s], unit(q, "down", g) + 1)
                e.dma_start(raw2[:, s, :, :], f2[:, q * KH:(q + 1) * KH, ds(g * (2 * P) + s * P, P)]).then_inc(ld_u[s], 16)

            def y_out(g, s):
                e.wait_ge(y_done[s], g + 2)
                c = ds(g * (2 * P) + s * P, P)
                e.dma_start(A["y_sample"][0].rearrange("(t p) c -> p t c", p=P)[:, :, c], yo[:, s, 0:CT, :]).then_inc(st_y[s], 16)
                e.dma_start(A["y_prompt"][0][:, c], yo[:, s, CT, :]).then_inc(st_y[s], 16)

            for s in range(2):
                up_in(0, 0, s)
            for i in range(4):
                e.wait_ge(wo_mm, i + 1)
                e.dma_start(W[:, i, :, :], wo[:, :, (4 + i) * P:(5 + i) * P]).then_inc(ld_o[i], 16)
            with e.Fori(1, KH) as f:
                for s in range(2):
                    up_in(0, f, s)
            with e.Fori(0, KD // 2) as g:
                for s in range(2):
                    down_in(0, g, s)
            with e.Fori(0, KH) as f:
                for s in range(2):
                    up_in(1, f, s)
            for s in range(2):
                down_in(1, 0, s)
            with e.Fori(1, KD // 2) as g:
                for s in range(2):
                    down_in(1, g, s)
                for s in range(2):
                    y_out(g - 1, s)
            for s in range(2):
                y_out(KD // 2 - 1, s)
            for s in range(2):
                e.wait_ge(st_y[s], 32 * (KD // 2) + 32)

        @block.tensor
        def _(e):
            e.wait_ge(ld_const, 32)
            e.wait_ge(ld_vec, 16 * 7)
            e.transpose(ps[:, 0, 0:81], rows[0:81, 0, :], sq_c[0:81, ID, 0:81])
            e.transpose(ps[:, 0, 128:200], rows[0:72, 1, :], sq_c[0:72, ID, 0:72]).then_inc(vec_turned, 1)
            for t in range(NT):
                e.wait_ge(ld_x[t], 16)
                for j in range(2):
                    n = 2 * t + j
                    if n >= 4:
                        e.wait_ge(x_out, n - 3)
                    for k in range(4):
                        m = e.transpose(ps[:, 1 + n % 4, k * P:(k + 1) * P], xin[:, t, (4 * j + k) * P:(4 * j + k + 1) * P], IDN)
                    m.then_inc(x_turned, 1)
            for k in range(KD):
                e.wait_ge(sq_done, k + 1)
                for b, (a, n) in enumerate(SEG):
                    m = e.matmul(ps[:, 5 + b, 0:n], ONES, sqx[:, k % 2, a:a + n], start=k == 0, stop=k == KD - 1, skip_group_check=True)
                m.then_inc(ss_done, 1)
            def ada_rows(dst, s):
                for k in range(KD):
                    m = e.matmul(dst, csT[:, :, k], WA[:, s:s + 2, k, :], start=k == 0, stop=k == KD - 1, skip_group_check=True)
                return m

            e.wait_ge(cond_silu, 1)
            e.wait_ge(x_out, 2 * NT)
            with e.Fori(0, 4) as i:
                for s in (0, 2):
                    for n in (s, s + 1):
                        e.wait_ge(ld_wa[n], i * 16 + 16)
                    e.wait_ge(ada_row, i * 2 + s // 2 + 1)
                    ada_rows(ps[0:2, 3 + s // 2, 0:2 * P], s).then_inc(ada_mm, 1)
            e.wait_ge(ada_row, 10)
            for c in range(16):
                m = e.transpose(ps[:, 7, 2 * c:2 * c + 2], arow0[0:2, c * P:(c + 1) * P], sq_c[0:2, ID, 0:2])
            m.then_inc(ada_mm, 1)
            def strip_mm(kind, k, h1):
                if k == 0:
                    e.wait_ge(ld_w[kind], h1 * 16)
                for b, (a, n) in enumerate(SEG):
                    m = e.matmul(ps[:, b, 0:n], W[:, slot[kind], k, :], hT[:, k, a:a + n], start=k == 0, stop=k == KD - 1, skip_group_check=True)
                if k == KD - 1:
                    m.then_inc(strip[kind], 1)

            e.wait_ge(vec_out, 1)
            e.wait_ge(ld_ba, 48)
            e.wait_ge(rms_done, 1)
            for k in range(KD):
                e.wait_ge(h_done, k + 1)
                strip_mm("q", k, 1)
                for b, (a, n) in enumerate(SEG):
                    m = e.matmul(ps[0:4 * H, 5 + b, 0:n], wba[:, k, :], hT[:, k, a:a + n], start=k == 0, stop=k == KD - 1, skip_group_check=True)
            m.then_inc(ba_mm, 1)
            for kind, before in (("k", "q"), ("v", "k")):
                e.wait_ge(raw[before], 1)
                for k in range(KD):
                    strip_mm(kind, k, 1)
                    if kind == "k" and k == 2:
                        e.wait_ge(ba_T, 1)
                        for t in range(NT):
                            m = e.transpose(ps[:, 7, 64 + t * 32:96 + t * 32], baT[:, t * P:(t + 1) * P], sq_c[0:4 * H, ID, 0:4 * H])
                        m.then_inc(ba_turned, 1)
                    if kind == "v" and k == 3:
                        e.wait_ge(ba_dve, 6)
                        gl = sp[:, 3, :, :]
                        for n, (mat, d) in enumerate(((LE, 0), (GE, 1), (GT, 0), (LT, 1), (ONE, 0), (ONE, 1))):
                            m = e.matmul(ps[:, 2, n * 40:(n + 1) * 40], sq_c[:, mat, :], gl[:, :, d * H:(d + 1) * H], start=True, stop=True, skip_group_check=True)
                        m.then_inc(cum_mm, 1)
            e.sem_inc(strip_e, 1)
            e.sem_inc(pe_dn.sem, pe_dn.n)

            def head(h, more):
                def wait(steps, name, turn=h):
                    e.wait_ge(steps.sem, steps.value(turn, name))

                fill = [(kind, k) for kind in (("k", 1, "v") if more else (2, 3, 4, 5)) for k in range(KD)]
                zfill = [("z", k) for k in range(KD)]

                def extra_mm(j, k):
                    if k == 0:
                        e.wait_ge(ld_e, h * (16 * NE) + 16 * (j + 1))
                    for b, (a, n) in enumerate(SEG):
                        m = e.matmul(ps[:, b, 0:n], WE[:, k, :], hT[:, k, a:a + n], start=k == 0, stop=k == KD - 1, skip_group_check=True)
                    if k == KD - 1:
                        m.then_inc(strip_e, 1)

                def filler(queue, n=1):
                    for _ in range(min(n, len(queue))):
                        kind, k = queue.pop(0)
                        if k == 0:
                            before = {"k": 1, "v": 2} if more else {2: 2, 3: 3, 4: 4, 5: 5, "z": 6}
                            if kind in before:
                                e.wait_ge(e_out, h * NE + (before[kind] + 1))
                            else:
                                e.wait_ge(raw[{1: "k", "z": "v"}[kind]], h + 2)
                        if isinstance(kind, int):
                            extra_mm(kind, k)
                        else:
                            strip_mm(kind, k, h + 1 if kind == "z" else h + 2)

                wait(pool_dn, "g mask")
                wait(dve_dn, "o out", h - 1)
                wait(act_dn, "ada", h - 1)
                for d in range(2):
                    e.matmul(ps[:, 2 + d, :], sq_c[:, (GT, LT)[d], :], gm[:, d * NT:d * NT + CT, :], start=True, stop=True)
                    m = e.matmul(ps[:, 4, d * P:(d + 1) * P], sq_c[:, (GT, LT)[d], :], gm[:, d * NT + CT, :], start=True, stop=True, skip_group_check=True)
                pe_dn.done(m, "dt")
                e.wait_ge(e_out, h * NE + 1)
                e.wait_ge(raw["v"], h + 1)
                for k in range(KD):
                    if more:
                        strip_mm("q", k, h + 2)
                    else:
                        extra_mm(0, k)
                wait(act_dn, "square")
                for w in range(2):
                    for t in range(NT):
                        m = e.matmul(ps[:, 7, 256 + w * NT + t:257 + w * NT + t], sqkq[:, t, w, :], sq_c[:, ONE, 0:1], start=True, stop=True, skip_group_check=True)
                pe_dn.done(m, "norm")
                for t in range(NT):
                    m = e.matmul(ps[:, 5 + t // 2, (t % 2) * 256:(t % 2) * 256 + 256], kq[:, t, 0, :], kq[:, t, :, :], start=True, stop=True, skip_group_check=True)
                pe_dn.done(m, "kq")
                wait(act_dn, "decay")
                wait(act_dn, "silu v")
                for w in range(2):
                    for t in range(NT):
                        at = 1 + t * P + (t == CT)
                        src = kq[:, t, 0, :] if w == 0 else conv[:, 2, at:at + P]
                        dst = ps[:, 2 + w, t * P:(t + 1) * P] if t < CT else ps[:, 4, w * P:(w + 1) * P]
                        m = e.transpose(dst, src, IDN)
                pe_dn.done(m, "turn k v")
                if more:
                    e.wait_ge(raw["q"], h + 2)
                else:
                    e.wait_ge(e_out, h * NE + 2)
                for k in range(KD):
                    extra_mm(0 if more else 1, k)
                wait(act_dn, "L diag")
                wait(dve_dn, "L diag")
                for u in range(U):
                    m = e.matmul(ps[:, 5, u * 32:(u + 1) * 32], LNTd[:, u, :], lv_c[:, 2 * len(LEVELS), :], start=True, stop=True, skip_group_check=True)
                pe_dn.done(m, "P0")
                for n in range(1, 6):
                    filler(fill, 2 if more else (3, 2, 3)[(2 * n - 2) % 3])
                    wait(dve_dn, f"X{n - 1}")
                    if n == 5:
                        wait(act_dn, "L pairs")
                    for u in range(U):
                        m = e.matmul(ps[:, 5, u * 32:(u + 1) * 32], (LNTd if n < 5 else LNTp)[:, u, :], Xc[:, u, :], start=True, stop=True, skip_group_check=True)
                    pe_dn.done(m, f"P{n}")
                    filler(fill, 2 if more else (3, 2, 3)[(2 * n - 1) % 3])
                    wait(dve_dn, f"XT{n - 1}")
                    if n < 5:
                        wait(dve_dn, f"P{n}")
                    else:
                        wait(act_dn, "P5")
                    for u in range(U):
                        m = e.matmul(ps[:, 6, u * 32:(u + 1) * 32], XTd[:, u, :], Pc[:, u, :], start=True, stop=True, skip_group_check=True)
                    pe_dn.done(m, f"Y{n}")
                filler(fill, 2)
                wait_apart(e, vec_out, (act_dn.sem, act_dn.value(h, "Y5")), (dve_dn.sem, dve_dn.value(h, "Y5")))
                for u in range(U):
                    lo, hi, d = (0, 64, 0) if u < NT else (64, 0, 1)
                    c = (u % NT) * 64
                    m = e.matmul(ps[hi:hi + 64, 5 + d, c:c + 64], LNT[lo:lo + 64, u, hi:hi + 64], X64[lo:lo + 64, u, :], start=True, stop=True, skip_group_check=True)
                pe_dn.done(m, "P6")
                filler(fill, 2 if more else 3)
                wait_apart(e, vec_out, (act_dn.sem, act_dn.value(h, "P6")), (dve_dn.sem, dve_dn.value(h, "P6")))
                for u in range(U):
                    lo, hi, d = (0, 64, 0) if u < NT else (64, 0, 1)
                    c = (u % NT) * 64
                    m = e.matmul(ps[lo:lo + 64, 2 + d, c:c + 64], P6c[hi:hi + 64, u, :], XT[hi:hi + 64, u, hi:hi + 64], start=True, stop=True, skip_group_check=True)
                pe_dn.done(m, "Y6")
                wait(act_dn, "Y6")
                wait(dve_dn, "Y6")
                wait(pool_dn, "kd")
                wait(pool_dn, "A")
                e.wait_ge(ld_S, 32 * (h + 1))
                for s in range(NT):
                    tile = ((CT, CT), (0, 3), (1, 2), (2, 1), (3, 0))[s]
                    if s:
                        for d in range(2):
                            if s > 1:
                                wait(dve_dn, f"S {s - 1} {'fb'[d]}")
                            for w in range(2):
                                m = e.matmul(ps[:, 2 + d, w * P:(w + 1) * P], kq[:, tile[d], w, :], S[:, d, :], start=True, stop=True, skip_group_check=True)
                            pe_dn.done(m, f"ks {s} {'fb'[d]}")
                        filler(zfill)
                    for d in range(2):
                        u = d * NT + tile[d]
                        if s:
                            wait(dve_dn, f"r {s} {'fb'[d]}")
                        m = e.matmul(ps[:, (4, 6)[d], 0:P], XT[:, u, :], rr[:, d, :] if s else vrow[:, CT, :], start=True, stop=True)
                        pe_dn.done(m, f"y {s} {'fb'[d]}")
                    filler(zfill)
                    for d in range(2):
                        u = d * NT + tile[d]
                        wait(act_dn, f"v {s} {'fb'[d]}")
                        if s:
                            wait(dve_dn, f"o {s - 1} {'fb'[d]}")
                        if s == 1:
                            wait(act_dn, f"state {'fb'[d]}")
                        if s < NT - 1:
                            e.matmul(ps[:, (5, 7)[d], P:2 * P], kd[:, u, :], vn[:, d, :], start=True, stop=True, skip_group_check=True)
                        m = e.matmul(ps[:, (5, 7)[d], 0:P], AT[:, u, :], vn[:, d, :], start=True, stop=True, skip_group_check=True)
                        pe_dn.done(m, f"av {s} {'fb'[d]}")
                filler(zfill, 99)
                wait(act_dn, f"v {NT - 1} f")
                for s in (0, 2):
                    for n in (s, s + 1):
                        e.wait_ge(ld_wa[n], h * 16 + 80)
                    m = ada_rows(ps[0:2, 4, s * P:(s + 2) * P], s)
                pe_dn.done(m, "ada rows")
                wait(act_dn, "silu z")
                for k in range(KD):
                    extra_mm((NE if more else NE_LAST) - 1, k)
                wait_apart(e, vec_out, (act_dn.sem, act_dn.value(h, "ada rows")), (dve_dn.sem, dve_dn.value(h, f"o {NT - 1} b")))
                for s in range(4):
                    m = e.transpose(ps[:, 7, 272 + 2 * s:274 + 2 * s], arow[0:2, s * P:(s + 1) * P], sq_c[0:2, ID, 0:2])
                pe_dn.done(m, "ada")
                wait(dve_dn, "o normed")
                for t in range(NT):
                    dst = ps[:, 2, t * P:(t + 1) * P] if t < CT else ps[:, 3, 0:P]
                    m = e.transpose(dst, osum[:, t, :], IDN)
                pe_dn.done(m, "turn o")

            with e.Fori(0, H - 1) as h:
                head(h, True)
            head(H - 1, False)

            e.wait_ge(act_dn.sem, act_dn.value(H - 1, "ada"))
            e.wait_ge(dve_dn.sem, dve_dn.value(H - 1, "o out"))
            e.wait_ge(e_out, NE * (H - 1) + NE_LAST + 1)
            for j in range(3):
                e.wait_ge(ld_fq[j], 16)
                for t in range(NT):
                    n = j * NT + t
                    if n >= 4:
                        e.wait_ge(proj_out, n - 3)
                    for s in range(KP):
                        m = e.transpose(ps[:, n % 4, s * P:(s + 1) * P], (fq, fk, fv)[j][:, s, t * P:(t + 1) * P], IDN)
                    m.then_inc(proj_mm, 1)
            e.wait_ge(proj_out, 3 * NT)
            e.sem_inc(pe_na.sem, pe_na.n)

            def pair(p):
                def wait(steps, name, turn=p):
                    e.wait_ge(steps.sem, steps.value(turn, name))

                fill = [(s, k) for s in range(2) for k in range(KD)]

                def filler(i):
                    if i % 5 == 4:
                        return
                    s, k = fill.pop(0)
                    if k == 0:
                        e.wait_ge(ld_pa[s], p * 16 + 16)
                        e.wait_ge(pa_out, 2 * p + (s + 1))
                    for b, (a, n) in enumerate(SEG):
                        m = e.matmul(ps[:, 6 + b, 0:n], W[:, s, k, :], oT[:, k, a:a + n], start=k == 0, stop=k == KD - 1, skip_group_check=True)
                    if k == KD - 1:
                        m.then_inc(pa_mm, 1)

                def score(i):
                    hh, c = UNITS[i]
                    tiles, at, _ = key_tiles(c)
                    rows_ = slice(64 * hh, 64 * hh + 64)
                    if i >= 2:
                        wait(dve_na, f"max {i - 2}")
                    q = qT[rows_, c, :] if c < CT else cT[rows_, 0, :]
                    if tiles:
                        keys = kT[rows_, tiles[0]:tiles[-1] + 1, :]
                        e.matmul(ps[:, i % 2, at:at + len(tiles) * P], q, keys, start=True, stop=True, skip_group_check=True)
                    m = e.matmul(ps[:, i % 2, 3 * P:4 * P], q, cT[rows_, 2 if c < CT else 1, :], start=True, stop=True, skip_group_check=True)
                    pe_na.done(m, f"score {i}")

                wait(dve_na, "k rows")
                wait(act_na, "T lat", p - 1)
                wait(dve_na, "T ctx", p - 1)
                wait(act_na, "out", p - 1)
                e.wait_ge(pa_out, 2 * p + 1)
                for t in range(CT):
                    e.transpose(ps[:, 6, t * P:(t + 1) * P], qrow[:, t, :], IDN)
                    e.transpose(ps[:, 7, t * P:(t + 1) * P], krow_n[:, t, :], IDN)
                e.transpose(ps[:, 5, 0:P], qrow[:, CT, :], IDN)
                e.transpose(ps[:, 5, P:2 * P], krow_n[:, CT, :], IDN)
                pe_na.done(e.transpose(ps[:, 5, 2 * P:3 * P], krow_n[:, NT, :], IDN), "turn")
                wait(act_na, "T lat")
                wait(dve_na, "T ctx")
                score(0)
                score(1)
                wait(act_na, "v rows")
                for i, (hh, c) in enumerate(UNITS):
                    tiles, at, _ = key_tiles(c)
                    chunks = [(at // P + j, t) for j, t in enumerate(tiles)] + [(3, NT if c < CT else CT)]
                    filler(i)
                    wait(dve_na, f"P {i}")
                    if i >= 2:
                        wait(act_na, f"PT {i - 2}")
                    for b, _ in chunks:
                        m = e.transpose(ps[:, 2 + i % 2, b * P:(b + 1) * P], Sx[:, i % 2, b * P:(b + 1) * P], IDN)
                    pe_na.done(m, f"turn P {i}")
                    if i + 2 < NU:
                        score(i + 2)
                    filler(i)
                    wait(act_na, f"PT {i}")
                    out = ps[64 * hh:64 * hh + 64, 4, c * P:(c + 1) * P] if c < CT else ps[64 * hh:64 * hh + 64, 5, 3 * P:4 * P]
                    for j, (b, t) in enumerate(chunks):
                        m = e.matmul(out, vrow_n[:, t, 64 * hh:64 * hh + 64], PT[:, i % 2, b * P:(b + 1) * P],
                                     start=j == 0, stop=j == len(chunks) - 1, skip_group_check=True)
                    pe_na.done(m, f"PV {i}")

            with e.Fori(0, KP) as p:
                pair(p)

            def product(bank, w, k_n, x, wait_k=None):
                for k in range(k_n):
                    if wait_k:
                        e.wait_ge(wait_k, k + 1)
                    for b, (a, n) in enumerate(SEG):
                        m = e.matmul(ps[:, bank + b, 0:n], w[:, k, :], x[:, k, a:a + n], start=k == 0, stop=k == k_n - 1, skip_group_check=True)
                return m

            e.wait_ge(act_na.sem, act_na.value(KP - 1, "out"))
            e.sem_inc(pe_mg.sem, pe_mg.n)
            with e.Fori(0, KD // 2) as f:
                for i, name in enumerate(pe_mg.names):
                    e.wait_ge(ld_m[i], f * 16 + 16)
                    e.wait_ge(dve_mg.sem, dve_mg.value(f - 1, f"y{i}"))
                    pe_mg.done(product(2 * i, W[:, 2 + i, :, :], KP, naT), name)

            def squares(k):
                e.wait_ge(sq2_done, k + 1)
                for b, (a, n) in enumerate(SEG):
                    m = e.matmul(ps[:, 6 + b, 0:n], ONES, sq2[:, k % 2, a:a + n], start=k == 0, stop=k == KD - 1, skip_group_check=True)
                m.then_inc(ss2_mm, 1)

            for s in range(2):
                e.sem_inc(w_used[s], 1)
            e.wait_ge(dve_mg.sem, dve_mg.value(KD // 2 - 1, "y1"))
            for n in range(KD):
                e.wait_ge(ld_o[n % 4], 16 * (n // 4 + 1))
                if n >= 3:
                    e.wait_ge(wo_x, n - 2)
                product(2 * (n % 3), W[:, n % 4, :, :], KD, yT).then_inc(wo_mm, 1)
                if n >= 2:
                    squares(n - 2)
            for k in (KD - 2, KD - 1):
                squares(k)

            def split_product(bank, s, k_n, x_part, wait_k):
                for k in range(k_n):
                    wait_k(k)
                    for n, (wp, xp) in enumerate(((0, 0), (0, 1), (1, 0))):
                        for b, (a, w) in enumerate(HALVES):
                            m = e.matmul(ps[:, bank + b, 0:w], w_part[wp][:, s, k, :], x_part[xp][:, k, a:a + w],
                                         start=k == 0 and n == 0, stop=k == k_n - 1 and n == 2, skip_group_check=True)
                return m

            def up(q, f, s, first=False):
                e.wait_ge(w_lo[s], unit(q, "up", f) + 2)
                e.wait_ge((silu_done, hid_done)[s], f + (KH * q + 1))

                def wait_k(k):
                    if first:
                        e.wait_ge(h_lo, k + 1)
                split_product(2 * s, s, KD, h_part, wait_k).then_inc(w_used[s], 1)

            def down(q, g, s):
                e.wait_ge(w_lo[s], unit(q, "down", g) + 2)
                e.wait_ge(x_done[s], g + (KD // 2 * q + 1))

                def wait_k(k):
                    if s == 0 and k in (0, KH - 1) and isinstance(g, int) and g == 0:
                        e.wait_ge(a_lo, KH * q + (KH + 1 if k else KH))
                split_product(4 + 2 * s, s, KH, a_part, wait_k).then_inc(w_used[s], 1)

            def turn_y(g, s):
                e.wait_ge(x_done[s], g + (KD // 2 + 2))
                e.wait_ge(y_done[s], g + 1)
                for t in range(NT):
                    m = e.transpose(ps[:, 2 * s + t // CT, (t % CT) * P:(t % CT + 1) * P], xo[:, s, t * P:(t + 1) * P], IDN)
                m.then_inc(y_turned[s], 1)

            for s in range(2):
                e.sem_inc(y_turned[s], 1)
            for q in range(2):
                if q == 0:
                    for s in range(2):
                        up(0, 0, s, first=True)
                with e.Fori(1 - q, KH) as f:
                    for s in range(2):
                        up(q, f, s)
                for s in range(2):
                    down(q, 0, s)
                    if q and s:
                        turn_y(0, 0)
                with e.Fori(1, KD // 2) as g:
                    for s in range(2):
                        down(q, g, s)
                        if q:
                            turn_y(g - (1 - s), 1 - s)
            turn_y(KD // 2 - 1, 1)

        @block.scalar
        def _(e):
            e.wait_ge(vec_turned, 1)
            e.activation(csT[:, :, :], ps[:, 0, 65:81].rearrange("p (a k) -> p a k", a=2), ACT.Silu).then_inc(cond_silu, 1)
            e.activation(cols[:, 0:65], ps[:, 0, 0:65], ACT.Copy)
            e.activation(cols[:, CONV:CONV + 72], ps[:, 0, 128:200], ACT.Copy).then_inc(vec_out, 1)
            for t in range(NT):
                for j in range(2):
                    n = 2 * t + j
                    e.wait_ge(x_turned, n + 1)
                    e.activation(xT[:, 4 * j:4 * j + 4, t * P:(t + 1) * P], ps[:, 1 + n % 4, :].rearrange("p (k c) -> p k c", k=4), ACT.Copy).then_inc(x_out, 1)
            e.wait_ge(x_out, 2 * NT)
            for k in range(KD):
                if k >= 2:
                    e.wait_ge(ss_done, k - 1)
                e.activation(sqx[:, k % 2, :], xT[:, k, :], ACT.Square).then_inc(sq_done, 1)
            e.wait_ge(ss_done, KD)
            e.wait_ge(zero_done, 1)
            for b, (a, n) in enumerate(SEG):
                m = e.activation(rms[:, a:a + n], ps[:, 5 + b, 0:n], ACT.Sqrt, bias=epsc[:, 0:1], scale=1.0 / D)
            m.then_inc(rms_done, 1)
            e.sem_inc(ada_row, 2)
            with e.Fori(0, 4) as i:
                for s in range(2):
                    e.wait_ge(ada_mm, i * 2 + (s + 1))
                    e.activation(arow0[0:2, ds(i * 4 * P + s * 2 * P, 2 * P)], ps[0:2, 3 + s, 0:2 * P], ACT.Copy).then_inc(ada_row, 1)
            def raw_out(kind, h1):
                j = "qkv".index(kind)
                e.wait_ge(strip[kind], h1)
                e.activation(raws[:, j, 1:1 + LAT], ps[:, 0, :], ACT.Copy)
                e.activation(raws[:, j, 2 + LAT:2 + TOK], ps[:, 1, 0:CTX], ACT.Copy).then_inc(raw[kind], 1)

            e.wait_ge(ld_ba, 48)
            e.activation(alog[:, :], alog[:, :], ACT.Exp).then_inc(ba_act, 1)
            e.wait_ge(ba_mm, 1)
            for b, (a, n) in enumerate(SEG):
                m = e.activation(baT[:, a:a + n], ps[0:4 * H, 5 + b, 0:n], ACT.Copy)
            m.then_inc(ba_T, 1)
            e.wait_ge(zero_done, 2)
            raw_out("q", 1)
            e.wait_ge(ba_dve, 1)
            e.activation(sp[:, 1, :, :], sp[:, 0, :, :], ACT.Abs).then_inc(ba_act, 1)
            e.wait_ge(ba_act, 2)
            e.activation(sp[:, 2, :, :], sp[:, 1, :, :], ACT.Exp, scale=-1.0).then_inc(ba_act, 1)
            e.wait_ge(ba_act, 3)
            e.activation(sp[:, 1, :, :], sp[:, 2, :, :], ACT.Ln, bias=1.0).then_inc(ba_act, 1)
            bet = ba[:, :, 0:2 * H].rearrange("p t (d h) -> p t d h", d=2)
            e.wait_ge(ba_dve, 1)
            pu = params[:, :, :, :].rearrange("p h k (d t) -> p h k d t", d=2)
            for d in range(2):
                e.activation(pu[:, :, BETA, d, :].rearrange("p h t -> p t h"), bet[:, :, d, :], ACT.Sigmoid)
            raw_out("k", 1)
            e.wait_ge(cum_mm, 1)
            for n in range(6):
                kind, d = (EG, EG, EK, EK, GL, GL)[n], n % 2
                src = ps[:, 2, n * 40:(n + 1) * 40].rearrange("p (t h) -> p t h", h=H)
                m = e.activation(pu[:, :, kind, d, :].rearrange("p h t -> p t h"), src, ACT.Exp)
            m.then_inc(prm_done, 1)

            def extra_out(j, h):
                e.wait_ge(strip_e, h * NE + (j + 2))
                e.wait_ge(st_e, h * (16 * NE) + 16 * (j + 1))
                blocks = ps[:, 0, :].rearrange("p (r b c) -> p b r c", r=ROWS, c=KC)
                e.activation(stage[:, 0:LAT].rearrange("p (b r c) -> p b r c", b=CT, c=KC), blocks, ACT.Copy)
                e.activation(stage[:, LAT:TOK], ps[:, 1, 0:CTX], ACT.Copy).then_inc(e_out, 1)

            raw_out("v", 1)
            e.sem_inc(st_e, 16)
            e.sem_inc(e_out, 1)
            e.sem_inc(act_dn.sem, act_dn.n)

            def head(h, more):
                def wait(steps, name, turn=h):
                    e.wait_ge(steps.sem, steps.value(turn, name))

                wait(pe_dn, "dt")
                wait(dve_dn, "L", h - 1)
                wait(pool_dn, "A", h - 1)
                for d in range(2):
                    e.activation(dt[:, d * NT:d * NT + CT, :], ps[:, 2 + d, :].rearrange("p (t c) -> p t c", t=CT), ACT.Exp)
                    m = e.activation(dt[:, d * NT + CT, :], ps[:, 4, d * P:(d + 1) * P], ACT.Exp)
                act_dn.done(m, "decay")
                wait(pe_dn, "turn o", h - 1)
                for kind in "qkv":
                    j = "qkv".index(kind)
                    wait(dve_dn, f"conv {kind}")
                    lat, ctx = conv[:, j, 1:1 + LAT], conv[:, j, 2 + LAT:2 + TOK]
                    to_lat, to_ctx = (lat, ctx) if kind == "v" else (kq[:, 0:CT, 1 - j, :], kq[:, CT, 1 - j, :])
                    if kind != "v":
                        lat = lat.rearrange("p (t c) -> p t c", t=CT)
                    e.activation(to_lat, lat, ACT.Silu)
                    m = e.activation(to_ctx, ctx, ACT.Silu)
                    act_dn.done(m, f"silu {kind}")
                wait(act_dn, "silu k")
                act_dn.done(e.activation(sqkq[:, :, :, :], kq[:, :, :, :], ACT.Square), "square")
                if more:
                    raw_out("q", h + 2)
                else:
                    extra_out(0, h)
                wait(pe_dn, "norm")
                wait(pe_dn, "kq")
                e.activation(nrm[:, 0, :], ps[:, 7, 256:256 + NT], ACT.Sqrt, bias=epsc[:, 0:1], scale=1.0)
                m = e.activation(nrm[:, 1, :], ps[:, 7, 256 + NT:256 + 2 * NT], ACT.Sqrt, bias=epsc[:, 1:2], scale=float(DK))
                act_dn.done(m, "norm")
                wait(pool_dn, "A", h - 1)
                for b in range(3):
                    n = 2 if b < 2 else 1
                    m = e.activation(kqs[:, 2 * b:2 * b + n, :, :], ps[:, 5 + b, 0:n * 256].rearrange("p (t w c) -> p t w c", t=n, w=2), ACT.Copy)
                act_dn.done(m, "kq")
                wait(pe_dn, "turn k v")
                wait(pool_dn, "kd", h - 1)
                act_dn.done(e.activation(krow[:, 0:CT, :], ps[:, 2, :].rearrange("p (t c) -> p t c", t=CT), ACT.Copy), "k rows")
                wait(dve_dn, "L")
                for q in (2, 3):
                    m = e.activation(LNTd[q * 32:q * 32 + 32, :, q * 32:q * 32 + 32], LNT[q * 32:q * 32 + 32, :, q * 32:q * 32 + 32], ACT.Copy)
                act_dn.done(m, "L diag")
                for p, c, u in ((0, 32, 0), (64, 96, 0), (32, 0, NT), (96, 64, NT)):
                    m = e.activation(LNTp[p:p + 32, u:u + NT, c:c + 32], LNT[p:p + 32, u:u + NT, c:c + 32], ACT.Copy)
                act_dn.done(m, "L pairs")
                if more:
                    extra_out(0, h)
                    raw_out("k", h + 2)
                    extra_out(1, h)
                else:
                    for j in (1, 2, 3, 4):
                        extra_out(j, h)
                wait(pe_dn, "P5")
                act_dn.done(e.activation(Pc[:, :, :], ps[:, 5, 0:U * 32].rearrange("p (u c) -> p u c", u=U), ACT.Copy), "P5")
                wait(pe_dn, "Y5")
                act_dn.done(e.activation(Yc[:, :, :], ps[:, 6, 0:U * 32].rearrange("p (u c) -> p u c", u=U), ACT.Copy), "Y5")
                wait(pe_dn, "P6")
                act_dn.done(e.activation(P6c[64:128, 0:NT, :], ps[64:128, 5, 0:NT * 64].rearrange("p (u c) -> p u c", u=NT), ACT.Copy), "P6")
                if more:
                    raw_out("v", h + 2)
                else:
                    extra_out(5, h)
                wait(pe_dn, "Y6")
                act_dn.done(e.activation(XT[0:64, 0:NT, 64:128], ps[0:64, 2, 0:NT * 64].rearrange("p (u c) -> p u c", u=NT), ACT.Copy), "Y6")
                for s in range(NT):
                    tile = ((CT, CT), (0, 3), (1, 2), (2, 1), (3, 0))[s]
                    if s:
                        for d in range(2):
                            u = d * NT + tile[d]
                            wait(pe_dn, f"ks {s} {'fb'[d]}")
                            if s > 1:
                                wait(dve_dn, f"o {s - 1} {'fb'[d]}")
                            wait(dve_dn, f"r {s} {'fb'[d]}")
                            act_dn.done(e.activation(tq[:, d, :], ps[:, 2 + d, P:2 * P], ACT.Copy, scale=prm[:, EG, u:u + 1]), f"qs {s} {'fb'[d]}")
                    for d in range(2):
                        u = d * NT + tile[d]
                        wait(pe_dn, f"y {s} {'fb'[d]}")
                        if s:
                            wait(pe_dn, f"av {s - 1} {'fb'[d]}")
                        act_dn.done(e.activation(vn[:, d, :], ps[:, (4, 6)[d], 0:P], ACT.Copy, scale=bk[:, 0, u:u + 1]), f"v {s} {'fb'[d]}")
                    if not s:
                        e.wait_ge(st_S, (h * 2 + 2) * 16)
                        for d in range(2):
                            wait(pe_dn, f"av 0 {'fb'[d]}")
                            wait(dve_dn, f"o 0 {'fb'[d]}")
                            act_dn.done(e.activation(Sc[:, d, :], ps[:, (5, 7)[d], P:2 * P], ACT.Copy), f"state {'fb'[d]}")
                e.wait_ge(strip["z"], h + 2)
                wait(dve_dn, "o out", h - 1)
                e.activation(zs[:, 0:LAT], ps[:, 0, :], ACT.Silu)
                act_dn.done(e.activation(zs[:, LAT:TOK], ps[:, 1, 0:CTX], ACT.Silu), "silu z")
                wait(pe_dn, "ada rows")
                wait(pe_dn, "ada", h - 1)
                act_dn.done(e.activation(arow[0:2, :], ps[0:2, 4, :], ACT.Copy), "ada rows")
                wait(dve_dn, "o scaled")
                for t in range(NT):
                    m = e.activation(osq[:, t, :], osc[:, t, :], ACT.Square, accum_out=oss[:, t:t + 1])
                act_dn.done(m, "o square")
                wait(act_dn, "o square")
                act_dn.done(e.activation(orm[:, :], oss[:, :], ACT.Sqrt, bias=epsc[:, 0:1], scale=1.0 / DK), "o norm")
                wait(pe_dn, "ada")
                m = e.activation(mods[:, ds(16 + h * 4, 4), :], ps[:, 7, 272:280].rearrange("p (s c) -> p s c", s=4), ACT.Copy)
                act_dn.done(m, "ada")
                extra_out((NE if more else NE_LAST) - 1, h)

            with e.Fori(0, H - 1) as h:
                head(h, True)
            head(H - 1, False)

            e.wait_ge(dve_dn.sem, dve_dn.value(H - 1, "o out"))
            e.wait_ge(pe_dn.sem, pe_dn.value(H - 1, "turn o"))
            e.wait_ge(pool_dn.sem, pool_dn.value(H - 1, "A"))
            for j in range(3):
                for t in range(NT):
                    n = j * NT + t
                    e.wait_ge(proj_mm, n + 1)
                    e.activation(qkv[:, j, t, :], ps[:, n % 4, :], ACT.Copy).then_inc(proj_out, 1)
                    if j < 2:
                        if n >= 2:
                            e.wait_ge(nss_done, n - 1)
                        e.wait_ge(proj_out, n + 1)
                        e.activation(nsq[:, n % 2, :], qkv[:, j, t, :], ACT.Square).then_inc(nsq_done, 1)
                if j < 2:
                    e.wait_ge(nss_done, NT * (j + 1))
                    e.activation(nrms[:, j, :, :], nss[:, j, :, :], ACT.Sqrt, bias=epsc[:, 0:1], scale=1.0 / NA_D).then_inc(nrms_done, 1)
            e.wait_ge(ld_nc, 80)
            e.wait_ge(proj_out, 3 * NT)
            e.sem_inc(pa_out, 1)
            e.sem_inc(act_na.sem, act_na.n)

            def pair(p):
                def wait(steps, name, turn=p):
                    e.wait_ge(steps.sem, steps.value(turn, name))

                wait(pe_na, f"PV {NU - 1}", p - 1)
                e.activation(vrow_n[:, 0:NT, :], qkv[:, 2, :, ds(p * P, P)], ACT.Copy)
                act_na.done(e.activation(vrow_n[:, NT, :], cv[:, ds(p * P, P)], ACT.Copy), "v rows")
                wait(pe_na, "turn")
                e.activation(qT[:, :, :], ps[:, 6, :].rearrange("p (t c) -> p t c", t=CT), ACT.Copy)
                act_na.done(e.activation(kT[:, :, :], ps[:, 7, :].rearrange("p (t c) -> p t c", t=CT), ACT.Copy), "T lat")
                for i in range(NU + 1):
                    if i and i % 5 == 0:
                        s = i // 5 - 1
                        e.wait_ge(pa_mm, 2 * p + (s + 1))
                        e.activation(hT[:, ds(2 * p + s, 1), 0:LAT].rearrange("p o c -> p (o c)"), ps[:, 6, :], ACT.Copy)
                        e.activation(hT[:, ds(2 * p + s, 1), LAT:TOK].rearrange("p o c -> p (o c)"), ps[:, 7, 0:CTX], ACT.Copy).then_inc(pa_out, 1)
                    if i < NU:
                        _, _, (lo, hi) = key_tiles(UNITS[i][1])
                        wait(dve_na, f"-max {i}")
                        m = e.activation(Sx[:, i % 2, lo:hi], Sx[:, i % 2, lo:hi], ACT.Exp, bias=nmx[:, i:i + 1], accum_out=sm[:, i:i + 1])
                        act_na.done(m, f"exp {i}")
                    if i:
                        _, at, (lo, hi) = key_tiles(UNITS[i - 1][1])
                        wait(pe_na, f"turn P {i - 1}")
                        if i >= 3:
                            wait(pe_na, f"PV {i - 3}")
                        act_na.done(e.activation(PT[:, (i - 1) % 2, lo:hi], ps[:, 2 + (i - 1) % 2, lo:hi], ACT.Copy), f"PT {i - 1}")
                wait(pe_na, f"PV {NU - 1}")
                o = naT[:, ds(p, 1), 0:LAT].rearrange("p o (r b c) -> p (o b) r c", r=ROWS, c=KC)
                e.activation(o, ps[:, 4, :].rearrange("p (b r c) -> p b r c", b=CT, c=KC), ACT.Copy)
                act_na.done(e.activation(naT[:, ds(p, 1), LAT:TOK].rearrange("p o c -> p (o c)"), ps[:, 5, 3 * P:4 * P], ACT.Copy), "out")

            with e.Fori(0, KP) as p:
                pair(p)

            e.wait_ge(act_na.sem, act_na.value(KP - 1, "out"))
            e.wait_ge(dve_na.sem, dve_na.value(KP - 1, f"P {NU - 1}"))
            e.wait_ge(st_v, 16)
            e.wait_ge(st_k, 16 * KP + 16)
            e.wait_ge(pool_na.sem, pool_na.value(KP - 1, "bias 1"))
            e.sem_inc(act_mg.sem, 2)
            with e.Fori(0, KD // 2) as f:
                for i in range(2):
                    e.wait_ge(ld_g[i], f * 32 + 32)
                    e.wait_ge(dve_mg.sem, dve_mg.value(f - 1, f"yB{i}"))
                    for g in range(2):
                        blocks = gates[:, i, g, 0:LAT].rearrange("p (b r c) -> p r b c", b=CT, c=KC)
                        e.activation(sgm[:, i, g, 0:LAT].rearrange("p (r b c) -> p r b c", b=CT, c=KC), blocks, ACT.Sigmoid)
                    act_mg.done(e.activation(sgm[:, i, :, LAT:TOK], gates[:, i, :, LAT:TOK], ACT.Sigmoid), f"g{i}")

            for n in range(KD):
                e.wait_ge(wo_x, n + 1)
                if n >= 2:
                    e.wait_ge(ss2_mm, n - 1)
                e.activation(sq2[:, n % 2, :], xT[:, n, :], ACT.Square).then_inc(sq2_done, 1)
            e.wait_ge(ss2_mm, KD)
            for b, (a, n) in enumerate(SEG):
                m = e.activation(rms2[:, a:a + n], ps[:, 6 + b, 0:n], ACT.Sqrt, bias=epsc[:, 0:1], scale=1.0 / D)
            m.then_inc(rms2_done, 1)

            def w_big(q, kind, turn, s):
                e.wait_ge(ld_u[s], unit(q, kind, turn) * 16 + 16)
                e.wait_ge(w_used[s], unit(q, kind, turn) + 1)
                k = KD if kind == "up" else KH
                e.activation(w_part[0][:, s, 0:k, :], raw2[:, s, 0:k, :], ACT.Copy).then_inc(w_hi[s], 1)

            w_big(0, "up", 0, 0)
            w_big(0, "up", 0, 1)
            for k in range(KD):
                e.wait_ge(xn2_done, k + 1)
                for b, (a, n) in enumerate(SEG):
                    m = e.activation(h2[:, k % 2, a:a + n], h2[:, k % 2, a:a + n], ACT.Identity, scale=gain2[:, k, b:b + 1], bias=mods[:, 24 + k, b:b + 1])
                m.then_inc(h2_done, 1)
                e.wait_ge(h2_done, k + 1)
                e.activation(h_part[0][:, k, :], h2[:, k % 2, :], ACT.Copy).then_inc(h_hi, 1)

            def silu(q, f):
                e.wait_ge(w_used[0], unit(q, "up", f) + 2)
                e.wait_ge(hid_done, f + (KH * q + 1))
                for b, (a, n) in enumerate(HALVES):
                    m = e.activation(sg[:, a:a + n], ps[:, b, 0:n], ACT.Silu)
                m.then_inc(silu_done, 1)

            def hid_big(q, f):
                e.wait_ge(hid_done, f + (KH * q + 2))
                e.activation(a_part[0][:, ds(f, 1), :].rearrange("p o c -> p (o c)"), hid, ACT.Copy).then_inc(a_hi, 1)

            def y_out(g, s):
                e.wait_ge(y_turned[s], g + 2)
                e.wait_ge(st_y[s], g * 32 + 32)
                e.activation(yo[:, s, 0:CT, :], ps[:, 2 * s, :].rearrange("p (t c) -> p t c", t=CT), ACT.Copy)
                e.activation(yo[:, s, CT, :], ps[:, 2 * s + 1, 0:P], ACT.Copy).then_inc(y_done[s], 1)

            e.sem_inc(silu_done, 1)
            for s in range(2):
                e.sem_inc(y_done[s], 1)
                e.sem_inc(st_y[s], 32)
            silu(0, 0)
            for q in range(2):
                if q:
                    w_big(1, "up", 0, 0)
                    w_big(1, "up", 0, 1)
                    silu(1, 0)
                with e.Fori(1, KH) as f:
                    w_big(q, "up", f, 0)
                    hid_big(q, f - 1)
                    w_big(q, "up", f, 1)
                    silu(q, f)
                w_big(q, "down", 0, 0)
                hid_big(q, KH - 1)
                w_big(q, "down", 0, 1)
                with e.Fori(1, KD // 2) as g:
                    for s in range(2):
                        w_big(q, "down", g, s)
                        if q:
                            y_out(g - 1, s)
            for s in range(2):
                y_out(KD // 2 - 1, s)

        @block.vector
        def _(e):
            e.memset(epsc[:, 0:1], EPS)
            e.memset(epsc[:, 1:2], DK * EPS).then_inc(zero_done, 1)
            e.memset(raws[:, :, :], 0.0).then_inc(zero_done, 1)
            e.memset(LNTd[:, :, :], 0.0)
            e.memset(LNTp[:, :, :], 0.0)
            e.memset(XTd[:, :, :], 0.0)
            e.memset(XT[:, :, :], 0.0)
            e.memset(X64[:, :, :], 0.0)
            e.memset(conv[:, :, :], 0.0).then_inc(zero_done, 1)
            e.wait_ge(rms_done, 1)
            e.reciprocal(rstd[:, :], rms[:, :]).then_inc(rstd_done, 1)
            e.wait_ge(vec_out, 1)
            e.wait_ge(ada_mm, 9)
            b = cols[:, B_ADA:B_ADA + 16].unsqueeze(2).to_broadcast([P, 16, 2])
            e.tensor_tensor(mods[:, 0:16, :], ps[:, 7, 0:32].rearrange("p (s c) -> p s c", s=16), b, ALU.add).then_inc(ada_out, 1)
            e.wait_ge(ada_out, 1)
            e.scalar_tensor_tensor(gain1[:, :, :], mods[:, 8:16, :], 1.0, cols[:, N1:N1 + 8].unsqueeze(2).to_broadcast([P, KD, 2]), ALU.add, ALU.mult).then_inc(gain_done, 1)
            e.wait_ge(gain_done, 1)
            e.wait_ge(rstd_done, 1)
            e.wait_ge(x_out, 2 * NT)
            for k in range(KD):
                e.tensor_tensor(hT[:, k, :], xT[:, k, :], rstd[:, :], ALU.mult).then_inc(xn_done, 1)
                e.wait_ge(xn_done, k + 1)
                for b, (a, n) in enumerate(SEG):
                    m = e.tensor_scalar(hT[:, k, a:a + n], hT[:, k, a:a + n], gain1[:, k, b:b + 1], mods[:, k, b:b + 1], ALU.mult, ALU.add)
                m.then_inc(h_done, 1)
            e.wait_ge(ba_turned, 1)
            e.wait_ge(ld_ba, 48)
            e.tensor_copy(ba[:, :, :], ps[:, 7, 64:64 + NT * 32].rearrange("p (t c) -> p t c", t=NT))
            e.tensor_tensor(sp[:, 0, :, :], ps[:, 7, 64:64 + NT * 32].rearrange("p (t c) -> p t c", t=NT)[:, :, 2 * H:4 * H], dtb[:, :].unsqueeze(1).to_broadcast([P, NT, 2 * H]), ALU.add).then_inc(ba_dve, 1)
            e.wait_ge(ba_dve, 1)
            e.tensor_scalar(sp[:, 3, :, :], sp[:, 0, :, :], 0.0, None, ALU.max).then_inc(ba_dve, 1)
            e.wait_ge(ba_dve, 2)
            e.wait_ge(ba_act, 4)
            e.tensor_tensor(sp[:, 2, :, :], sp[:, 3, :, :], sp[:, 1, :, :], ALU.add).then_inc(ba_dve, 1)
            e.wait_ge(ba_dve, 3)
            e.tensor_scalar(sp[:, 0, :, :], sp[:, 2, :, :], -1.0, None, ALU.mult).then_inc(ba_dve, 1)
            e.wait_ge(ba_dve, 4)
            e.tensor_tensor(sp[:, 3, :, :], sp[:, 0, :, :], alog[:, :].unsqueeze(1).to_broadcast([P, NT, 2 * H]), ALU.mult).then_inc(ba_dve, 1)
            e.wait_ge(ba_dve, 5)
            pu = params[:, :, :, :].rearrange("p h k (d t) -> p h k d t", d=2)
            for d in range(2):
                m = e.tensor_copy(pu[:, :, G, d, :].rearrange("p h t -> p t h"), sp[:, 3, :, d * H:(d + 1) * H])
            m.then_inc(ba_dve, 1)
            e.wait_ge(prm_done, 1)
            e.tensor_scalar(params[:, :, NEG_EG, :], params[:, :, EG, :], -1.0, None, ALU.mult).then_inc(prm_done, 1)
            e.wait_ge(prm_done, 2)
            e.wait_ge(cum_mm, 1)
            e.wait_ge(zero_done, 3)
            e.sem_inc(dve_dn.sem, dve_dn.n)

            def head(h, more):
                def wait(steps, name, turn=h):
                    e.wait_ge(steps.sem, steps.value(turn, name))

                def done(m, name):
                    dve_dn.done(m, name)

                wait(act_dn, f"v {NT - 1} b", h - 1)
                wait(pool_dn, "kd", h - 1)
                done(e.tensor_copy(prm[:, :, :], params[:, ds(h, 1), :, :].rearrange("p o k u -> p (o k) u")), "prm")
                ctap = cols[:, CONV:CONV + 72].rearrange("p (t j h) -> p t j h", t=3, j=3)
                done(e.tensor_copy(taps[:, :, :], ctap[:, :, :, ds(h, 1)].rearrange("p t j o -> p t (j o)")), "taps")
                wait(dve_dn, "taps")
                w = TOK + 1
                for kind in "qkv":
                    j = "qkv".index(kind)
                    e.wait_ge(raw[kind], h + 1)
                    if kind == "v":
                        wait(pe_dn, "turn k v", h - 1)
                    else:
                        wait(act_dn, f"silu {kind}", h - 1)
                    e.tensor_scalar(conv[:, j, 1:1 + w], raws[:, j, 1:1 + w], taps[:, 1, j:j + 1], None, ALU.mult).then_inc(conv_part, 1)
                    e.wait_ge(conv_part, h * 6 + 2 * j + 1)
                    e.scalar_tensor_tensor(conv[:, j, 1:1 + w], raws[:, j, 0:w], taps[:, 0, j:j + 1], conv[:, j, 1:1 + w], ALU.mult, ALU.add).then_inc(conv_part, 1)
                    e.wait_ge(conv_part, h * 6 + 2 * j + 2)
                    done(e.scalar_tensor_tensor(conv[:, j, 1:1 + w], raws[:, j, 2:2 + w], taps[:, 2, j:j + 1], conv[:, j, 1:1 + w], ALU.mult, ALU.add), f"conv {kind}")
                wait(act_dn, "norm")
                done(e.reciprocal(rn[:, :, :], nrm[:, :, :]), "1/norm")
                wait(dve_dn, "1/norm")
                b2 = prm[:, BETA, :].rearrange("p (d t) -> p d t", d=2)
                bko = bk[:, :, :].rearrange("p s (d t) -> p s d t", d=2)
                rk = rn[:, 0, :].unsqueeze(1).to_broadcast([P, 2, NT])
                done(e.tensor_tensor(bko[:, 1, :, :], b2, rk, ALU.mult), "beta")
                wait(dve_dn, "beta")
                e.tensor_tensor(bko[:, 0, :, :], bko[:, 1, :, :], rk, ALU.mult).then_inc(bk_part, 1)
                e.wait_ge(bk_part, h + 1)
                done(e.tensor_scalar(bk[:, 1, :], bk[:, 0, :], -1.0, None, ALU.mult), "-beta")
                wait(pe_dn, "turn k v")
                vb = nrm[:, 0, 0:CT].unsqueeze(2).to_broadcast([P, CT, P])
                done(e.tensor_tensor(vrow[:, 0:CT, :], ps[:, 3, :].rearrange("p (t c) -> p t c", t=CT), vb, ALU.mult), "v rows")
                e.tensor_scalar(vrow[:, CT, :], ps[:, 4, P:2 * P], nrm[:, 0, CT:CT + 1], None, ALU.mult)
                done(e.tensor_copy(krow[:, CT, :], ps[:, 4, 0:P]), "kv ctx")
                wait(act_dn, "kq")
                wait(pool_dn, "decay")
                wait(dve_dn, "-beta")
                for u in range(U):
                    m = e.scalar_tensor_tensor(LNT[:, u, :], kqs[:, u % NT, 0, :], bk[:, 1, u:u + 1], dtm[:, u, :], ALU.mult, ALU.mult)
                done(m, "L")
                wait(dve_dn, "L")
                for q in (0, 1):
                    m = e.tensor_copy(LNTd[q * 32:q * 32 + 32, :, q * 32:q * 32 + 32], LNT[q * 32:q * 32 + 32, :, q * 32:q * 32 + 32])
                done(m, "L diag")
                pc4, xc4 = typed(Pc[:, :, :]), typed(Xc[:, :, :])
                for n in range(5):
                    wait(pe_dn, f"P{n}")
                    mask = lv_c[:, 2 * n:2 * n + 2, :].unsqueeze(2).to_broadcast([P, 2, NT, 32])
                    done(e.tensor_tensor(pc4, ps[:, 5, 0:U * 32].rearrange("p (d t c) -> p d t c", d=2, t=NT), mask, ALU.mult), f"P{n}")
                    if n:
                        wait(pe_dn, f"Y{n}")
                        done(e.tensor_tensor(Xc[:, :, :], Xc[:, :, :], ps[:, 6, 0:U * 32].rearrange("p (u c) -> p u c", u=U), ALU.add), f"X{n}")
                    else:
                        wait(dve_dn, "P0")
                        done(e.tensor_tensor(Xc[:, :, :], Pc[:, :, :], lv_c[:, 2 * len(LEVELS), :].unsqueeze(1).to_broadcast([P, U, 32]), ALU.add), "X0")
                    wait(dve_dn, f"X{n}")
                    for q in range(4):
                        m = e.transpose(XTd[q * 32:q * 32 + 32, :, q * 32:q * 32 + 32], Xc[q * 32:q * 32 + 32, :, :])
                    done(m, f"XT{n}")
                e.tensor_copy(X64[0:32, 0:NT, 0:32], Xc[0:32, 0:NT, :])
                e.tensor_copy(X64[32:64, 0:NT, 32:64], Xc[32:64, 0:NT, :])
                e.tensor_copy(X64[64:96, NT:U, 0:32], Xc[64:96, NT:U, :])
                done(e.tensor_copy(X64[96:128, NT:U, 32:64], Xc[96:128, NT:U, :]), "X64")
                for q in range(4):
                    m = e.transpose(XT[q * 32:q * 32 + 32, :, q * 32:q * 32 + 32], Xc[q * 32:q * 32 + 32, :, :])
                done(m, "XT diag")
                wait(act_dn, "Y5")
                e.tensor_copy(X64[32:64, 0:NT, 0:32], Yc[32:64, 0:NT, :])
                done(e.tensor_copy(X64[64:96, NT:U, 32:64], Yc[64:96, NT:U, :]), "Y5")
                e.transpose(XT[0:32, 0:NT, 32:64], Yc[32:64, 0:NT, :])
                e.transpose(XT[64:96, 0:NT, 96:128], Yc[96:128, 0:NT, :])
                e.transpose(XT[32:64, NT:U, 0:32], Yc[0:32, NT:U, :])
                done(e.transpose(XT[96:128, NT:U, 64:96], Yc[64:96, NT:U, :]), "XT64")
                wait(pe_dn, "P6")
                done(e.tensor_copy(P6c[0:64, NT:U, :], ps[0:64, 6, 0:NT * 64].rearrange("p (u c) -> p u c", u=NT)), "P6")
                wait(pe_dn, "Y6")
                done(e.tensor_copy(XT[64:128, NT:U, 0:64], ps[64:128, 3, 0:NT * 64].rearrange("p (u c) -> p u c", u=NT)), "Y6")
                for s in range(NT):
                    tile = ((CT, CT), (0, 3), (1, 2), (2, 1), (3, 0))[s]
                    if s:
                        for d in range(2):
                            u = d * NT + tile[d]
                            wait(pe_dn, f"ks {s} {'fb'[d]}")
                            wait(dve_dn, "kv ctx")
                            done(e.scalar_tensor_tensor(rr[:, d, :], ps[:, 2 + d, 0:P], prm[:, NEG_EG, u:u + 1], vrow[:, tile[d], :], ALU.mult, ALU.add), f"r {s} {'fb'[d]}")
                    for d in range(2):
                        u = d * NT + tile[d]
                        if 0 < s < NT - 1:
                            wait(pe_dn, f"av {s} {'fb'[d]}")
                            if s > 1:
                                wait(dve_dn, f"S {s - 1} {'fb'[d]}")
                            else:
                                e.wait_ge(ld_S, 32 * (h + 1))
                            done(e.scalar_tensor_tensor(S[:, d, :], S[:, d, :], prm[:, GL, u:u + 1], ps[:, (5, 7)[d], P:2 * P], ALU.mult, ALU.add), f"S {s} {'fb'[d]}")
                    for d in range(2):
                        wait(pe_dn, f"av {s} {'fb'[d]}")
                        if s:
                            wait(act_dn, f"qs {s} {'fb'[d]}")
                            m = e.tensor_tensor(ob[:, d, tile[d], :], ps[:, (5, 7)[d], 0:P], tq[:, d, :], ALU.add)
                        else:
                            m = e.tensor_copy(ob[:, d, CT, :], ps[:, (5, 7)[d], 0:P])
                        done(m, f"o {s} {'fb'[d]}")
                wait(dve_dn, f"o {NT - 1} b")
                wait(pe_dn, "turn o", h - 1)
                done(e.tensor_tensor(osum[:, :, :], ob[:, 0, :, :], ob[:, 1, :, :], ALU.add), "o sum")
                wait(dve_dn, "o sum")
                done(e.tensor_tensor(osc[:, :, :], osum[:, :, :], rn[:, 1, :].unsqueeze(2).to_broadcast([P, NT, P]), ALU.mult), "o scaled")
                wait(act_dn, "o norm")
                done(e.reciprocal(orn[:, :], orm[:, :]), "1/o norm")
                wait(dve_dn, "1/o norm")
                done(e.tensor_tensor(osum[:, :, :], osc[:, :, :], orn[:, :].unsqueeze(2).to_broadcast([P, NT, P]), ALU.mult), "o normed")
                wait(pe_dn, "turn o")
                wait(act_dn, "silu z")
                oh = oT[:, ds(h, 1), :].rearrange("p o c -> p (o c)")
                e.scalar_tensor_tensor(oT[:, ds(h, 1), 0:LAT].rearrange("p o c -> p (o c)"), ps[:, 2, :], cols[:, DNG:DNG + 1], zs[:, 0:LAT], ALU.mult, ALU.mult)
                done(e.scalar_tensor_tensor(oT[:, ds(h, 1), LAT:TOK].rearrange("p o c -> p (o c)"), ps[:, 3, 0:CTX], cols[:, DNG:DNG + 1], zs[:, LAT:TOK], ALU.mult, ALU.mult), "o out")

            with e.Fori(0, H - 1) as h:
                head(h, True)
            head(H - 1, False)

            for j in range(2):
                for t in range(NT):
                    n = j * NT + t
                    e.wait_ge(nsq_done, n + 1)
                    e.tensor_reduce(nss[:, j, t, :], nsq[:, n % 2, :].rearrange("p (h d) -> p h d", d=NA_D), AX.X, ALU.add).then_inc(nss_done, 1)
                e.wait_ge(nrms_done, j + 1)
                e.reciprocal(nrn[:, j, :, :], nrms[:, j, :, :]).then_inc(nrn_done, 1)
                e.wait_ge(nrn_done, j + 1)
                for t in range(NT):
                    row = qkv[:, j, t, :].rearrange("p (h d) -> p h d", d=NA_D)
                    m = e.tensor_tensor(row, row, nrn[:, j, t, :].unsqueeze(2).to_broadcast([P, NA_H, NA_D]), ALU.mult)
                m.then_inc(nrow_done, 1)
            e.wait_ge(ld_nc, 80)
            e.tensor_scalar(ngain[:, 0, :], ngain[:, 0, :], float(NA_D) ** -0.5, None, ALU.mult).then_inc(ngain_done, 1)
            e.wait_ge(ngain_done, 1)
            e.wait_ge(nrow_done, 2)
            e.sem_inc(dve_na.sem, dve_na.n)
            e.sem_inc(st_k, 16)

            def pair(p):
                def wait(steps, name, turn=p):
                    e.wait_ge(steps.sem, steps.value(turn, name))

                wait(pe_na, "turn", p - 1)
                for j, rows_ in enumerate((qrow, krow_n)):
                    if j:
                        e.wait_ge(st_k, p * 16 + 16)
                        e.tensor_copy(krow_n[:, NT, :], ck[:, ds(p * P, P)])
                    g = ngain[:, j, :].unsqueeze(1).to_broadcast([P, 2 * NT, NA_D])
                    src = qkv[:, j, :, ds(p * P, P)].rearrange("p t (h d) -> p t h d", d=NA_D)
                    dst = rows_[:, 0:NT, :].rearrange("p t (h d) -> p t h d", d=NA_D)
                    g = ngain[:, j, :].unsqueeze(1).unsqueeze(1).to_broadcast([P, NT, 2, NA_D])
                    dve_na.done(e.tensor_tensor(dst, src, g, ALU.mult), ("q rows", "k rows")[j])
                wait(pe_na, "turn")
                dve_na.done(e.tensor_copy(cT[:, :, :], ps[:, 5, 0:3 * P].rearrange("p (t c) -> p t c", t=3)), "T ctx")
                for i in range(NU + 1):
                    if i < NU:
                        hh, c = UNITS[i]
                        _, _, (lo, hi) = key_tiles(c)
                        wait_apart(e, ngain_done, (pe_na.sem, pe_na.value(p, f"score {i}")), (pool_na.sem, pool_na.value(p, f"bias {hh}")))
                        add = bm[:, hh, c if c < CT else 0, lo:hi]
                        m = e.tensor_tensor_reduce(Sx[:, i % 2, lo:hi], ps[:, i % 2, lo:hi], add, 1.0, -3.0e38, ALU.add, ALU.max, mx[:, i:i + 1])
                        dve_na.done(m, f"max {i}")
                        wait(dve_na, f"max {i}")
                        dve_na.done(e.tensor_scalar(nmx[:, i:i + 1], mx[:, i:i + 1], -1.0, None, ALU.mult), f"-max {i}")
                    if i:
                        _, _, (lo, hi) = key_tiles(UNITS[i - 1][1])
                        wait(act_na, f"exp {i - 1}")
                        dve_na.done(e.reciprocal(rs[:, i - 1:i], sm[:, i - 1:i]), f"1/sum {i - 1}")
                        wait(dve_na, f"1/sum {i - 1}")
                        row = Sx[:, (i - 1) % 2, lo:hi]
                        dve_na.done(e.tensor_scalar(row, row, rs[:, i - 1:i], None, ALU.mult), f"P {i - 1}")

            with e.Fori(0, KP) as p:
                pair(p)

            e.tensor_tensor(mods[:, 16:48, :], mods[:, 16:48, :], cols[:, B_ADA + 16:B_ADA + 48].unsqueeze(2).to_broadcast([P, 32, 2]), ALU.add).then_inc(mods_done, 1)
            e.wait_ge(mods_done, 1)
            e.scalar_tensor_tensor(gain2[:, :, :], mods[:, 32:40, :], 1.0, cols[:, N2:N2 + 8].unsqueeze(2).to_broadcast([P, KD, 2]), ALU.add, ALU.mult).then_inc(mods_done, 1)
            e.wait_ge(mods_done, 2)
            e.wait_ge(act_na.sem, act_na.value(KP - 1, "out"))
            e.sem_inc(dve_mg.sem, dve_mg.n)
            with e.Fori(0, KD // 2) as f:
                for i in range(2):
                    e.wait_ge(act_mg.sem, act_mg.value(f, f"g{i}"))
                    e.wait_ge(dve_mg.sem, dve_mg.value(f - 1, f"y{i}"))
                    e.wait_ge(pa_out, KD + 1)
                    of_dn = hT[:, ds(2 * f + i, 1), :].rearrange("p o c -> p (o c)")
                    dve_mg.done(e.tensor_tensor(prod[:, i, 0, :], sgm[:, i, 0, :], of_dn, ALU.mult), f"yA{i}")
                    e.wait_ge(pe_mg.sem, pe_mg.value(f, f"pB{i}"))
                    for b, (a, n) in enumerate(SEG):
                        m = e.tensor_tensor(prod[:, i, 1, a:a + n], sgm[:, i, 1, a:a + n], ps[:, 2 * i + b, 0:n], ALU.mult)
                    dve_mg.done(m, f"yB{i}")
                    e.wait_ge(dve_mg.sem, dve_mg.value(f, f"yB{i}"))
                    y = yT[:, ds(2 * f + i, 1), :].rearrange("p o c -> p (o c)")
                    dve_mg.done(e.tensor_tensor(y, prod[:, i, 0, :], prod[:, i, 1, :], ALU.add), f"y{i}")

            for n in range(KD):
                e.wait_ge(wo_mm, n + 1)
                for b, (a, w) in enumerate(SEG):
                    m = e.scalar_tensor_tensor(xT[:, n, a:a + w], ps[:, 2 * (n % 3) + b, 0:w], mods[:, 16 + n, b:b + 1], xT[:, n, a:a + w], ALU.mult, ALU.add)
                m.then_inc(wo_x, 1)

            def w_small(q, kind, turn, s):
                e.wait_ge(w_hi[s], unit(q, kind, turn) + 1)
                k = KD if kind == "up" else KH
                e.tensor_tensor(w_part[1][:, s, 0:k, :], raw2[:, s, 0:k, :], w_part[0][:, s, 0:k, :], ALU.subtract).then_inc(w_lo[s], 1)

            for s in range(2):
                e.sem_inc(w_lo[s], 1)
            e.wait_ge(rms2_done, 1)
            e.reciprocal(rstd2[:, :], rms2).then_inc(rstd2_done, 1)
            w_small(0, "up", 0, 0)
            w_small(0, "up", 0, 1)
            e.wait_ge(rstd2_done, 1)
            for k in range(KD + 1):
                if k < KD:
                    if k >= 2:
                        e.wait_ge(h_lo, k - 1)
                    e.tensor_tensor(h2[:, k % 2, :], xT[:, k, :], rstd2[:, :], ALU.mult).then_inc(xn2_done, 1)
                if k:
                    e.wait_ge(h_hi, k)
                    e.tensor_tensor(h_part[1][:, k - 1, :], h2[:, (k - 1) % 2, :], h_part[0][:, k - 1, :], ALU.subtract).then_inc(h_lo, 1)

            def hidden(q, f):
                e.wait_ge(silu_done, f + (KH * q + 2))
                e.wait_ge(w_used[1], unit(q, "up", f) + 2)
                e.wait_ge(a_lo, f + (KH * q + 1))
                for b, (a, n) in enumerate(HALVES):
                    m = e.tensor_tensor(hid[:, a:a + n], sg[:, a:a + n], ps[:, 2 + b, 0:n], ALU.mult)
                m.then_inc(hid_done, 1)
                e.wait_ge(a_hi, f + (KH * q + 1))
                big, small = (part[:, ds(f, 1), :].rearrange("p o c -> p (o c)") for part in a_part)
                e.tensor_tensor(small, hid, big, ALU.subtract).then_inc(a_lo, 1)

            def result(q, g, s):
                e.wait_ge(w_used[s], unit(q, "down", g) + 2)
                if q:
                    e.wait_ge(y_turned[s], g + 1)
                for b, a, n, c in PIECES:
                    x = xT[:, ds(g * 2 + s, 1), a:a + n].rearrange("p o c -> p (o c)")
                    gate = mods[:, ds(g * 2 + (s + 40), 1), c]
                    m = e.scalar_tensor_tensor(xo[:, s, a:a + n] if q else x, ps[:, 4 + 2 * s + b, a - b * HT:a - b * HT + n], gate, x, ALU.mult, ALU.add)
                m.then_inc(x_done[s], 1)

            e.sem_inc(hid_done, 1)
            e.sem_inc(a_lo, 1)
            for s in range(2):
                e.sem_inc(x_done[s], 1)
            for q in range(2):
                if q:
                    w_small(1, "up", 0, 0)
                    result(0, KD // 2 - 1, 1)
                    w_small(1, "up", 0, 1)
                with e.Fori(1, KH) as f:
                    w_small(q, "up", f, 0)
                    hidden(q, f - 1)
                    w_small(q, "up", f, 1)
                w_small(q, "down", 0, 0)
                hidden(q, KH - 1)
                w_small(q, "down", 0, 1)
                result(q, 0, 0)
                with e.Fori(1, KD // 2) as g:
                    w_small(q, "down", g, 0)
                    result(q, g - 1, 1)
                    w_small(q, "down", g, 1)
                    result(q, g, 0)
            result(1, KD // 2 - 1, 1)

        @block.gpsimd
        def _(e):
            e.wait_ge(prm_done, 2)
            e.wait_ge(zero_done, 3)
            e.sem_inc(strip["z"], 1)
            e.sem_inc(st_S, 32)
            e.sem_inc(pool_dn.sem, pool_dn.n)

            def head(h, more):
                def wait(steps, name, turn=h):
                    e.wait_ge(steps.sem, steps.value(turn, name))

                def per_unit(kind):
                    return prm[:, kind, :].rearrange("p (d t) -> p d t", d=2).unsqueeze(3).to_broadcast([P, 2, NT, P])

                wait(dve_dn, "prm")
                wait(pe_dn, f"av {NT - 1} b", h - 1)
                tri = sq_c[:, LE:GE + 1, :].unsqueeze(2).to_broadcast([P, 2, NT, P])
                pool_dn.done(e.tensor_tensor(typed(gm[:, :, :]), tri, per_unit(G), ALU.mult), "g mask")
                wait(act_dn, "decay")
                pool_dn.done(e.tensor_tensor(typed(dtm[:, :, :]), typed(dt[:, :, :]), tri, ALU.mult), "decay")
                wait(act_dn, "k rows")
                wait(dve_dn, "kv ctx")
                wait(pe_dn, "turn o", h - 1)
                pool_dn.done(e.tensor_tensor(typed(kd[:, :, :]), krow[:, :, :].unsqueeze(1).to_broadcast([P, 2, NT, P]), per_unit(EK), ALU.mult), "kd")
                wait(act_dn, "kq")
                wait(pool_dn, "decay")
                pool_dn.done(e.tensor_tensor(typed(AT[:, :, :]), kqs[:, :, 1, :].unsqueeze(1).to_broadcast([P, 2, NT, P]), typed(dtm[:, :, :]), ALU.mult), "A")

            with e.Fori(0, H - 1) as h:
                head(h, True)
            head(H - 1, False)

            e.wait_ge(dve_dn.sem, dve_dn.value(H - 1, "o out"))
            e.wait_ge(act_dn.sem, act_dn.value(H - 1, "ada"))
            e.wait_ge(pe_dn.sem, pe_dn.value(H - 1, "turn o"))
            e.memset(zrow[:, :], 0.0).then_inc(zrow_done, 1)
            e.memset(bm[:, :, :, :], 0.0).then_inc(zrow_done, 1)
            e.wait_ge(zrow_done, 2)
            e.wait_ge(ld_nc, 80)
            e.sem_inc(pool_na.sem, 2)

            def pair(p):
                for hh in range(2):
                    e.wait_ge(ld_bias[hh], p * (16 * ROWS) + 16 * ROWS)
                    e.wait_ge(dve_na.sem, dve_na.value(p - 1, f"max {NU // 2 * (hh + 1) - 1}"))
                    for c in range(CT):
                        tiles, at, _ = key_tiles(c)
                        rel = tiles[0] - c + 1
                        n = len(tiles)
                        b = bias[:, hh, :, :].rearrange("p r (t x) -> p t r x", t=3)
                        w = win[:, c, :].rearrange("p (t x) -> p t x", t=3)
                        for j in range(n):
                            dst = bm[:, hh, c, at + j * P:at + (j + 1) * P].rearrange("p (r x) -> p r x", r=ROWS)
                            m = e.tensor_tensor(dst, b[:, rel + j, :, :], w[:, rel + j, :].unsqueeze(1).to_broadcast([P, ROWS, KC]), ALU.add)
                    pool_na.done(m, f"bias {hh}")

            with e.Fori(0, KP) as p:
                pair(p)


_INS = ["x_prompt", "x_sample", "c", "cache_na_k", "cache_na_v", "state_dn", "c_ctx", "w_ada", "b_ada", "norm1_g", "w_in",
        "dn_conv", "dn_a_log", "dn_dt_bias", "dn_norm_g", "w_pa", "na_qnorm_g", "na_knorm_g", "na_rpb", "w_pb", "w_out",
        "norm2_g", "ffn_w1", "ffn_w3", "ffn_w2"]
_OUTS = [("y_prompt", (1, CTX, D)), ("y_sample", (1, LAT, D)), ("new_k", (1, 1, CTX, NA_H, NA_D)),
         ("new_v", (1, 1, CTX, NA_H, NA_D)), ("new_state", (1, 1, 2, H, DK, DK))]


def kernel(**inputs):
    import concourse.bacc as bacc
    from concourse.bass_utils import run_bass_kernel_spmd

    nc = bacc.Bacc("TRN2", target_bir_lowering=False, num_devices=1)
    arrays = {name: np.ascontiguousarray(inputs[name]) for name in _INS}
    arrays.update(zip(("squares", "levels", "window"), shape_constants()))
    A = {n: nc.dram_tensor("in_" + n, a.shape, mybir.dt.from_np(a.dtype), kind="ExternalInput").ap() for n, a in arrays.items()}
    for name, shape in _OUTS:
        A[name] = nc.dram_tensor("out_" + name, shape, F32, kind="ExternalOutput").ap()
    build(nc, A)
    r = run_bass_kernel_spmd(nc, [{"in_" + n: a for n, a in arrays.items()}], core_ids=[0])
    return tuple(r.results[0]["out_" + name] for name, _ in _OUTS)
```
